# Optimizing a Trainium2 kernel written in Bass

```python
import jax, jax.numpy as jnp
from jax import lax
import numpy as np
import math

D_MODEL = 1024
BATCH = 1
SEQ = 512
DEPTH = 2

N_MIXERS = 4
GROUP_WIDTH = D_MODEL // N_MIXERS
HEAD_DIM = 64
FOX_HEADS = GROUP_WIDTH // HEAD_DIM
RET_HEADS = GROUP_WIDTH // HEAD_DIM
POOL_WINDOWS = (2, 4, 8, 16)
POOL_GROUPS = len(POOL_WINDOWS)
POOL_GROUP_DIM = GROUP_WIDTH // POOL_GROUPS
CONV_WIDTH = 31
CONV_CH = GROUP_WIDTH
N_IN = 3 * GROUP_WIDTH + FOX_HEADS + GROUP_WIDTH + 4 * GROUP_WIDTH + 2 * CONV_CH
D_FF = ((8 * D_MODEL + 3 * 256 - 1) // (3 * 256)) * 256
Q_BLOCK = 128
RET_CHUNK = 128
ROPE_BASE = 10000.0
EPS = 1e-6


def rmsnorm(x, g):
    xf = x.astype(jnp.float32)
    y = xf * lax.rsqrt(jnp.mean(xf * xf, axis=-1, keepdims=True) + EPS)
    return (y * g.astype(jnp.float32)).astype(x.dtype)

def layernorm(x, g, b):
    xf = x.astype(jnp.float32)
    mu = jnp.mean(xf, axis=-1, keepdims=True)
    var = jnp.mean(jnp.square(xf - mu), axis=-1, keepdims=True)
    y = (xf - mu) * lax.rsqrt(var + EPS)
    return (y * g.astype(jnp.float32) + b.astype(jnp.float32)).astype(x.dtype)

def rope(x, positions):
    half = x.shape[-1] // 2
    inv = ROPE_BASE ** (-jnp.arange(half, dtype=jnp.float32) / half)
    ang = positions.astype(jnp.float32)[..., None] * inv
    cos = jnp.cos(ang)[:, :, None, :]
    sin = jnp.sin(ang)[:, :, None, :]
    x1, x2 = x[..., :half], x[..., half:]
    return jnp.concatenate([x1 * cos - x2 * sin, x1 * sin + x2 * cos], axis=-1).astype(x.dtype)

def fox_attention(q, k, v, f_logit, f_bias):
    B, S, H, Dh = q.shape
    log_f = jax.nn.log_sigmoid((f_logit + f_bias).astype(jnp.float32))
    cum = jnp.cumsum(log_f, axis=1).transpose(0, 2, 1)
    key_pos = jnp.arange(S)
    scale = Dh ** -0.5

    def block(i):
        start = i * Q_BLOCK
        qb = lax.dynamic_slice_in_dim(q, start, Q_BLOCK, axis=1)
        cq = lax.dynamic_slice_in_dim(cum, start, Q_BLOCK, axis=2)
        s = jnp.einsum('bqhd,bkhd->bhqk', qb, k).astype(jnp.float32) * scale
        s = s + cq[..., :, None] - cum[:, :, None, :]
        q_pos = start + jnp.arange(Q_BLOCK)
        causal = key_pos[None, :] <= q_pos[:, None]
        s = jnp.where(causal, s, -jnp.inf)
        p = jax.nn.softmax(s, axis=-1).astype(v.dtype)
        return jnp.einsum('bhqk,bkhd->bqhd', p, v)

    out = lax.map(block, jnp.arange(S // Q_BLOCK))
    return out.transpose(1, 0, 2, 3, 4).reshape(B, S, H * Dh)

def pool_mixer(u, pool_w, pool_scale):
    B, S, _ = u.shape
    ug = u.reshape(B, S, POOL_GROUPS, POOL_GROUP_DIM)
    cs = jnp.cumsum(ug.astype(jnp.float32), axis=1)
    pos = jnp.arange(S)
    means = []
    for gi, w in enumerate(POOL_WINDOWS):
        c_g = cs[:, :, gi]
        shifted = jnp.pad(c_g, ((0, 0), (w, 0), (0, 0)))[:, :S]
        count = jnp.minimum(pos + 1, w).astype(jnp.float32)[None, :, None]
        means.append((c_g - shifted) / count)
    pooled = jnp.stack(means, axis=2)
    delta = (pooled - ug.astype(jnp.float32)).astype(u.dtype)
    mixed = jnp.einsum('bsgc,gcd->bsgd', delta, pool_w).reshape(B, S, GROUP_WIDTH)
    return mixed * pool_scale

def retention(q, k, v, g, positions, gn_g):
    B, S, H, Dh = q.shape
    q = rope(q, positions)
    k = rope(k, positions) * (Dh ** -0.5)
    log_gamma = jnp.log(1.0 - 2.0 ** (-5.0 - jnp.arange(H, dtype=jnp.float32)))
    C = RET_CHUNK
    NC = S // C
    idx = jnp.arange(C, dtype=jnp.float32)
    diff = idx[:, None] - idx[None, :]
    dmask = jnp.where(diff >= 0, jnp.exp(log_gamma[:, None, None] * jnp.maximum(diff, 0.0)), 0.0)
    zeta = jnp.exp(log_gamma[:, None] * (C - 1 - idx))
    xi = jnp.exp(log_gamma[:, None] * (idx + 1))
    chunk_decay = jnp.exp(log_gamma * C)

    qc = q.reshape(B, NC, C, H, Dh)
    kc = k.reshape(B, NC, C, H, Dh)
    vc = v.reshape(B, NC, C, H, Dh)
    intra_s = jnp.einsum('bnqhd,bnkhd->bnhqk', qc, kc) * dmask
    intra = jnp.einsum('bnhqk,bnkhe->bnqhe', intra_s, vc)
    kv = jnp.einsum('bnkhd,hk,bnkhe->bnhde', kc, zeta, vc)

    def step(state, xs):
        q_n, kv_n = xs
        cross = jnp.einsum('bqhd,bhde->bqhe', q_n, state)
        new = (state * chunk_decay[None, :, None, None] + kv_n).astype(state.dtype)
        return new, cross

    state0 = jnp.zeros((B, H, Dh, Dh), dtype=kv.dtype)
    _, cross = lax.scan(step, state0, (qc.transpose(1, 0, 2, 3, 4), kv.transpose(1, 0, 2, 3, 4)))
    cross = cross.transpose(1, 0, 2, 3, 4) * xi.T[None, None, :, :, None]
    o = (intra + cross).reshape(B, S, H, Dh).astype(jnp.float32)
    mu = jnp.mean(o, axis=-1, keepdims=True)
    var = jnp.mean(jnp.square(o - mu), axis=-1, keepdims=True)
    o = (o - mu) * lax.rsqrt(var + EPS) * gn_g.reshape(H, Dh).astype(jnp.float32)
    o = o.reshape(B, S, H * Dh).astype(g.dtype)
    return jax.nn.silu(g) * o

def conformer_conv(u, conv_w, conv_b, ln_g, ln_b):
    a, gate = jnp.split(u, 2, axis=-1)
    h = a * jax.nn.sigmoid(gate)
    h = lax.conv_general_dilated(
        h, conv_w[:, None, :], window_strides=(1,), padding=[(CONV_WIDTH - 1, 0)],
        dimension_numbers=('NWC', 'WIO', 'NWC'), feature_group_count=CONV_CH) + conv_b
    return jax.nn.silu(layernorm(h, ln_g, ln_b))

def first_inputs(seed: int = 0) -> dict:
    key = jax.random.key(seed)
    ks = jax.random.split(key, 24)
    f32 = jnp.float32
    D, G = D_MODEL, GROUP_WIDTH
    nrm = lambda k, shape, s: jax.random.normal(k, shape, f32) * s
    return {
        "x": jax.random.normal(ks[0], (BATCH, SEQ, D), f32),
        "c": jax.random.normal(ks[1], (BATCH, D), f32),
        "positions": jnp.broadcast_to(jnp.arange(SEQ, dtype=jnp.int32)[None, :], (BATCH, SEQ)),
        "ada_w": nrm(ks[2], (DEPTH, D, 6 * D), 0.5 * D ** -0.5),
        "ada_b": nrm(ks[3], (DEPTH, 6 * D), 0.01),
        "norm_mix_g": 1.0 + nrm(ks[4], (DEPTH, D), 0.1),
        "norm_ffn_g": 1.0 + nrm(ks[5], (DEPTH, D), 0.1),
        "w_in": nrm(ks[6], (DEPTH, D, N_IN), D ** -0.5),
        "fox_fb": jax.random.uniform(ks[7], (DEPTH, FOX_HEADS), f32, 2.0, 5.0),
        "pool_w": nrm(ks[8], (DEPTH, POOL_GROUPS, POOL_GROUP_DIM, POOL_GROUP_DIM), POOL_GROUP_DIM ** -0.5),
        "pool_scale": 1.0 + nrm(ks[9], (DEPTH, G), 0.1),
        "ret_gn_g": 1.0 + nrm(ks[10], (DEPTH, G), 0.1),
        "conv_w": nrm(ks[11], (DEPTH, CONV_WIDTH, CONV_CH), CONV_WIDTH ** -0.5),
        "conv_b": nrm(ks[12], (DEPTH, CONV_CH), 0.01),
        "conv_ln_g": 1.0 + nrm(ks[13], (DEPTH, CONV_CH), 0.1),
        "conv_ln_b": nrm(ks[14], (DEPTH, CONV_CH), 0.01),
        "w_out": nrm(ks[15], (DEPTH, D, D), D ** -0.5),
        "ffn_w1": nrm(ks[16], (DEPTH, D, D_FF), D ** -0.5),
        "ffn_w3": nrm(ks[17], (DEPTH, D, D_FF), D ** -0.5),
        "ffn_w2": nrm(ks[18], (DEPTH, D_FF, D), D_FF ** -0.5),
        "final_g": 1.0 + nrm(ks[19], (D,), 0.1),
    }

def first_block(x, c, positions, ada_w, ada_b, norm_mix_g, norm_ffn_g, w_in, fox_fb,
              pool_w, pool_scale, ret_gn_g, conv_w, conv_b, conv_ln_g, conv_ln_b,
              w_out, ffn_w1, ffn_w3, ffn_w2, final_g):
    B, S, _ = x.shape
    G, H, Dh = GROUP_WIDTH, FOX_HEADS, HEAD_DIM
    bounds = [G, 2 * G, 3 * G, 3 * G + H,
              4 * G + H,
              5 * G + H, 6 * G + H, 7 * G + H, 8 * G + H]
    c_act = jax.nn.silu(c)
    for l in range(DEPTH):
        mod = (c_act @ ada_w[l] + ada_b[l])[:, None, :]
        sh1, sc1, g1, sh2, sc2, g2 = jnp.split(mod, 6, axis=-1)

        h = rmsnorm(x, norm_mix_g[l]) * (1.0 + sc1) + sh1
        u = h @ w_in[l]
        fq, fk, fv, ff, pu, rq, rk, rv, rg, cu = jnp.split(u, bounds, axis=-1)
        y_fox = fox_attention(fq.reshape(B, S, H, Dh), fk.reshape(B, S, H, Dh),
                              fv.reshape(B, S, H, Dh), ff, fox_fb[l])
        y_pool = pool_mixer(pu, pool_w[l], pool_scale[l])
        y_ret = retention(rq.reshape(B, S, RET_HEADS, Dh), rk.reshape(B, S, RET_HEADS, Dh),
                          rv.reshape(B, S, RET_HEADS, Dh), rg, positions, ret_gn_g[l])
        y_conv = conformer_conv(cu, conv_w[l], conv_b[l], conv_ln_g[l], conv_ln_b[l])
        mix = jnp.concatenate([y_fox, y_pool, y_ret, y_conv], axis=-1)
        x = x + g1 * (mix @ w_out[l])

        h = rmsnorm(x, norm_ffn_g[l]) * (1.0 + sc2) + sh2
        f = (jax.nn.silu(h @ ffn_w1[l]) * (h @ ffn_w3[l])) @ ffn_w2[l]
        x = x + g2 * f
    return rmsnorm(x, final_g)


CHUNK = 64
N_HEADS = 8
N_KV_HEADS = 2
ATTN_WIDTH = N_HEADS * HEAD_DIM
ROPE_DIM = HEAD_DIM // 4
ROPE_THETA = 500000.0
N_IDX_HEADS = 4
IDX_DIM = 64
TOPK_MAX = 256
SGU_CHUNK = 128
SGU_GROUPS = 8
SGU_WIDTH = D_MODEL - ATTN_WIDTH
SGU_GROUP_DIM = SGU_WIDTH // SGU_GROUPS
D_FF_2 = -(-(8 * D_MODEL) // (3 * 256)) * 256
PLE_DIM = 256
ALPHA = (2 * DEPTH) ** 0.25
BETA = (8 * DEPTH) ** -0.25
LN_EPS = 1e-5

Q_COLS = N_HEADS * HEAD_DIM
KV_COLS = N_KV_HEADS * HEAD_DIM
IQ_COLS = N_IDX_HEADS * IDX_DIM
IK_COLS = IDX_DIM
IW_COLS = N_IDX_HEADS
IN_SPLITS = (Q_COLS, KV_COLS, KV_COLS, IQ_COLS, IK_COLS, IW_COLS, SGU_WIDTH, SGU_WIDTH)
IN_COLS = Q_COLS + 2 * KV_COLS + IQ_COLS + IK_COLS + IW_COLS + 2 * SGU_WIDTH


def layer_norm(x, g, b):
    xf = x.astype(jnp.float32)
    mu = jnp.mean(xf, axis=-1, keepdims=True)
    var = jnp.mean(jnp.square(xf - mu), axis=-1, keepdims=True)
    y = (xf - mu) * lax.rsqrt(var + LN_EPS)
    return (y * g.astype(jnp.float32) + b.astype(jnp.float32)).astype(x.dtype)

def partial_rope(x, pos):
    half = ROPE_DIM // 2
    inv = ROPE_THETA ** (-2.0 * jnp.arange(half, dtype=jnp.float32) / ROPE_DIM)
    ang = pos.astype(jnp.float32)[..., None] * inv
    cos = jnp.cos(ang)[:, :, None, :]
    sin = jnp.sin(ang)[:, :, None, :]
    xr = x[..., :ROPE_DIM].astype(jnp.float32)
    x1, x2 = xr[..., :half], xr[..., half:]
    rot = jnp.concatenate([x1 * cos - x2 * sin, x2 * cos + x1 * sin], axis=-1)
    return jnp.concatenate([rot.astype(x.dtype), x[..., ROPE_DIM:]], axis=-1)

def dsa_attention(q, k, v, qi, ki, wi):
    B, S = q.shape[0], q.shape[1]
    topk = min(TOPK_MAX, S // 4)
    nb = S // Q_BLOCK
    G = N_KV_HEADS
    R = N_HEADS // N_KV_HEADS
    key_chunk = jnp.arange(S) // CHUNK

    def to_blocks(a):
        return jnp.moveaxis(a.reshape((B, nb, Q_BLOCK) + a.shape[2:]), 1, 0)

    q_b = to_blocks(q.reshape(B, S, G, R, HEAD_DIM))
    qi_b = to_blocks(qi)
    wi_b = to_blocks(wi)
    t_b = jnp.arange(S).reshape(nb, Q_BLOCK)

    def block(args):
        qb, qib, wib, tb = args
        q_chunk = tb // CHUNK
        allowed = key_chunk[None, :] <= q_chunk[:, None]
        logits = jnp.einsum('bqhd,bsd->bqhs', qib, ki)
        score = jnp.einsum('bqhs,bqh->bqs', jax.nn.relu(logits), wib).astype(jnp.float32)
        score = jnp.where(allowed[None], score, -jnp.inf)
        _, idx = lax.top_k(score, topk)
        k_sel = jax.vmap(lambda kb, ib: kb[ib])(k, idx)
        v_sel = jax.vmap(lambda vb, ib: vb[ib])(v, idx)
        valid = key_chunk[idx] <= q_chunk[None, :, None]
        s = jnp.einsum('bqgrd,bqkgd->bqgrk', qb, k_sel).astype(jnp.float32) * (HEAD_DIM ** -0.5)
        s = jnp.where(valid[:, :, None, None, :], s, -jnp.inf)
        pr = jax.nn.softmax(s, axis=-1).astype(v.dtype)
        return jnp.einsum('bqgrk,bqkgd->bqgrd', pr, v_sel)

    out = lax.map(block, (q_b, qi_b, wi_b, t_b))
    return jnp.moveaxis(out, 0, 1).reshape(B, S, ATTN_WIDTH)

def spatial_gating(u, v, w_s, b_s, g, bta):
    B, S = u.shape[0], u.shape[1]
    v = layer_norm(v, g, bta)
    nc = S // SGU_CHUNK
    vb = v.reshape(B, nc, SGU_CHUNK, SGU_GROUPS, SGU_GROUP_DIM)
    tri = jnp.tril(jnp.ones((SGU_CHUNK, SGU_CHUNK), dtype=bool))
    w = jnp.where(tri[None], w_s, jnp.zeros_like(w_s))
    mixed = jnp.einsum('gts,bcsgd->bctgd', w, vb) + jnp.swapaxes(b_s, 0, 1)[None, None, :, :, None]
    return u * mixed.reshape(B, S, SGU_WIDTH)

def second_inputs(seed: int = 0) -> dict:
    key = jax.random.key(seed)
    ks = jax.random.split(key, 20)

    def nrm(k, shape, scale):
        return jax.random.normal(k, shape, jnp.float32) * scale

    x = nrm(ks[0], (BATCH, SEQ, D_MODEL), 1.0)
    p = nrm(ks[1], (DEPTH, BATCH, SEQ, PLE_DIM), 1.0)
    start = jax.random.randint(ks[2], (BATCH, 1), 0, 64, dtype=jnp.int32) * CHUNK
    positions = (start + jnp.arange(SEQ, dtype=jnp.int32)[None, :]).astype(jnp.int32)
    return {
        "x": x,
        "p": p,
        "positions": positions,
        "w_in": nrm(ks[3], (DEPTH, D_MODEL, IN_COLS), D_MODEL ** -0.5),
        "w_o": nrm(ks[4], (DEPTH, D_MODEL, D_MODEL), BETA * D_MODEL ** -0.5),
        "ln1_g": 1.0 + nrm(ks[5], (DEPTH, D_MODEL), 0.02),
        "ln1_b": nrm(ks[6], (DEPTH, D_MODEL), 0.02),
        "ln2_g": 1.0 + nrm(ks[7], (DEPTH, D_MODEL), 0.02),
        "ln2_b": nrm(ks[8], (DEPTH, D_MODEL), 0.02),
        "sgu_w": nrm(ks[9], (DEPTH, SGU_GROUPS, SGU_CHUNK, SGU_CHUNK), SGU_CHUNK ** -0.5),
        "sgu_b": 1.0 + nrm(ks[10], (DEPTH, SGU_GROUPS, SGU_CHUNK), 0.02),
        "sgu_ln_g": 1.0 + nrm(ks[11], (DEPTH, SGU_WIDTH), 0.02),
        "sgu_ln_b": nrm(ks[12], (DEPTH, SGU_WIDTH), 0.02),
        "w_ffn_in": nrm(ks[13], (DEPTH, D_MODEL, 2 * D_FF_2), D_MODEL ** -0.5),
        "w_ffn_out": nrm(ks[14], (DEPTH, D_FF_2, D_MODEL), BETA * D_FF_2 ** -0.5),
        "w_ple": nrm(ks[15], (DEPTH, PLE_DIM, D_MODEL), PLE_DIM ** -0.5),
        "w_ple_gate": nrm(ks[16], (DEPTH, D_MODEL, D_MODEL), D_MODEL ** -0.5),
    }

def second_block(x, p, positions, w_in, w_o, ln1_g, ln1_b, ln2_g, ln2_b, sgu_w, sgu_b,
              sgu_ln_g, sgu_ln_b, w_ffn_in, w_ffn_out, w_ple, w_ple_gate):
    B, S = x.shape[0], x.shape[1]
    split_points = [int(o) for o in np.cumsum(IN_SPLITS)[:-1]]
    for i in range(DEPTH):
        h = x @ w_in[i]
        q, k, v, qi, ki, wi, u, vs = jnp.split(h, split_points, axis=-1)
        q = partial_rope(q.reshape(B, S, N_HEADS, HEAD_DIM), positions)
        k = partial_rope(k.reshape(B, S, N_KV_HEADS, HEAD_DIM), positions)
        v = v.reshape(B, S, N_KV_HEADS, HEAD_DIM)
        qi = partial_rope(qi.reshape(B, S, N_IDX_HEADS, IDX_DIM), positions)
        ki = partial_rope(ki.reshape(B, S, 1, IDX_DIM), positions)[:, :, 0]
        wi = wi * ((N_IDX_HEADS * IDX_DIM) ** -0.5)
        a_out = dsa_attention(q, k, v, qi, ki, wi)
        b_out = spatial_gating(jax.nn.gelu(u), jax.nn.gelu(vs), sgu_w[i], sgu_b[i],
                               sgu_ln_g[i], sgu_ln_b[i])
        mix = jnp.concatenate([a_out, b_out], axis=-1) @ w_o[i]
        x = layer_norm(ALPHA * x + mix, ln1_g[i], ln1_b[i])
        gate, up = jnp.split(x @ w_ffn_in[i], 2, axis=-1)
        ffn = (jax.nn.silu(gate) * up) @ w_ffn_out[i]
        ple = (p[i] @ w_ple[i]) * jax.nn.sigmoid(x @ w_ple_gate[i])
        x = layer_norm(ALPHA * x + ffn + ple, ln2_g[i], ln2_b[i])
    return x


def setup_inputs(seed=0):
    out = dict(first_inputs(seed))
    for name, value in second_inputs(seed + 1).items():
        if name != "x":
            out[name + "_2"] = value
    return out


def reference(
    x, c, positions, ada_w, ada_b, norm_mix_g, norm_ffn_g, w_in, fox_fb, pool_w, pool_scale,
    ret_gn_g, conv_w, conv_b, conv_ln_g, conv_ln_b, w_out, ffn_w1, ffn_w3, ffn_w2, final_g, p_2,
    positions_2, w_in_2, w_o_2, ln1_g_2, ln1_b_2, ln2_g_2, ln2_b_2, sgu_w_2, sgu_b_2,
    sgu_ln_g_2, sgu_ln_b_2, w_ffn_in_2, w_ffn_out_2, w_ple_2, w_ple_gate_2,
):
    x = first_block(
        x, c, positions, ada_w, ada_b, norm_mix_g, norm_ffn_g, w_in, fox_fb, pool_w, pool_scale,
        ret_gn_g, conv_w, conv_b, conv_ln_g, conv_ln_b, w_out, ffn_w1, ffn_w3, ffn_w2, final_g,
    )
    return second_block(
        x, p_2, positions_2, w_in_2, w_o_2, ln1_g_2, ln1_b_2, ln2_g_2, ln2_b_2, sgu_w_2,
        sgu_b_2, sgu_ln_g_2, sgu_ln_b_2, w_ffn_in_2, w_ffn_out_2, w_ple_2, w_ple_gate_2,
    )


_drawn_inputs = setup_inputs


def setup_inputs(seed=0):
    import zlib

    import numpy as np

    out = dict(_drawn_inputs(seed))
    spreads = {}
    factors = {'ada_b': 3.427,
     'pool_scale': 2.854,
     'ret_gn_g': 3.783,
     'conv_b': 8.0,
     'conv_ln_g': 3.529,
     'conv_ln_b': 36.078,
     'sgu_b_2': 22.655,
     'sgu_ln_g_2': 85.423,
     'sgu_ln_b_2': 92.92}
    for name, (base, spread) in spreads.items():
        noise = np.random.default_rng([zlib.crc32(name.encode()), seed]).standard_normal(out[name].shape)
        drawn = base * np.exp(spread * noise) if base else spread * noise
        out[name] = __import__('jax').numpy.asarray(drawn.astype(out[name].dtype))
    for name, factor in factors.items():
        out[name] = (out[name] * factor).astype(out[name].dtype)
    return out
```

```python
from contextlib import ExitStack

import numpy as np
import concourse.bass as bass
from concourse import mybir

F32 = mybir.dt.float32
F32R = mybir.dt.float32r
I32 = mybir.dt.int32
ALU = mybir.AluOpType
ACT = mybir.ActivationFunctionType
AX = mybir.AxisListType.X

P = 128
T = 512
D = 1024
KD = D // P
NB = T // P
G = 256
HD = 64
FF = 2816
KF = FF // P
DEPTH = 2
TAPS = 31
MODS = 6 * KD
NEG = -1e30
FLOOR = -3e38
TAKEN = -3.4e38
TOPK = T // 4
EPS, LN_EPS = 1e-6, 1e-5
ALPHA = (2 * DEPTH) ** 0.25
IN1 = dict(fq=0, fk=256, fv=512, ff=768, pu=772, rq=1028, rk=1284, rv=1540, rg=1796, ca=2052, cg=2308)
IN2 = dict(q=0, k=512, v=640, qi=768, ki=1024, wi=1088, u=1092, vs=1604)
CAUSAL = [P * (i + 1) for i in range(NB)]
P_AT = [P * i * (i + 1) // 2 for i in range(NB)]
PT_AT = [0, 512, 896, 1152]
TRI = sum(CAUSAL)
BY_QUERY = [(0, 2), (1,), (3,)]
BY_KEY = [(1, 3), (2,), (0,)]

UNITS = {1: 10 + 4 + 22 + 16, 2: 9 + 4 + 5 + 22 + 16}
UNIT0 = {1: 0, 2: DEPTH * UNITS[1]}


def consts():
    eye = np.eye(P)
    k = np.arange(P)[:, None]
    q = np.arange(P)[None, :]
    parts = {}
    parts["eye"] = eye
    parts["causal"] = np.where(k >= q, 0.0, NEG)
    parts["chunked"] = np.where((k < 64) & (q >= 64), NEG, 0.0)
    parts["tril"] = (k <= q) * 1.0
    parts["heads"] = (k // HD == q // HD) / float(HD)
    for name, half, width in (("turn1", HD // 2, HD), ("turn2", HD // 8, HD // 4)):
        m = np.zeros((P, P))
        for p in range(P):
            r = p % HD
            if r < half:
                m[p + half, p] = -1.0
            elif r < width:
                m[p - half, p] = 1.0
        parts[name] = m
    sel = np.zeros((P, 4, P))
    for h in range(4):
        sel[h, h] = sel[32 + h, h] = -8.0
    parts["pick"] = sel.reshape(P, -1)
    sel = np.zeros((P, 4, P))
    for m in range(4):
        for p in range(P):
            sel[2 * m + p // HD, m, p] = 1.0
    parts["pairs"] = sel.reshape(P, -1)
    p = np.arange(P)
    parts["freq1"] = (10000.0 ** (-(p % 32) / 32.0))[:, None]
    parts["freq2"] = np.where(p % HD < 16, 500000.0 ** (-2.0 * (p % 8) / 16.0), 0.0)[:, None]
    w = np.stack([np.where(p < 64, 2, 4), np.where(p < 64, 8, 16)], 1)
    parts["window"] = 1.0 / w
    parts["counts"] = (1.0 / np.minimum(np.arange(1, 17)[None, None, :], w[:, :, None])).reshape(P, -1)
    at, cols = {}, 0
    for name, a in parts.items():
        at[name] = (cols, a.shape[1])
        cols += a.shape[1]
    table = np.concatenate(list(parts.values()), 1).astype(np.float32)
    t = np.arange(T)[None, :] - np.arange(P)[:, None]
    decay = [np.where(t >= 0, HD ** -0.5 * np.exp(np.log(1.0 - 2.0 ** (-5.0 - h)) * np.maximum(t, 0)), 0.0)
             for h in range(4)]
    return table, at, np.stack(decay, 1).astype(np.float32)


class Named:
    pass


def build(nc, a, table_at, out):
    with ExitStack() as ctx:
        top = [nc.sbuf_base + 31 & ~31]

        def place(name, shape, dt, at=None):
            size = 4
            for x in shape[1:]:
                size *= x
            off = top[0] if at is None else at
            t = nc.alloc_sbuf_tensor_at(name, shape, dt, offset=off)
            if at is None:
                top[0] = off + (size + 31 & ~31)
            return t

        b = Named()
        b.x = place("x", [P, KD, T], F32)
        b.h_hi = place("h_hi", [P, KD, T], F32R)
        b.h_lo = place("h_lo", [P, KD, T], F32R)
        b.raw = [place(f"raw{i}", [P, 2048], F32) for i in range(2)]
        b.w_hi = [place(f"w_hi{i}", [P, 2048], F32R) for i in range(2)]
        b.w_lo = [place(f"w_lo{i}", [P, 2048], F32R) for i in range(2)]
        ncst = sum(n for nm, (_, n) in table_at.items())
        b.eye = place("eye", [P, P], F32)
        b.ones = place("ones", [P, P], F32)
        b.turn = place("turn", [P, P], F32)
        b.heads = place("heads", [P, P], F32)
        b.tril = place("tril", [P, P], F32)
        b.eye_r = place("eye_r", [P, P], F32R)
        b.causal_r = place("causal_r", [P, P], F32R)
        b.chunked_r = place("chunked_r", [P, P], F32R)
        b.pick_r = place("pick_r", [P, 4, P], F32R)
        b.freq = place("freq", [P, 2], F32)
        b.window = place("window", [P, 2], F32)
        b.counts = place("counts", [P, 2, 16], F32)
        b.eps = place("eps", [P, 4], F32)
        b.wff = place("wff", [P, KD, 4], F32)
        b.cosine = place("cosine", [P, T], F32)
        b.sine = place("sine", [P, T], F32)
        b.r = place("r", [P, T], F32)
        b.mod = place("mod", [P, MODS], F32)
        b.gain = place("gain", [P, 2 * KD], F32)
        b.par = place("par", [P, 74], F32)
        b.taps = place("taps", [P, 2 * TAPS], F32)
        b.c = place("c", [P, KD], F32)
        b.fb = place("fb", [4, 1], F32)
        b.fg = place("fg", [P, KD], F32)
        b.small = place("small", [P, 24], F32)
        b.base = top[0]
        mid = b.base

        class Region:
            def __init__(self, tag, at):
                self.tag, self.at = tag, at

            def __call__(self, name, shape, dt=F32):
                size = 4
                for x in shape[1:]:
                    size *= x
                t = place(self.tag + name, shape, dt, at=self.at)
                self.at += size + 31 & ~31
                assert self.at <= nc.sbuf_usable_end, (self.tag, name, self.at - nc.sbuf_usable_end)
                return t

        z = Region("z_", mid)
        b.z_tab = z("tab", [P, ncst])
        b.z_x = z("x", [P, NB, D])
        b.z_c = z("c", [KD, P])
        b.z_cs = z("cs", [KD, P])
        b.z_fg = z("fg", [KD, P])
        z2 = Region("trig_", mid + 61440)
        b.t_pi = z2("pi", [P, T], I32)
        b.t_pf = z2("pf", [P, T])
        b.t_ang = z2("ang", [P, T])
        b.t_n = z2("n", [P, T])
        b.t_ni = z2("ni", [P, T], I32)
        b.t_a = z2("a", [P, T])
        b.t_b = z2("b", [P, T])
        f = Region("f_", mid)
        b.f_hi = f("hi", [P, KF, T], F32R)
        b.f_lo = f("lo", [P, KF, T], F32R)
        b.f_act = f("act", [P, 2, T])
        b.f_full = f("full", [P, 2, T])
        m = Region("m_", mid)
        b.sq = m("sq", [P, KD, T])
        b.mf = place("mf", [P, KD, T], F32, at=mid)
        full_at = m.at
        b.hf = m("hf", [P, KD, T])
        mm = Region("mm_", full_at)
        b.rq = mm("rq", [P, 2, T])
        b.rk = mm("rk", [P, 2, T])
        b.rv = mm("rv", [P, NB, G])
        b.rg = mm("rg", [P, 2, T])
        b.rraw = place("m_rraw", [P, 2, T], F32, at=m.at)
        b.wb = m("wb", [P, 2, T + 16])
        b.cgate = m("cgate", [P, 2, T + 16])
        b.ch = m("ch", [P, 2, T + TAPS - 1])
        b.cv = m("cv", [P, 2, T])
        b.fq = m("fq", [P, 2, T])
        b.fk = m("fk", [P, 2, T])
        b.fv = m("fv", [P, NB, G])
        b.pu = m("pu", [P, 2, T + 16])
        pool_at = m.at
        b.ln_d = m("ln_d", [P, 2, T])
        b.ln_s = m("ln_s", [P, 2, T])
        b.pw = m("pw", [P, 2, HD])
        b.ls = place("m_ls", [4, 4, T], F32, at=m.at)
        b.prob = m("prob", [P, TRI])
        b.probT = m("probT", [P, TRI])
        b.rs = m("rs", [P, TRI])
        b.decay = m("decay", [P, 4, T])
        b.cum = m("cum", [P, T], F32R)
        mA = Region("mA_", mid)
        b.a_raw = [mA(f"raw{i}", [P, KD, G]) for i in range(2)]
        b.a_acc = [mA(f"acc{i}", [P, G]) for i in range(2)]
        b.rows = mA("rows", [74, P])
        b.rows2 = mA("rows2", [2 * TAPS, P])
        n = Region("n_", mid)
        b.n_sq = n("sq", [P, KD, T])
        b.n_rows = n("rows", [32, P])
        b.n_q = n("q", [P, 4, T])
        b.n_k = n("k", [P, 2, T])
        b.n_ki = n("ki", [P, 1, T])
        b.n_qi = n("qi", [P, 2, T])
        b.n_v = n("v", [P, NB, P])
        b.n_wi = n("wi", [P, NB, 4])
        b.n_wiw = n("wiw", [P, KD, 4])
        b.n_score = n("score", [P, 3, T])
        b.n_work = n("work", [P, 3, T])
        b.n_relu = n("relu", [P, 2, T])
        b.n_top = n("top", [P, 3, 8])
        b.n_mask = n("mask", [P, 3, T], F32R)
        b.n_u = n("u", [P, 4, T])
        b.n_vs = n("vs", [P, NB, T])
        b.n_g = n("g", [P, T])
        b.n_b = n("b", [P, T])
        b.n_swT = n("swT", [P, 8, P])
        b.n_sb = n("sb", [8, P])
        b.pairs = n("pairs", [8, 4, P])
        b.n_st = n("st", [P, NB, 8])
        b.n_bn = n("bn", [P, NB, 6])
        b.n_raw = place("n_raw", [P, 2, T], F32, at=n.at + 4096)
        b.n_sw = place("n_sw", [P, 8, P], F32, at=n.at)
        b.n_prob = n("prob", [P, TRI])
        b.n_probT = n("probT", [P, TRI])
        e = Region("e_", mid)
        b.e_sq = e("sq", [P, KD, T])
        b.e_p = e("p", [P, NB, G])
        b.e_pf = e("pf", [P, 2, T])
        b.e_hi = e("hi", [P, 2, T], F32R)
        b.e_lo = e("lo", [P, 2, T], F32R)
        b.e_ple = e("ple", [P, KD, T])
        b.e_sig = e("sig", [P, 2, T])
        b.y_out = place("y_out", [P, NB, D], F32, at=mid + 4 * KD * T)

        bank = [ctx.enter_context(nc.psum_tensor(f"bank{i}", [P, T], F32)) for i in range(8)]
        s = Sems(nc, ctx)
        block = ctx.enter_context(nc.Block())
        e = Named()
        e.nc, e.a, e.b, e.s, e.bank, e.at, e.out = nc, a, b, s, bank, table_at, out

        @block.sync
        def _(eng):
            sp_program(eng, e)

        @block.scalar
        def _(eng):
            act_program(eng, e)

        @block.gpsimd
        def _(eng):
            pool_program(eng, e)

        @block.vector
        def _(eng):
            dve_program(eng, e)

        @block.tensor
        def _(eng):
            pe_program(eng, e)


class Signal:
    def __init__(self, up, per, credit=0):
        self.up, self.per, self.credit = up, per, credit

    def __call__(self, turn, k):
        return self.up, turn * self.per + (self.credit + k)


class Sems:
    def __init__(self, nc, ctx):
        def up(name, per, credit=0):
            return Signal(ctx.enter_context(nc.semaphore(name)), per, credit)

        self.z_in = up("z_in", 0)
        self.z_ready = up("z_ready", 0)
        self.z_copied = up("z_copied", 0)
        self.z_xt = up("z_xt", 0)
        self.z_x = up("z_x", 0)
        self.z_act = up("z_act", 0)
        self.trig_in = up("trig_in", 0)
        self.trig = up("trig", 0)
        self.trig_sin = up("trig_sin", 0)
        self.par_in = up("par_in", 224)
        self.par_t = up("par_t", 2)
        self.par = up("par", 2)
        self.a_acc = up("a_acc", 192, 16)
        self.a_pe = up("a_pe", 24, 2)
        self.mod = up("mod", 1)
        self.gain = up("gain", 2)
        self.a_in0 = up("a_in0", 192)
        self.a_in1 = up("a_in1", 192)
        self.sq = up("sq", 8)
        self.ssq = up("ssq", 7)
        self.rms = up("rms", 1)
        self.r_ln = up("r_ln", 1)
        self.r = up("r", 1)
        self.xr = up("xr", 8)
        self.hf = up("hf", 8)
        self.hh = up("hh", 8)
        self.hl = up("hl", 8)
        self.ff = up("ff", 1)
        self.ls_a = up("ls_a", 3)
        self.ls_d = up("ls_d", 4)
        self.ls_1 = up("ls_1", 2)
        self.ck = up("ck", 1)
        self.pads = up("pads", 2)
        self.conv = up("conv", 62)
        self.rot = up("rot", 4)
        self.rope = up("rope", 12)
        self.rs_ps = up("rs_ps", 12)
        self.rs = up("rs", 16)
        self.rv_ps = up("rv_ps", 4)
        self.rv_o = up("rv_o", 4)
        self.sc = up("sc", 12)
        self.mxr = up("mxr", 16)
        self.mx = up("mx", 12)
        self.ex = up("ex", 16)
        self.rcp = up("rcp", 4)
        self.pn = up("pn", 16)
        self.tp = up("tp", 12)
        self.pt = up("pt", 12)
        self.pv = up("pv", 4)
        self.po = up("po", 4)
        self.gn_ps = up("gn_ps", 4)
        self.gn_sq = up("gn_sq", 2)
        self.gn_ln = up("gn_ln", 2)
        self.gn_r = up("gn_r", 2)
        self.gn_x = up("gn_x", 2)
        self.gn_m = up("gn_m", 2)
        self.gn_o = up("gn_o", 2)
        self.pl_sum = up("pl_sum", 6)
        self.pl_up = up("pl_up", 2)
        self.pl_d = up("pl_d", 4)
        self.pl_ps = up("pl_ps", 2)
        self.cn_ps = up("cn_ps", 2)
        self.cn_sq = up("cn_sq", 2)
        self.cn_ln = up("cn_ln", 1)
        self.cn_r = up("cn_r", 1)
        self.cn_x = up("cn_x", 2)
        self.cn_xr = up("cn_xr", 2)
        self.cn_o = up("cn_o", 2)
        self.mh = up("mh", 8)
        self.ml = up("ml", 8)
        self.silu = up("silu", 22)
        self.fh = up("fh", 22)
        self.fl = up("fl", 22, 2)
        self.up0 = up("up0", 11, 1)
        self.up1 = up("up1", 11, 1)
        self.raw0 = up("raw0", 0)
        self.raw1 = up("raw1", 0)
        self.hi = up("hi", 0)
        self.lo = up("lo", 0, 2)
        self.half = up("half", 0, 4)
        self.bank0 = up("bank0", 0, 1)
        self.bank1 = up("bank1", 0, 1)
        self.in2 = up("in2", 224)
        self.par2 = up("par2", 1)
        self.par2_t = up("par2_t", 3)
        self.swt = up("swt", 8)
        self.wi_ps = up("wi_ps", 1)
        self.wi = up("wi", 1)
        self.rot2 = up("rot2", 9)
        self.rope2 = up("rope2", 27)
        self.is_ps = up("is_ps", 12)
        self.is_sum = up("is_sum", 21)
        self.floor = up("floor", 3)
        self.top = up("top", 48)
        self.cut = up("cut", 48)
        self.mask = up("mask", 6)
        self.sc2 = up("sc2", 24)
        self.mxr2 = up("mxr2", 32)
        self.mx2 = up("mx2", 24)
        self.ex2 = up("ex2", 32)
        self.rcp2 = up("rcp2", 8)
        self.pn2 = up("pn2", 32)
        self.tp2 = up("tp2", 24)
        self.pt2 = up("pt2", 24)
        self.pv2 = up("pv2", 8)
        self.po2 = up("po2", 8)
        self.bn = up("bn", 8)
        self.v_ln = up("v_ln", 1)
        self.v_r = up("v_r", 1)
        self.v_n = up("v_n", 4)
        self.v_g = up("v_g", 8)
        self.sg = up("sg", 4)
        self.mh2 = up("mh2", 8)
        self.ml2 = up("ml2", 8)
        self.lsum = up("lsum", 7)
        self.lmean = up("lmean", 1)
        self.ld = up("ld", 8)
        self.lsq = up("lsq", 8)
        self.lvar = up("lvar", 1)
        self.l_ln = up("l_ln", 1)
        self.l_r = up("l_r", 1)
        self.lxr = up("lxr", 8)
        self.lx = up("lx", 8, 8)
        self.lhh = up("lhh", 8, 8)
        self.lhl = up("lhl", 8, 8)
        self.p_in = up("p_in", 16)
        self.p_t = up("p_t", 2)
        self.p_f = up("p_f", 2)
        self.p_h = up("p_h", 2)
        self.p_l = up("p_l", 2)
        self.ple = up("ple", 7)
        self.gx = up("gx", 16)
        self.passed = up("passed", 0)
        self.y_t = up("y_t", 0)
        self.y = up("y", 0)
        self.y_out = up("y_out", 0)
        self.raw, self.bank, self.upb = (self.raw0, self.raw1), (self.bank0, self.bank1), (self.up0, self.up1)
        self.a_in = (self.a_in0, self.a_in1)

    def raw_in(self, n2, p):
        return self.raw[p].up, n2 * 64 + 64

    def raw_free(self, n2, p):
        return self.lo.up, n2 * 2 + (p + 1)

    def slot_free(self, n2, p):
        return self.half.up, n2 * 4 + (2 * p + 2)

    def hi_in(self, n2, p):
        return self.hi.up, n2 * 2 + (p + 1)

    def lo_in(self, n2, p):
        return self.lo.up, n2 * 2 + (p + 3)

    def tile(self, n2, p, m):
        return self.half.up, n2 * 4 + (2 * p + m + 5)


USES = {1: 10 + 4 + 4 + 11 + 4, 2: 9 + 2 + 4 + 4 + 4 + 11 + 4}
USE0 = {1: 0, 2: DEPTH * USES[1]}


def attention(s, blk):
    t = Named()
    if blk == 1:
        t.sc, t.mxr, t.mx, t.ex, t.rcp, t.pn, t.tp, t.pt, t.pv, t.po = (
            s.sc, s.mxr, s.mx, s.ex, s.rcp, s.pn, s.tp, s.pt, s.pv, s.po)
    else:
        t.sc, t.mxr, t.mx, t.ex, t.rcp, t.pn, t.tp, t.pt, t.pv, t.po = (
            s.sc2, s.mxr2, s.mx2, s.ex2, s.rcp2, s.pn2, s.tp2, s.pt2, s.pv2, s.po2)
    return t


class Layer:
    def __init__(self, s, blk, l):
        self.s, self.blk, self.l = s, blk, l
        self.pair0 = l * (UNITS[blk] // 2) + UNIT0[blk] // 2
        self.use0 = l * USES[blk] + USE0[blk]
        self.ffn = l + DEPTH * (blk - 1)

    def pair(self, j):
        return self.pair0 + j

    def bank_free(self, m, q):
        return self.s.bank[m].up, self.use0 + (q + 1)

    def bank_out(self, m, q):
        return self.s.bank[m].up, self.use0 + (q + 2)


Q_GN1, Q_GN2, Q_POOL, Q_CONV, Q_OUT, Q_FFN, Q_W2 = 10, 11, 12, 13, 14, 18, 29
Q2_SGU, Q2_OUT, Q2_PLE, Q2_GATE, Q2_FFN, Q2_W2 = 9, 11, 15, 19, 23, 34
MIX2_ORDER = [4, 5, 6, 7, 0, 1, 2, 3]
MIX_ORDER = [4, 5, 2, 3, 6, 7, 0, 1]
UNIT_COLS1 = ["cg", "ca", "rq", "rk", "rv", "fq", "fk", "fv", "pu", "rg"]


def lone_wait(eng, s, sem, value):
    eng.wait_ge(sem, value)
    eng.sem_inc(s.passed.up, 1)


def cols(buf, j):
    return buf[:, :, :].rearrange("p k t -> p (k t)")[:, bass.ts(j, T)]


def w8(buf):
    return buf[:, :].rearrange("p (k c) -> p k c", k=KD)


def w11(buf):
    return buf[:, 0:11 * P].rearrange("p (k c) -> p k c", k=11)



def sp_unit(sp, e, lay, j2, p, dst, src):
    s = e.s
    lone_wait(sp, s, *s.raw_free(lay.pair(j2), p))
    sp.dma_start(dst, src).then_inc(s.raw[p].up, 64)


def sp_weights(sp, e, lay, j, w, l, c0):
    sp_unit(sp, e, lay, j // 2, j % 2, w8(e.b.raw[j % 2]),
            w[l, :, c0:c0 + G].rearrange("(k p) c -> p k c", p=P))


def sp_ffn(sp, e, lay, j0, w1, w3, c3, w2, l):
    s, b = e.s, e.b

    with sp.Fori(0, 11) as i:
        for p, (w, c0) in enumerate(((w1, 0), (w3, c3))):
            sp_unit(sp, e, lay, i + j0 // 2, p, w8(b.raw[p]),
                    w[l, :, c0:c0 + FF].rearrange("(k p) c -> p k c", p=P)[:, :, bass.ts(i, G)])
    with sp.Fori(0, 8) as i:
        for p in range(2):
            sp_unit(sp, e, lay, i + (j0 // 2 + 11), p, w11(b.raw[p]),
                    w2[l, :, :].rearrange("(h k p) c -> h p k c", p=P, h=2)[p, :, :, bass.ts(i, P)])


def sp_layer1(sp, e, l):
    a, b, s = e.a, e.b, e.s
    lay = Layer(s, 1, l)
    sp.wait_ge(*lay.bank_free(0, 0))
    sp.wait_ge(*lay.bank_free(1, 0))
    r = 0
    for name, n in (("norm_mix_g", 8), ("norm_ffn_g", 8), ("ada_b", 48), ("pool_scale", 2), ("ret_gn_g", 2),
                    ("conv_b", 2), ("conv_ln_g", 2), ("conv_ln_b", 2)):
        sp.dma_start(b.rows[r:r + n, :], a[name][l, :].rearrange("(n p) -> n p", p=P)).then_inc(s.par_in.up, 16)
        r += n
    sp.dma_start(b.rows2[:, :], a["conv_w"][l, :, :].rearrange("t (m p) -> (t m) p", p=P)).then_inc(s.par_in.up, 16)
    sp.dma_start(b.fb[:, :], a["fox_fb"][l, :].rearrange("(h o) -> h o", o=1)).then_inc(s.par_in.up, 16)
    sp.dma_start(b.wff[:, :, :], a["w_in"][l, :, IN1["ff"]:IN1["ff"] + 4].rearrange("(k p) c -> p k c", p=P))\
      .then_inc(s.par_in.up, 16)
    sp.dma_start(b.decay[:, :, :], a["decay"]).then_inc(s.par_in.up, 16)
    for m in range(2):
        sp.dma_start(b.pw[:, m, :], a["pool_w"][l, 2 * m:2 * m + 2, :, :].rearrange("e c d -> (e c) d"))\
          .then_inc(s.par_in.up, 16)
    with sp.Fori(0, 12) as i:
        for p in range(2):
            sp.wait_ge(s.a_acc.up, l * s.a_acc.per + i * 16 + (8 * p + 8))
            sp.dma_start(b.a_raw[p][:, :, :],
                         a["ada_w"][l, :, :].rearrange("(k p) c -> p k c", p=P)[:, :, bass.ts(i * 2 + p, G)]
                         ).then_inc(s.a_in[p].up, 16)
    for j, name in enumerate(UNIT_COLS1):
        sp_weights(sp, e, lay, j, a["w_in"], l, IN1[name])
    for j in range(4):
        sp_weights(sp, e, lay, 10 + j, a["w_out"], l, G * j)
    sp_ffn(sp, e, lay, 14, a["ffn_w1"], a["ffn_w3"], 0, a["ffn_w2"], l)


def sp_layer2(sp, e, l):
    a, b, s = e.a, e.b, e.s
    lay = Layer(s, 2, l)
    for m in range(2):
        sp.wait_ge(*lay.bank_free(m, 0))
    for n, name in enumerate(("ln1_g_2", "ln1_b_2", "ln2_g_2", "ln2_b_2")):
        sp.dma_start(b.n_rows[8 * n:8 * n + 8, :], a[name][l, :].rearrange("(n p) -> n p", p=P)).then_inc(s.in2.up, 16)
    sp.dma_start(b.n_wiw[:, :, :], a["w_in_2"][l, :, IN2["wi"]:IN2["wi"] + 4].rearrange("(k p) c -> p k c", p=P))\
      .then_inc(s.in2.up, 16)
    sp.dma_start(b.n_g[:, :], a["sgu_ln_g_2"][l, :].partition_broadcast(P)).then_inc(s.in2.up, 16)
    sp.dma_start(b.n_b[:, :], a["sgu_ln_b_2"][l, :].partition_broadcast(P)).then_inc(s.in2.up, 16)
    sp.dma_start(b.n_sw[:, :, :], a["sgu_w_2"][l, :, :, :].rearrange("g t s -> t g s")).then_inc(s.in2.up, 16)
    sp.dma_start(b.n_sb[:, :], a["sgu_b_2"][l, :, :]).then_inc(s.in2.up, 16)
    c, n = e.at["pairs"]
    sp.dma_start(b.pairs[:, :, :].rearrange("p a b -> p (a b)"), a["table"][0:8, c:c + n]).then_inc(s.in2.up, 16)
    c, n = e.at["turn2"]
    sp.dma_start(b.turn[:, :], a["table"][:, c:c + n]).then_inc(s.in2.up, 64)
    w = a["w_in_2"]

    def piece(c0, n):
        return w[l, :, c0:c0 + n].rearrange("(k p) c -> p k c", p=P)

    sp_weights(sp, e, lay, 0, w, l, IN2["qi"])
    lone_wait(sp, s, *s.raw_free(lay.pair(0), 1))
    dst = w8(b.raw[1])
    sp.dma_start(dst[:, :, 0:P], piece(IN2["v"], P)).then_inc(s.raw[1].up, 32)
    for at in (P, P + HD):
        sp.dma_start(dst[:, :, at:at + HD], piece(IN2["ki"], HD)).then_inc(s.raw[1].up, 16)
    lone_wait(sp, s, *s.raw_free(lay.pair(1), 0))
    dst = w8(b.raw[0])
    for n in range(4):
        sp.dma_start(dst[:, :, n * HD:(n + 1) * HD], piece(IN2["k"] + HD * (n // 2), HD)).then_inc(s.raw[0].up, 16)
    for j, c0 in enumerate((IN2["q"], IN2["q"] + G, IN2["u"], IN2["u"] + G, IN2["vs"], IN2["vs"] + G)):
        sp_weights(sp, e, lay, 3 + j, w, l, c0)
    for j in range(4):
        sp_weights(sp, e, lay, 9 + j, a["w_o_2"], l, G * j)
    sp_unit(sp, e, lay, 6, 1, b.raw[1][:, :].rearrange("p (k c) -> p k c", k=2),
            a["w_ple_2"][l, :, :].rearrange("(k p) c -> p k c", p=P))
    sp_weights(sp, e, lay, 14, a["w_ple_gate_2"], l, 0)
    for m in range(2):
        lone_wait(sp, s, *lay.bank_free(m, Q2_PLE))
    sp.dma_start(b.e_p[:, :, :], a["p_2"][l, 0, :, :].rearrange("(t p) c -> p t c", p=P)).then_inc(s.p_in.up, 16)
    for j in range(1, 4):
        sp_weights(sp, e, lay, 14 + j, a["w_ple_gate_2"], l, G * j)
    sp_ffn(sp, e, lay, 18, a["w_ffn_in_2"], a["w_ffn_in_2"], FF, a["w_ffn_out_2"], l)


def sp_program(sp, e):
    a, b, s = e.a, e.b, e.s
    for dst, src in ((b.z_tab[:, :], a["table"]),
                     (b.z_x[:, :, :], a["x"][0, :, :].rearrange("(t p) d -> p t d", p=P)),
                     (b.z_c[:, :], a["c"][0, :].rearrange("(n p) -> n p", p=P)),
                     (b.z_fg[:, :], a["final_g"].rearrange("(n p) -> n p", p=P))):
        sp.dma_start(dst, src).then_inc(s.z_in.up, 16)
    sp.wait_ge(s.z_copied.up, Z_COPIES)
    sp.wait_ge(s.z_xt.up, KD + 2)
    sp.dma_start(b.t_pi[:, :], a["positions"].partition_broadcast(P)).then_inc(s.trig_in.up, 16)
    sp.wait_ge(s.trig_sin.up, 3)
    with sp.Fori(0, DEPTH) as l:
        sp_layer1(sp, e, l)
    lay = Layer(s, 1, DEPTH)
    for m in range(2):
        sp.wait_ge(*lay.bank_free(m, 0))
    sp.wait_ge(*s.hf(2 * DEPTH, KD))
    sp.dma_start(b.t_pi[:, :], a["positions_2"].partition_broadcast(P)).then_inc(s.trig_in.up, 16)
    with sp.Fori(0, DEPTH) as l:
        sp_layer2(sp, e, l)
    for t in range(NB):
        sp.wait_ge(s.y.up, 2 * t + 2)
        sp.dma_start(e.out[0, t * P:(t + 1) * P, :], b.y_out[:, t, :]).then_inc(s.y_out.up, 16)
    sp.wait_ge(s.y_out.up, 16 * NB)



def act_split(act, e, lay, j2, p, n=2048):
    s, b, u = e.s, e.b, lay.pair(j2)
    act.wait_ge(*s.raw_in(u, p))
    act.wait_ge(*s.slot_free(u, p))
    act.activation(b.w_hi[p][:, 0:n], b.raw[p][:, 0:n], ACT.Copy).then_inc(s.hi.up, 1)


def act_rms(act, e, c, ready, gain, shift, full):
    s, b, bank = e.s, e.b, e.bank
    for k in range(KD):
        ready(act, k)
        act.activation(b.sq[:, k, :], b.x[:, k, :], ACT.Square).then_inc(s.sq.up, 1)
    act.preload_act_table_set("natural_log_exp_and_others")
    act.wait_ge(*s.rms(c, 1))
    act.activation(b.r[:, :], bank[7][:, :], ACT.Ln, bias=b.eps[:, 0:1], scale=1.0 / D).then_inc(s.r_ln.up, 1)
    act.wait_ge(*s.r_ln(c, 1))
    act.activation(b.r[:, :], b.r[:, :], ACT.Exp, scale=-0.5).then_inc(s.r.up, 1)
    if full:
        for k in range(KD):
            act.wait_ge(*s.xr(c, k + 1))
            act.activation(b.h_hi[:, k, :], b.sq[:, k, :], ACT.Identity,
                           bias=0.0 if shift is None else shift[:, k:k + 1],
                           scale=gain[:, k:k + 1]).then_inc(s.hh.up, 1)


def act_ffn(act, e, lay, j0, q0):
    s, b, bank = e.s, e.b, e.bank
    act.preload_act_table(ACT.Silu)

    def body(i, last):
        for m in range(2):
            act.wait_ge(*s.tile(lay.pair(i + j0 // 2), 0, m))
            act.wait_ge(*s.upb[m](lay.ffn, i))
            act.activation(b.f_act[:, m, :], bank[m][:, :], ACT.Silu).then_inc(s.bank[m].up, 1)
        n = 11 * P if last else 2048
        act_split(act, e, lay, i + (j0 // 2 + 1), 0, n)
        for m in range(2):
            act.wait_ge(*s.upb[m](lay.ffn, i + 1))
            act.activation(cols(b.f_hi, i * 2 + m), b.f_full[:, m, :], ACT.Copy).then_inc(s.fh.up, 1)
        act_split(act, e, lay, i + (j0 // 2 + 1), 1, n)

    with act.Fori(0, 10) as i:
        body(i, False)
    body(10, True)
    with act.Fori(0, 7) as i:
        for p in range(2):
            act_split(act, e, lay, i + (j0 // 2 + 12), p, 11 * P)


def act_attn_exp(act, e, blk, l, h, prob):
    s, b, bank = e.s, e.b, e.bank
    t = attention(s, blk)
    if h >= 1:
        act.wait_ge(*t.tp(l, 3 * h))
    for g, blocks in enumerate(BY_QUERY):
        act.wait_ge(*t.mx(l, 3 * h + g + 1))
        for i in blocks:
            c = 0 if len(blocks) == 1 else (0 if i == 0 else P)
            act.activation(prob[:, P_AT[i]:P_AT[i] + CAUSAL[i]], bank[SC_BANK[g]][:, c:c + CAUSAL[i]], ACT.Exp,
                           bias=b.small[:, i:i + 1], scale=HD ** -0.5,
                           accum_out=b.small[:, 4 + i:5 + i]).then_inc(t.ex.up, 1)


def act_attn_pt(act, e, blk, l, h, probT):
    s, bank = e.s, e.bank
    t = attention(s, blk)
    if h >= 1:
        act.wait_ge(*t.pv(l, h))
    for g, blocks in enumerate(BY_KEY):
        act.wait_ge(*t.tp(l, 3 * h + g + 1))
        for j in blocks:
            c, n = (0 if j != 3 else 384), T - P * j
            op = act.activation(probT[:, PT_AT[j]:PT_AT[j] + n], bank[TP_BANK[g]][:, c:c + n], ACT.Copy)
        op.then_inc(t.pt.up, 1)


def act_attn_out(act, e, blk, l, h, mf, tile):
    s, bank = e.s, e.bank
    t = attention(s, blk)
    o = HD * (h % 2)
    act.wait_ge(*t.pv(l, h + 1))
    act.activation(mf[o:o + HD, tile, :], bank[5][o:o + HD, :], ACT.Copy).then_inc(t.po.up, 1)


SC_BANK = [3, 4, 2]
TP_BANK = [6, 7, 5]


def act_layer1(act, e, l):
    s, b, bank = e.s, e.b, e.bank
    lay = Layer(s, 1, l)
    act_split(act, e, lay, 0, 0)
    act_split(act, e, lay, 0, 1)

    def x_ready(eng, k):
        if k == 0:
            eng.wait_ge(*lay.bank_free(0, 0))
            eng.wait_ge(*lay.bank_free(1, 0))
            eng.wait_ge(*s.gain(l, 2))

    act_rms_pair(act, e, l, 0, x_ready)
    act.wait_ge(*s.ls_d(l, 1))
    act.activation(b.ls[:, 0, :], b.ls[:, 1, :], ACT.Abs).then_inc(s.ls_a.up, 1)
    act.wait_ge(*s.ls_a(l, 1))
    act.activation(b.ls[:, 0, :], b.ls[:, 0, :], ACT.Exp, scale=-1.0).then_inc(s.ls_a.up, 1)
    act.wait_ge(*s.ls_a(l, 2))
    act.activation(b.ls[:, 0, :], b.ls[:, 0, :], ACT.Ln, bias=b.eps[0:4, 3:4]).then_inc(s.ls_a.up, 1)

    def take(j, m, out, func=ACT.Copy):
        act.wait_ge(*s.tile(lay.pair(j // 2), j % 2, m))
        act.activation(out, bank[m][:, :], func).then_inc(s.bank[m].up, 1)

    def split(j):
        act_split(act, e, lay, j // 2, j % 2)

    for m in range(2):
        take(0, m, b.cgate[:, m, 0:T], ACT.Sigmoid)
    act.preload_act_table_set("natural_log_exp_and_others")
    split(2)
    split(3)
    for j in (2, 3):
        for m in range(2):
            if j == 3:
                act.wait_ge(*s.rot(l, m + 1))
                act.wait_ge(*s.rope(l, 3 * m + 1))
            take(j, m, b.rraw[:, m, :])
        split(j + 2)
    for m in range(2):
        take(4, m, b.rv[:, 2 * m:2 * m + 2, :].rearrange("p t c -> p (t c)"))
    split(6)
    for m in range(2):
        take(5, m, b.fq[:, m, :])
    act.wait_ge(*s.ls_d(l, 3))
    act.activation(b.cum[0:4, :], b.ls[:, 2, :], ACT.Copy).then_inc(s.ck.up, 1)
    split(7)
    for m in range(2):
        take(6, m, b.fk[:, m, :])
    split(8)
    for m in range(2):
        take(7, m, b.fv[:, 2 * m:2 * m + 2, :].rearrange("p t c -> p (t c)"))
    split(9)
    for m in range(2):
        act.wait_ge(*s.pads(l, 2))
        take(8, m, b.pu[:, m, 16:16 + T])
    split(10)
    act_attn_exp(act, e, 1, l, 0, b.prob)
    for m in range(2):
        take(9, m, b.rg[:, m, :], ACT.Silu)
    act.preload_act_table_set("natural_log_exp_and_others")
    split(11)
    act_attn_pt(act, e, 1, l, 0, b.probT)
    act_attn_exp(act, e, 1, l, 1, b.prob)
    for m in range(2):
        act.wait_ge(*s.gn_x(l, m + 1))
        act.activation(b.ln_s[:, m, :], b.ln_d[:, m, :], ACT.Square).then_inc(s.gn_sq.up, 1)
    act_attn_out(act, e, 1, l, 0, b.mf, 0)
    act_attn_pt(act, e, 1, l, 1, b.probT)
    act_attn_exp(act, e, 1, l, 2, b.prob)
    for m in range(2):
        act.wait_ge(*s.gn_ps(l, 2 + m + 1))
        act.activation(b.ln_s[:, m, :], bank[m][:, :], ACT.Ln, bias=b.eps[:, 0:1]).then_inc(s.bank[m].up, 1)
        act.wait_ge(*lay.bank_out(m, Q_GN2))
        act.activation(b.ln_s[:, m, :], b.ln_s[:, m, :], ACT.Exp, scale=-0.5).then_inc(s.gn_r.up, 1)
    for m in range(2):
        act.wait_ge(*s.pl_sum(l, 6))
        act.activation(b.cgate[HD:P, m, 16:], b.wb[HD:P, m, 16:], ACT.Copy).then_inc(s.pl_up.up, 1)
    act_attn_out(act, e, 1, l, 1, b.mf, 0)
    act_attn_pt(act, e, 1, l, 2, b.probT)
    act_attn_exp(act, e, 1, l, 3, b.prob)
    for m in range(2):
        act.wait_ge(*s.pl_ps(l, m + 1))
        act.activation(b.mf[:, 2 + m, :], bank[m][:, :], ACT.Identity, scale=b.par[:, 64 + m:65 + m])\
           .then_inc(s.bank[m].up, 1)
    act_attn_out(act, e, 1, l, 2, b.mf, 1)
    act_attn_pt(act, e, 1, l, 3, b.probT)
    for m in range(2):
        act.wait_ge(*s.cn_x(l, m + 1))
        act.activation(b.ln_s[:, m, :], b.ln_d[:, m, :], ACT.Square).then_inc(s.cn_sq.up, 1)
    act.wait_ge(*s.cn_ps(l, 2))
    act.activation(b.r[:, :], bank[1][:, :], ACT.Ln, bias=b.eps[:, 0:1], scale=1.0 / G).then_inc(s.bank[1].up, 1)
    act.wait_ge(*lay.bank_out(1, Q_CONV))
    act.activation(b.r[:, :], b.r[:, :], ACT.Exp, scale=-0.5).then_inc(s.cn_r.up, 1)
    act_attn_out(act, e, 1, l, 3, b.mf, 1)
    for m in range(2):
        act.wait_ge(*s.cn_xr(l, m + 1))
        act.activation(b.mf[:, 6 + m, :], b.ln_d[:, m, :], ACT.Silu, bias=b.par[:, 72 + m:73 + m],
                       scale=b.par[:, 70 + m:71 + m]).then_inc(s.cn_o.up, 1)
    act.wait_ge(*s.tile(lay.pair(4), 1, 1))
    for n, k in enumerate(MIX_ORDER):
        act.wait_ge(*{0: s.po(l, 2), 1: s.po(l, 4), 2: lay.bank_out(0, Q_POOL), 3: lay.bank_out(1, Q_POOL),
                      4: s.gn_o(l, 1), 5: s.gn_o(l, 2), 6: s.cn_o(l, 1), 7: s.cn_o(l, 2)}[k])
        act.activation(b.h_hi[:, k, :], b.mf[:, k, :], ACT.Copy).then_inc(s.mh.up, 1)
    split(12)
    split(13)
    split(14)
    split(15)

    def x_mixed(eng, k):
        eng.wait_ge(*lay.bank_out(k % 2, Q_OUT + k // 2))

    act_rms_pair(act, e, l, 1, x_mixed)
    act_ffn(act, e, lay, 14, Q_FFN)


def act_rms_pair(act, e, l, j, ready):
    b = e.b
    shift = b.mod[:, 0:8] if j == 0 else b.mod[:, 24:32]
    act_rms(act, e, l * 2 + j, ready, b.gain[:, 8 * j:8 * j + 8], shift, True)


def act_layer_norm(act, e, c, g0):
    s, b, bank = e.s, e.b, e.bank
    for k in range(KD):
        act.wait_ge(*s.ld(c, k + 1))
        act.activation(b.sq[:, k, :], b.x[:, k, :], ACT.Square).then_inc(s.lsq.up, 1)
    act.preload_act_table_set("natural_log_exp_and_others")
    act.wait_ge(*s.lvar(c, 1))
    act.activation(b.r[:, :], bank[7][:, :], ACT.Ln, bias=b.eps[:, 1:2], scale=1.0 / D).then_inc(s.l_ln.up, 1)
    act.wait_ge(*s.l_ln(c, 1))
    act.activation(b.r[:, :], b.r[:, :], ACT.Exp, scale=-0.5).then_inc(s.l_r.up, 1)
    for k in range(KD):
        act.wait_ge(*s.lxr(c, k + 1))
        act.activation(b.h_hi[:, k, :], b.sq[:, k, :], ACT.Identity, bias=b.par[:, g0 + 8 + k:g0 + 9 + k],
                       scale=b.par[:, g0 + k:g0 + k + 1]).then_inc(s.lhh.up, 1)


def act_layer2(act, e, l):
    s, b, bank = e.s, e.b, e.bank
    lay = Layer(s, 2, l)

    def split(j):
        act_split(act, e, lay, j // 2, j % 2)

    def take(j, m, out, func=ACT.Copy):
        act.wait_ge(*s.tile(lay.pair(j // 2), j % 2, m))
        act.activation(out, bank[m][:, :], func).then_inc(s.bank[m].up, 1)

    def raw(r, j, m):
        if r >= 2:
            act.wait_ge(*s.rot2(l, r - 1))
            act.wait_ge(*s.rope2(l, 3 * (r - 2) + 1))
        else:
            act.wait_ge(*s.swt(l, 8))
        take(j, m, b.n_raw[:, r % 2, :])

    split(0)
    split(1)
    raw(0, 0, 0)
    raw(1, 0, 1)
    split(2)
    take(1, 0, b.n_v[:, :, :].rearrange("p t c -> p (t c)"))
    raw(2, 1, 1)
    split(3)
    raw(3, 2, 0)
    raw(4, 2, 1)
    split(4)
    raw(5, 3, 0)
    raw(6, 3, 1)
    split(5)
    raw(7, 4, 0)
    raw(8, 4, 1)
    split(6)
    act.preload_act_table(ACT.Gelu_apprx_tanh)
    for j in (5, 6):
        for m in range(2):
            take(j, m, b.n_u[:, 2 * (j - 5) + m, :], ACT.Gelu_apprx_tanh)
        split(j + 2)
    for j in (7, 8):
        for m in range(2):
            act.wait_ge(*s.tile(lay.pair(j // 2), j % 2, m))
            act.activation(b.n_vs[:, 2 * m:2 * m + 2, (j - 7) * G:(j - 6) * G],
                           bank[m][:, :].rearrange("p (t c) -> p t c", t=2), ACT.Gelu_apprx_tanh)\
               .then_inc(s.bank[m].up, 1)
        split(j + 2)
    act.preload_act_table_set("natural_log_exp_and_others")
    act.wait_ge(*s.bn(l, 8))
    act.activation(b.n_st[:, :, 6:7], b.n_st[:, :, 1:2], ACT.Ln, bias=b.eps[:, 1:2]).then_inc(s.v_ln.up, 1)
    act.wait_ge(*s.v_ln(l, 1))
    act.activation(b.n_st[:, :, 6:7], b.n_st[:, :, 6:7], ACT.Exp, scale=-0.5).then_inc(s.v_r.up, 1)
    for h in range(8):
        act_attn_exp(act, e, 2, l, h, b.n_prob)
        if h >= 1:
            act_attn_out(act, e, 2, l, h - 1, b.mf, (h - 1) // 2)
        act_attn_pt(act, e, 2, l, h, b.n_probT)
    act_attn_out(act, e, 2, l, 7, b.mf, 3)
    act.wait_ge(*s.tile(lay.pair(4), 0, 1))
    for n, k in enumerate(MIX2_ORDER):
        act.wait_ge(*(s.po2(l, 2 * k + 2) if k < 4 else lay.bank_out(k % 2, Q2_SGU + (k - 4) // 2)))
        act.activation(b.h_hi[:, k, :], b.mf[:, k, :], ACT.Copy).then_inc(s.mh2.up, 1)
    split(11)
    split(12)
    act_split(act, e, lay, 6, 1)
    split(14)
    for m in range(2):
        act.wait_ge(*s.p_t(l, m + 1))
        act.activation(b.e_pf[:, m, :], bank[2 + m][:, :], ACT.Copy).then_inc(s.p_f.up, 1)
    for m in range(2):
        act.wait_ge(*s.p_f(l, m + 1))
        act.activation(b.e_hi[:, m, :], b.e_pf[:, m, :], ACT.Copy).then_inc(s.p_h.up, 1)
    act_layer_norm(act, e, l * 2, 0)
    for k in range(KD):
        if k < KD - 1:
            act.wait_ge(*s.ple(l, k + 1))
        else:
            act.wait_ge(*s.tile(lay.pair(6), 1, 1))
        act.activation(b.e_ple[:, k, :], bank[k % 2][:, :], ACT.Copy).then_inc(s.bank[k % 2].up, 1)
    split(15)
    for k in range(KD):
        if k >= 2:
            act.wait_ge(*s.gx(l, 2 * (k - 2) + 2))
        take(14 + k // 2, k % 2, b.e_sig[:, k % 2, :], ACT.Sigmoid)
        if k % 2:
            split(16 + k // 2)
    act_ffn(act, e, lay, 18, Q2_FFN)
    act_layer_norm(act, e, l * 2 + 1, 16)


def act_program(act, e):
    s, b, bank = e.s, e.b, e.bank
    act.sem_inc(s.lhh.up, s.lhh.credit)
    act.wait_ge(s.z_in.up, 64)
    act.activation(b.z_cs[:, :], b.z_c[:, :], ACT.Silu).then_inc(s.z_act.up, 1)
    act_trig(act, e, 0)
    act.wait_ge(s.z_x.up, KD)
    with act.Fori(0, DEPTH) as l:
        act_layer1(act, e, l)
    lay = Layer(s, 1, DEPTH)

    def x_ready(eng, k):
        if k == 0:
            for m in range(2):
                eng.wait_ge(*lay.bank_free(m, 0))

    act_rms(act, e, 2 * DEPTH, x_ready, b.fg, None, True)
    act_trig(act, e, 1)
    with act.Fori(0, DEPTH) as l:
        act_layer2(act, e, l)


def act_trig(act, e, which):
    s, b = e.s, e.b
    act.wait_ge(s.trig.up, 8 * which + 8)
    act.activation(b.sine[:, :], b.t_a[:, :], ACT.Sin).then_inc(s.trig_sin.up, 1)
    act.activation(b.t_b[:, :], b.t_a[:, :], ACT.Abs).then_inc(s.trig_sin.up, 1)
    act.wait_ge(s.trig_sin.up, 3 * which + 2)
    act.activation(b.cosine[:, :], b.t_b[:, :], ACT.Sin, bias=b.eps[:, 2:3], scale=-1.0).then_inc(s.trig_sin.up, 1)



def pool_split(pool, e, lay, j2, p, n=2048):
    s, b, u = e.s, e.b, lay.pair(j2)
    pool.wait_ge(*s.hi_in(u, p))
    pool.tensor_tensor(b.w_lo[p][:, 0:n], b.raw[p][:, 0:n], b.w_hi[p][:, 0:n].bitcast(F32), ALU.subtract)\
        .then_inc(s.lo.up, 1)


def pool_h_lo(pool, e, c, full=None):
    s, b = e.s, e.b
    full = b.hf if full is None else full
    for k in range(KD):
        pool.wait_ge(*s.hf(c, k + 1))
        pool.wait_ge(*s.hh(c, k + 1))
        pool.tensor_tensor(b.h_lo[:, k, :], full[:, k, :], b.h_hi[:, k, :].bitcast(F32), ALU.subtract)\
            .then_inc(s.hl.up, 1)


def pool_ffn(pool, e, lay, j0):
    s, b = e.s, e.b

    def body(i, last):
        n = 11 * P if last else 2048
        pool_split(pool, e, lay, i + (j0 // 2 + 1), 0, n)
        for m in range(2):
            pool.wait_ge(s.fh.up, lay.ffn * 22 + i * 2 + (m + 1))
            pool.tensor_tensor(cols(b.f_lo, i * 2 + m), b.f_full[:, m, :], cols(b.f_hi, i * 2 + m).bitcast(F32),
                               ALU.subtract).then_inc(s.fl.up, 1)
        pool_split(pool, e, lay, i + (j0 // 2 + 1), 1, n)

    with pool.Fori(0, 10) as i:
        body(i, False)
    body(10, True)
    with pool.Fori(0, 7) as i:
        for p in range(2):
            pool_split(pool, e, lay, i + (j0 // 2 + 12), p, 11 * P)


def pool_window(pool, e, l):
    s, b = e.s, e.b
    lay = Layer(s, 1, l)
    steps = [(b.cgate, b.pu, 0, 0, 1, 2), (b.wb, b.cgate, 0, HD, 2, 4),
             (b.cgate, b.pu, 1, 0, 1, 2), (b.wb, b.cgate, 1, 0, 2, 4), (b.cgate, b.wb, 1, 0, 4, 8),
             (b.wb, b.cgate, 1, HD, 8, 16)]
    for n, (dst, src, m, lo, back, at) in enumerate(steps):
        pool.wait_ge(*lay.bank_out(m, 8))
        if n:
            pool.wait_ge(*s.pl_sum(l, n))
        pool.tensor_tensor(dst[lo:P, m, at:], src[lo:P, m, at:], src[lo:P, m, at - back:T + 16 - back], ALU.add)\
            .then_inc(s.pl_sum.up, 1)


def pool_layer1(pool, e, l):
    s, b = e.s, e.b
    lay = Layer(s, 1, l)
    for m in range(2):
        lone_wait(pool, s, *lay.bank_free(m, 0))
    pool.memset(b.ch[:, :, 0:TAPS - 1], 0.0).then_inc(s.pads.up, 1)
    pool.memset(b.pu[:, :, 0:16], 0.0).then_inc(s.pads.up, 1)
    for j in range(2):
        pool_split(pool, e, lay, 0, j)
    pool_h_lo(pool, e, l * 2)
    for j in range(2, 12):
        pool_split(pool, e, lay, j // 2, j % 2)
    pool_window(pool, e, l)
    for n, k in enumerate(MIX_ORDER):
        pool.wait_ge(*s.mh(l, n + 1))
        pool.tensor_tensor(b.h_lo[:, k, :], b.mf[:, k, :], b.h_hi[:, k, :].bitcast(F32), ALU.subtract)\
            .then_inc(s.ml.up, 1)
    for j in range(12, 16):
        pool_split(pool, e, lay, j // 2, j % 2)
    pool_h_lo(pool, e, l * 2 + 1)
    pool_ffn(pool, e, lay, 14)


def pool_layer_norm(pool, e, c):
    s, b = e.s, e.b
    for k in range(KD):
        pool.wait_ge(*s.lx(c, k + 1))
        pool.wait_ge(*s.lhh(c, k + 1))
        pool.tensor_tensor(b.h_lo[:, k, :], b.x[:, k, :], b.h_hi[:, k, :].bitcast(F32), ALU.subtract)\
            .then_inc(s.lhl.up, 1)


def pool_layer2(pool, e, l):
    s, b = e.s, e.b
    lay = Layer(s, 2, l)
    for j in range(11):
        pool_split(pool, e, lay, j // 2, j % 2)
    for t in range(NB):
        pool.wait_ge(*s.v_n(l, t + 1))
        pool.tensor_tensor(b.n_vs[:, t, :], b.n_vs[:, t, :], b.n_g[:, :], ALU.mult).then_inc(s.v_g.up, 1)
        pool.wait_ge(*s.v_g(l, 2 * t + 1))
        pool.tensor_tensor(b.n_vs[:, t, :], b.n_vs[:, t, :], b.n_b[:, :], ALU.add).then_inc(s.v_g.up, 1)
    for n, k in enumerate(MIX2_ORDER):
        pool.wait_ge(*s.mh2(l, n + 1))
        pool.tensor_tensor(b.h_lo[:, k, :], b.mf[:, k, :], b.h_hi[:, k, :].bitcast(F32), ALU.subtract)\
            .then_inc(s.ml2.up, 1)
    for j in range(11, 15):
        pool_split(pool, e, lay, j // 2, j % 2)
    for m in range(2):
        pool.wait_ge(*s.p_h(l, m + 1))
        pool.tensor_tensor(b.e_lo[:, m, :], b.e_pf[:, m, :], b.e_hi[:, m, :].bitcast(F32), ALU.subtract)\
            .then_inc(s.p_l.up, 1)
    pool_layer_norm(pool, e, l * 2)
    for j in range(15, 20):
        pool_split(pool, e, lay, j // 2, j % 2)
    pool_ffn(pool, e, lay, 18)
    pool_layer_norm(pool, e, l * 2 + 1)


def pool_program(pool, e):
    s, b = e.s, e.b
    pool.sem_inc(s.lo.up, s.lo.credit)
    pool.sem_inc(s.fl.up, s.fl.credit)
    pool.wait_ge(s.trig_sin.up, 3)
    pool.sem_inc(s.lhl.up, s.lhl.credit)
    with pool.Fori(0, DEPTH) as l:
        pool_layer1(pool, e, l)
    pool_h_lo(pool, e, 2 * DEPTH, b.x)
    with pool.Fori(0, DEPTH) as l:
        pool_layer2(pool, e, l)



COPIES = [("eye", "eye"), ("turn1", "t0"), ("heads", "heads"), ("tril", "tril"), ("eye", "eye_r"),
          ("causal", "causal_r"), ("chunked", "chunked_r"), ("pick", "pick_r"),
          ("freq1", "f0"), ("freq2", "f1"), ("window", "window"), ("counts", "counts")]
Z_COPIES = len(COPIES)
C1 = 6.28125
C2 = float(np.float32(round((2 * np.pi - C1) * 2 ** 21) / 2 ** 21))
C3 = float(np.float32(2 * np.pi - C1 - C2))


def dve_trig(dve, e, which):
    s, b = e.s, e.b
    n = [8 * which]

    def done(op):
        op.then_inc(s.trig.up, 1)
        n[0] += 1
        dve.wait_ge(s.trig.up, n[0])

    done(dve.tensor_copy(b.t_pf[:, :], b.t_pi[:, :]))
    done(dve.tensor_scalar(b.t_ang[:, :], b.t_pf[:, :], b.freq[:, which:which + 1], None, ALU.mult))
    done(dve.tensor_scalar(b.t_ni[:, :], b.t_ang[:, :], 1.0 / (2 * np.pi), None, ALU.mult))
    done(dve.tensor_copy(b.t_n[:, :], b.t_ni[:, :]))
    done(dve.scalar_tensor_tensor(b.t_a[:, :], b.t_n[:, :], -C1, b.t_ang[:, :], ALU.mult, ALU.add))
    done(dve.scalar_tensor_tensor(b.t_b[:, :], b.t_n[:, :], -C2, b.t_a[:, :], ALU.mult, ALU.add))
    done(dve.scalar_tensor_tensor(b.t_a[:, :], b.t_n[:, :], -C3, b.t_b[:, :], ALU.mult, ALU.add))
    dve.tensor_scalar(b.t_a[:, :], b.t_a[:, :], -3.1415925, 3.1415925, ALU.max, ALU.min).then_inc(s.trig.up, 1)


def dve_setup(dve, e):
    b, s, bank = e.b, e.s, e.bank
    dve.memset(b.ones[:, :], 1.0).then_inc(s.z_ready.up, 1)
    for n, v in enumerate((EPS, LN_EPS, float(np.pi / 2), 1.0)):
        dve.memset(b.eps[:, n:n + 1], v).then_inc(s.z_ready.up, 1)
    dve.wait_ge(s.z_in.up, 64)
    dst = dict(eye=b.eye, t0=b.turn, heads=b.heads, tril=b.tril, eye_r=b.eye_r, causal_r=b.causal_r,
               chunked_r=b.chunked_r, window=b.window)
    for src, name in COPIES:
        c, n = e.at[src]
        if name == "pick_r":
            op = dve.tensor_copy(b.pick_r[:, :, :].rearrange("p a b -> p (a b)"), b.z_tab[:, c:c + n])
        elif name == "counts":
            op = dve.tensor_copy(b.counts[:, :, :].rearrange("p a b -> p (a b)"), b.z_tab[:, c:c + n])
        elif name in ("f0", "f1"):
            op = dve.tensor_copy(b.freq[:, int(name[1]):int(name[1]) + 1], b.z_tab[:, c:c + n])
        else:
            op = dve.tensor_copy(dst[name][:, :], b.z_tab[:, c:c + n])
        op.then_inc(s.z_copied.up, 1)
    for k in range(KD):
        dve.wait_ge(s.z_xt.up, k + 1)
        dve.tensor_copy(b.x[:, k, :], bank[2 + k % 4][:, :]).then_inc(s.z_x.up, 1)
    dve.wait_ge(s.z_xt.up, KD + 1)
    dve.tensor_copy(b.c[:, :], bank[6][:, 0:KD]).then_inc(s.z_x.up, 1)
    dve.wait_ge(s.z_xt.up, KD + 2)
    dve.tensor_copy(b.fg[:, :], bank[7][:, 0:KD]).then_inc(s.z_x.up, 1)
    dve.wait_ge(s.z_copied.up, Z_COPIES)
    dve.wait_ge(s.trig_in.up, 16)
    dve_trig(dve, e, 0)


def dve_modulation(dve, e, l):
    s, b, bank = e.s, e.b, e.bank
    for n, (dst, w, k) in enumerate(((b.par, 74, 4), (b.taps, 2 * TAPS, 5))):
        dve.wait_ge(*s.par_t(l, n + 1))
        dve.tensor_copy(dst[:, 0:w], bank[k][:, 0:w]).then_inc(s.par.up, 1)
    with dve.Fori(0, 12) as i:
        for p in range(2):
            acc, raw = b.a_acc[p], b.a_raw[p]
            base = l * s.a_acc.per + i * 16 + (s.a_acc.credit + 8 * p)
            dve.wait_ge(s.a_in[p].up, l * 192 + i * 16 + 16)
            dve.wait_ge(s.a_pe.up, l * 24 + i * 2 + (p + 1))
            dve.tensor_scalar(acc[:, :], raw[:, 0, :], b.c[:, 0:1], None, ALU.mult).then_inc(s.a_acc.up, 1)
            for k in range(1, KD):
                dve.wait_ge(s.a_acc.up, base + k)
                dve.scalar_tensor_tensor(acc[:, :], raw[:, k, :], b.c[:, k:k + 1], acc[:, :], ALU.mult, ALU.add)\
                   .then_inc(s.a_acc.up, 1)
    dve.wait_ge(*s.a_pe(l, 24))
    dve.wait_ge(*s.par(l, 2))
    dve.tensor_tensor(b.mod[:, :], bank[6][:, 0:MODS], b.par[:, 16:16 + MODS], ALU.add).then_inc(s.mod.up, 1)
    dve.wait_ge(*s.mod(l, 1))
    for j in range(2):
        dve.scalar_tensor_tensor(b.gain[:, 8 * j:8 * j + 8], b.mod[:, 8 + 24 * j:16 + 24 * j], 1.0,
                                 b.par[:, 8 * j:8 * j + 8], ALU.add, ALU.mult).then_inc(s.gain.up, 1)


def dve_rms(dve, e, c, gain, shift, final=False):
    s, b = e.s, e.b
    for k in range(1, KD):
        dve.wait_ge(*s.sq(c, k + 1))
        if k > 1:
            dve.wait_ge(*s.ssq(c, k - 1))
        dve.tensor_tensor(b.sq[:, 0, :], b.sq[:, 0, :], b.sq[:, k, :], ALU.add).then_inc(s.ssq.up, 1)
    dve.wait_ge(*s.r(c, 1))

    def finish(k):
        dve.wait_ge(*s.xr(c, k + 1))
        if final:
            dve.tensor_scalar(b.x[:, k, :], b.sq[:, k, :], gain[:, k:k + 1], None, ALU.mult).then_inc(s.hf.up, 1)
        else:
            dve.tensor_scalar(b.hf[:, k, :], b.sq[:, k, :], gain[:, k:k + 1], shift[:, k:k + 1], ALU.mult, ALU.add)\
               .then_inc(s.hf.up, 1)

    for k in range(KD):
        dve.tensor_tensor(b.sq[:, k, :], b.x[:, k, :], b.r[:, :], ALU.mult).then_inc(s.xr.up, 1)
        if k:
            finish(k - 1)
    finish(KD - 1)


def dve_max(dve, e, blk, l, h):
    s, b, bank = e.s, e.b, e.bank
    t = attention(s, blk)
    if h:
        dve.wait_ge(*t.ex(l, 4 * h))
    for g, blocks in enumerate(BY_QUERY):
        dve.wait_ge(*t.sc(l, 3 * h + g + 1))
        for i in blocks:
            c = 0 if len(blocks) == 1 else (0 if i == 0 else P)
            dve.tensor_reduce(b.small[:, 16 + i:17 + i], bank[SC_BANK[g]][:, c:c + CAUSAL[i]], AX, ALU.max)\
               .then_inc(t.mxr.up, 1)
        n = (2, 3, 4)[g]
        dve.wait_ge(*t.mxr(l, 4 * h + n))
        first, step = blocks[0], (2 if g == 0 else 1)
        dve.tensor_scalar(b.small[:, first:blocks[-1] + 1:step], b.small[:, 16 + first:17 + blocks[-1]:step],
                          -HD ** -0.5, None, ALU.mult).then_inc(t.mx.up, 1)


def dve_normalise(dve, e, blk, l, h, prob):
    s, b = e.s, e.b
    t = attention(s, blk)
    dve.wait_ge(*t.ex(l, 4 * h + 4))
    dve.reciprocal(b.small[:, 8:12], b.small[:, 4:8]).then_inc(t.rcp.up, 1)
    dve.wait_ge(*t.rcp(l, h + 1))
    for i in (0, 2, 1, 3):
        v = prob[:, P_AT[i]:P_AT[i] + CAUSAL[i]]
        dve.tensor_scalar(v, v, b.small[:, 8 + i:9 + i], None, ALU.mult).then_inc(t.pn.up, 1)


def dve_ffn(dve, e, lay, j0, gate):
    s, b, bank = e.s, e.b, e.bank

    def body(i):
        for m in range(2):
            dve.wait_ge(*s.tile(lay.pair(i + j0 // 2), 1, m))
            dve.wait_ge(lay.s.bank[m].up, lay.use0 + i + (gate[0] + 2))
            dve.wait_ge(s.fl.up, lay.ffn * 22 + i * 2 + (m + 1))
            dve.tensor_tensor(b.f_full[:, m, :], b.f_act[:, m, :], bank[2 + m][:, :], ALU.mult)\
               .then_inc(s.upb[m].up, 1)

    with dve.Fori(0, 11) as i:
        body(i)


def dve_layer1(dve, e, l):
    s, b, bank = e.s, e.b, e.bank
    lay = Layer(s, 1, l)
    dve_modulation(dve, e, l)
    dve.wait_ge(*s.gain(l, 2))
    dve_rms(dve, e, l * 2, b.gain, b.mod[:, 0:8])
    dve.wait_ge(*s.ff(l, 1))
    dve.memset(b.ls[:, 3, :], 1.0).then_inc(s.ls_1.up, 1)
    dve.memset(b.cum[:, :].bitcast(F32), 0.0).then_inc(s.ls_1.up, 1)
    dve.tensor_scalar(b.ls[:, 1, :], bank[2][0:4, :], b.fb[:, 0:1], None, ALU.add).then_inc(s.ls_d.up, 1)
    dve.wait_ge(*s.ls_d(l, 1))
    dve.wait_ge(*s.ls_a(l, 3))
    dve.scalar_tensor_tensor(b.ls[:, 1, :], b.ls[:, 1, :], 0.0, b.ls[:, 0, :], ALU.min, ALU.subtract)\
       .then_inc(s.ls_d.up, 1)
    dve.wait_ge(*s.ls_d(l, 2))
    dve.wait_ge(*s.ls_1(l, 2))
    dve.tensor_tensor_scan(b.ls[:, 2, :], b.ls[:, 3, :], b.ls[:, 1, :], 0.0, ALU.mult, ALU.add)\
       .then_inc(s.ls_d.up, 1)
    for m in range(2):
        dve.wait_ge(*s.tile(lay.pair(0), 1, m))
        dve.wait_ge(*lay.bank_out(m, 0))
        dve.tensor_tensor(b.ch[:, m, TAPS - 1:], bank[m][:, :], b.cgate[:, m, 0:T], ALU.mult)\
           .then_inc(s.bank[m].up, 1)

    def conv(steps):
        for n in steps:
            t, m = n // 2, n % 2
            if n < 2:
                dve.wait_ge(*lay.bank_out(m, 1))
                dve.wait_ge(*s.pads(l, 2))
                dve.tensor_scalar(b.cv[:, m, :], b.ch[:, m, 0:T], b.taps[:, m:m + 1], b.par[:, 68 + m:69 + m],
                                  ALU.mult, ALU.add).then_inc(s.conv.up, 1)
            else:
                dve.wait_ge(*s.conv(l, n - 1))
                dve.scalar_tensor_tensor(b.cv[:, m, :], b.ch[:, m, t:t + T], b.taps[:, n:n + 1], b.cv[:, m, :],
                                         ALU.mult, ALU.add).then_inc(s.conv.up, 1)

    def rope(n):
        m, dst = n % 2, (b.rq if n < 2 else b.rk)
        dve.wait_ge(*lay.bank_out(m, 2 + n // 2))
        dve.tensor_tensor(dst[:, m, :], b.rraw[:, m, :], b.cosine[:, :], ALU.mult).then_inc(s.rope.up, 1)
        dve.wait_ge(*s.rot(l, n + 1))
        dve.tensor_tensor(b.ln_s[:, m, :], bank[2 + m][:, :], b.sine[:, :], ALU.mult).then_inc(s.rope.up, 1)
        dve.wait_ge(*s.rope(l, 3 * n + 2))
        dve.tensor_tensor(dst[:, m, :], dst[:, m, :], b.ln_s[:, m, :], ALU.add).then_inc(s.rope.up, 1)

    def decayed(h):
        if h:
            dve.wait_ge(*s.rv_ps(l, h))
        for g, blocks in enumerate(BY_KEY):
            dve.wait_ge(*s.rs_ps(l, 3 * h + g + 1))
            for j in blocks:
                c, n = (0 if j != 3 else 384), T - P * j
                dve.tensor_tensor(b.rs[:, PT_AT[j]:PT_AT[j] + n], bank[TP_BANK[g]][:, c:c + n],
                                  b.decay[:, h, 0:n], ALU.mult).then_inc(s.rs.up, 1)

    def retained(h):
        o = HD * (h % 2)
        dve.wait_ge(*s.rv_ps(l, h + 1))
        dve.tensor_copy(b.mf[o:o + HD, 4 + h // 2, :], bank[2][o:o + HD, :]).then_inc(s.rv_o.up, 1)

    conv(range(0, 8))
    rope(0)
    rope(1)
    dve.wait_ge(*s.ck(l, 1))
    dve.tensor_tensor(b.cum[32:36, :], b.ls[:, 2, :], b.cum[0:4, :].bitcast(F32), ALU.subtract)\
       .then_inc(s.ls_d.up, 1)
    conv(range(8, 12))
    rope(2)
    rope(3)
    conv(range(12, 24))
    decayed(0)
    conv(range(24, 34))
    retained(0)
    decayed(1)
    conv(range(34, 44))
    retained(1)
    decayed(2)
    conv(range(44, 54))
    retained(2)
    decayed(3)
    dve_max(dve, e, 1, l, 0)
    conv(range(54, 62))
    dve_normalise(dve, e, 1, l, 0, b.prob)
    retained(3)
    dve_max(dve, e, 1, l, 1)
    for m in range(2):
        dve.wait_ge(*s.gn_ps(l, m + 1))
        dve.tensor_tensor(b.ln_d[:, m, :], b.mf[:, 4 + m, :], bank[m][:, :], ALU.subtract).then_inc(s.gn_x.up, 1)
    dve_normalise(dve, e, 1, l, 1, b.prob)
    for m in range(2):
        dve.wait_ge(*s.gn_x(l, m + 1))
        dve.sem_inc(s.bank[m].up, 1)
    dve_max(dve, e, 1, l, 2)
    for m in range(2):
        dve.wait_ge(*s.gn_r(l, m + 1))
        dve.tensor_tensor(b.ln_d[:, m, :], b.ln_d[:, m, :], b.ln_s[:, m, :], ALU.mult).then_inc(s.gn_m.up, 1)
    for m in range(2):
        dve.wait_ge(*s.gn_m(l, m + 1))
        dve.wait_ge(*lay.bank_out(m, 9))
        dve.scalar_tensor_tensor(b.mf[:, 4 + m, :], b.ln_d[:, m, :], b.par[:, 66 + m:67 + m], b.rg[:, m, :],
                                 ALU.mult, ALU.mult).then_inc(s.gn_o.up, 1)
    for m in range(2):
        dve.wait_ge(*s.pl_up(l, m + 1))
        dve.scalar_tensor_tensor(b.wb[:, m, 0:T], b.cgate[:, m, 16:], b.window[:, m:m + 1], b.pu[:, m, 16:],
                                 ALU.mult, ALU.subtract).then_inc(s.pl_d.up, 1)
    dve.wait_ge(*s.pl_d(l, 2))
    dve.tensor_tensor(b.wb[:, :, 0:16], b.cgate[:, :, 16:32], b.counts[:, :, :], ALU.mult).then_inc(s.pl_d.up, 1)
    dve.wait_ge(*s.pl_d(l, 3))
    dve.tensor_tensor(b.wb[:, :, 0:16], b.wb[:, :, 0:16], b.pu[:, :, 16:32], ALU.subtract).then_inc(s.pl_d.up, 1)
    dve_normalise(dve, e, 1, l, 2, b.prob)
    dve_max(dve, e, 1, l, 3)
    dve.wait_ge(*s.cn_ps(l, 1))
    for m in range(2):
        dve.scalar_tensor_tensor(b.ln_d[:, m, :], bank[0][:, :], -1.0 / G, b.cv[:, m, :], ALU.mult, ALU.add)\
           .then_inc(s.cn_x.up, 1)
    dve_normalise(dve, e, 1, l, 3, b.prob)
    dve.wait_ge(*s.cn_x(l, 2))
    dve.sem_inc(s.bank[0].up, 1)
    dve.wait_ge(*s.cn_r(l, 1))
    for m in range(2):
        dve.tensor_tensor(b.ln_d[:, m, :], b.ln_d[:, m, :], b.r[:, :], ALU.mult).then_inc(s.cn_xr.up, 1)
    for k in range(KD):
        dve.wait_ge(*s.tile(lay.pair(5 + k // 4), k // 2 % 2, k % 2))
        dve.scalar_tensor_tensor(b.x[:, k, :], bank[k % 2][:, :], b.mod[:, 16 + k:17 + k], b.x[:, k, :],
                                 ALU.mult, ALU.add).then_inc(s.bank[k % 2].up, 1)
    dve_rms(dve, e, l * 2 + 1, b.gain[:, 8:16], b.mod[:, 24:32])
    dve_ffn(dve, e, lay, 14, (Q_FFN,))
    with dve.Fori(0, 4) as i:
        for m in range(2):
            dve.wait_ge(*s.tile(lay.pair(i * 2 + (18 + m)), 1, 1))
            xk = cols(b.x, i * 2 + m)
            dve.scalar_tensor_tensor(xk, bank[m][:, :], b.mod[:, bass.ds(i * 2 + (40 + m), 1)], xk,
                                     ALU.mult, ALU.add).then_inc(s.bank[m].up, 1)


def dve_layer_norm(dve, e, c, g0):
    s, b, bank = e.s, e.b, e.bank
    dve.wait_ge(*s.lmean(c, 1))
    for k in range(KD):
        dve.scalar_tensor_tensor(b.x[:, k, :], bank[6][:, :], -1.0 / D, b.x[:, k, :], ALU.mult, ALU.add)\
           .then_inc(s.ld.up, 1)
    dve.wait_ge(*s.l_r(c, 1))
    for k in range(KD):
        dve.wait_ge(*s.ld(c, k + 1))
        dve.tensor_tensor(b.sq[:, k, :], b.x[:, k, :], b.r[:, :], ALU.mult).then_inc(s.lxr.up, 1)
        dve.wait_ge(*s.lxr(c, k + 1))
        dve.tensor_scalar(b.x[:, k, :], b.sq[:, k, :], b.par[:, g0 + k:g0 + k + 1], b.par[:, g0 + 8 + k:g0 + 9 + k],
                          ALU.mult, ALU.add).then_inc(s.lx.up, 1)


def dve_add_up(dve, e, c, k, out):
    s, b = e.s, e.b
    if k == 0:
        return
    dve.wait_ge(*out(k))
    if k == 1:
        dve.wait_ge(*out(0))
        dve.tensor_tensor(b.r[:, :], b.x[:, 0, :], b.x[:, 1, :], ALU.add).then_inc(s.lsum.up, 1)
    else:
        dve.wait_ge(*s.lsum(c, k - 1))
        dve.tensor_tensor(b.r[:, :], b.r[:, :], b.x[:, k, :], ALU.add).then_inc(s.lsum.up, 1)


def dve_layer2(dve, e, l):
    s, b, bank = e.s, e.b, e.bank
    lay = Layer(s, 2, l)
    dve.wait_ge(*s.par2_t(l, 1))
    dve.wait_ge(*s.lhh(l * 2 - 1, KD))
    dve.wait_ge(*s.lx(l * 2 - 1, KD))
    dve.tensor_copy(b.par[:, 0:32], bank[2][:, 0:32]).then_inc(s.par2.up, 1)
    for g in range(8):
        dve.wait_ge(*s.par2_t(l, 2 + g // 4))
        dve.tensor_tensor(b.n_swT[:, g, :], bank[3 + g // 4][:, g % 4 * P:(g % 4 + 1) * P], b.tril[:, :], ALU.mult)\
           .then_inc(s.swt.up, 1)
    dve.wait_ge(*s.wi_ps(l, 1))
    dve.tensor_scalar(b.n_wi[:, :, :].rearrange("p t h -> p (t h)"), bank[5][:, 0:16], (4 * HD) ** -0.5, None,
                      ALU.mult).then_inc(s.wi.up, 1)

    def rope(r):
        dst = ([b.n_qi[:, 0, :], b.n_qi[:, 1, :], b.n_ki[:, 0, :], b.n_k[:, 0, :], b.n_k[:, 1, :]]
               + [b.n_q[:, m, :] for m in range(4)])[r]
        j, m = [(0, 0), (0, 1), (1, 1), (2, 0), (2, 1), (3, 0), (3, 1), (4, 0), (4, 1)][r]
        dve.wait_ge(*lay.bank_out(m, j))
        dve.tensor_tensor(dst, b.n_raw[:, r % 2, :], b.cosine[:, :], ALU.mult).then_inc(s.rope2.up, 1)
        dve.wait_ge(*s.rot2(l, r + 1))
        dve.tensor_tensor(b.sq[:, r % 2, :], bank[2 + r % 2][:, :], b.sine[:, :], ALU.mult).then_inc(s.rope2.up, 1)
        dve.wait_ge(*s.rope2(l, 3 * r + 2))
        dve.tensor_tensor(dst, dst, b.sq[:, r % 2, :], ALU.add).then_inc(s.rope2.up, 1)

    def index_scores(i):
        n = CAUSAL[i]
        score = b.n_score[:, i - 1, 0:n]
        for h in range(4):
            dve.wait_ge(*s.is_ps(l, 4 * (i - 1) + h + 1))
            dve.wait_ge(*s.wi(l, 1))
            if h >= 2:
                dve.wait_ge(*s.is_sum(l, 7 * (i - 1) + 2 * (h - 1) + 1))
            dst = score if h == 0 else b.n_relu[:, h % 2, 0:n]
            dve.tensor_scalar(dst, bank[4 + h][:, 0:n], 0.0, b.n_wi[:, i, h:h + 1], ALU.max, ALU.mult)\
               .then_inc(s.is_sum.up, 1)
            if h:
                dve.wait_ge(*s.is_sum(l, 7 * (i - 1) + 2 * h))
                dve.tensor_tensor(score, score, dst, ALU.add).then_inc(s.is_sum.up, 1)

    def top(i):
        n, at = CAUSAL[i], 16 * (i - 1)
        score, work, eight = b.n_score[:, i - 1, 0:n], b.n_work[:, i - 1, 0:n], b.n_top[:, i - 1, :]
        dve.wait_ge(*s.is_sum(l, 7 * i))
        dve.memset(b.n_score[0:HD, i - 1, n - HD:n], FLOOR).then_inc(s.floor.up, 1)
        lone_wait(dve, s, *s.floor(l, i))
        for n8 in range(TOPK // 8):
            src = score if n8 == 0 else work
            if n8:
                lone_wait(dve, s, *s.cut(l, at + n8))
            dve.max(eight, src).then_inc(s.top.up, 1)
            lone_wait(dve, s, *s.top(l, at + n8 + 1))
            dve.match_replace(work, eight, src, TAKEN).then_inc(s.cut.up, 1)
        dve.wait_ge(*s.cut(l, at + TOPK // 8))
        dve.tensor_tensor(work, work, score, ALU.is_equal).then_inc(s.mask.up, 1)
        dve.wait_ge(*s.mask(l, 2 * i - 1))
        dve.tensor_scalar(b.n_mask[:, i - 1, 0:n], work, NEG, None, ALU.mult).then_inc(s.mask.up, 1)

    rope(0)
    rope(1)
    rope(2)
    rope(3)
    rope(4)
    index_scores(1)
    rope(5)
    top(1)
    rope(6)
    index_scores(2)
    rope(7)
    rope(8)
    top(2)
    index_scores(3)
    top(3)
    for t in range(NB):
        dve.wait_ge(*lay.bank_out(t // 2, 8))
        dve.bn_stats(b.n_bn[:, t, :], b.n_vs[:, t, :]).then_inc(s.bn.up, 1)
    for t in range(NB):
        lone_wait(dve, s, *s.bn(l, t + 1))
        dve.bn_aggr(b.n_st[:, t, 0:2], b.n_bn[:, t, :]).then_inc(s.bn.up, 1)
    dve.wait_ge(*s.v_r(l, 1))
    for t in range(NB):
        dve.tensor_scalar(b.n_vs[:, t, :], b.n_vs[:, t, :], b.n_st[:, t, 0:1], b.n_st[:, t, 6:7],
                          ALU.subtract, ALU.mult).then_inc(s.v_n.up, 1)

    def gate(m):
        dve.wait_ge(*s.sg(l, m + 1))
        dve.tensor_tensor(b.mf[:, 4 + m, :], bank[m % 2][:, :], b.n_u[:, m, :], ALU.mult)\
           .then_inc(s.bank[m % 2].up, 1)

    for h in range(8):
        dve_max(dve, e, 2, l, h)
        dve_normalise(dve, e, 2, l, h, b.n_prob)
        if 3 <= h < 7:
            gate(h - 3)
    c = l * 2
    for k in range(KD):
        j = 9 + k // 2
        dve.wait_ge(*s.tile(lay.pair(j // 2), j % 2, k % 2))
        dve.scalar_tensor_tensor(b.x[:, k, :], b.x[:, k, :], ALPHA, bank[k % 2][:, :], ALU.mult, ALU.add)\
           .then_inc(s.bank[k % 2].up, 1)
        dve_add_up(dve, e, c, k, lambda k: lay.bank_out(k % 2, Q2_OUT + k // 2))
    dve_layer_norm(dve, e, c, 0)
    for k in range(KD):
        dve.wait_ge(*s.lhl(c, k + 1))
        dve.wait_ge(*lay.bank_out(k % 2, Q2_GATE + k // 2))
        sig = b.e_sig[:, k % 2, :]
        dve.tensor_tensor(sig, sig, b.e_ple[:, k, :], ALU.mult).then_inc(s.gx.up, 1)
        dve.wait_ge(*s.gx(l, 2 * k + 1))
        dve.scalar_tensor_tensor(b.x[:, k, :], b.x[:, k, :], ALPHA, sig, ALU.mult, ALU.add).then_inc(s.gx.up, 1)
    dve_ffn(dve, e, lay, 18, (Q2_FFN,))
    c = l * 2 + 1
    for k in range(KD):
        dve.wait_ge(*s.tile(lay.pair(20 + k), 1, 1))
        dve.tensor_tensor(b.x[:, k, :], bank[k % 2][:, :], b.x[:, k, :], ALU.add).then_inc(s.bank[k % 2].up, 1)
        dve_add_up(dve, e, c, k, lambda k: lay.bank_out(k % 2, Q2_W2 + k // 2))
    dve_layer_norm(dve, e, c, 16)


def dve_program(dve, e):
    s, b, bank = e.s, e.b, e.bank
    for x in (s.bank0, s.bank1, s.up0, s.up1, s.a_acc, s.lx):
        dve.sem_inc(x.up, x.credit)
    dve_setup(dve, e)
    with dve.Fori(0, DEPTH) as l:
        dve_layer1(dve, e, l)
    dve_rms(dve, e, 2 * DEPTH, b.fg, None, True)
    dve.wait_ge(s.trig_in.up, 32)
    dve_trig(dve, e, 1)
    with dve.Fori(0, DEPTH) as l:
        dve_layer2(dve, e, l)
    dve_output(dve, e)


def dve_output(dve, e):
    s, b, bank = e.s, e.b, e.bank
    for t in range(NB):
        for g in range(2):
            dve.wait_ge(s.y_t.up, 2 * t + g + 1)
            dve.tensor_copy(b.y_out[:, t, g * T:(g + 1) * T], bank[2 + 2 * (t % 2) + g][:, :]).then_inc(s.y.up, 1)



def three(pe, out, whi, wlo, xhi, xlo, start, stop):
    pe.matmul(out, wlo, xhi, start=start, stop=False)
    pe.matmul(out, whi, xlo, start=False, stop=False)
    return pe.matmul(out, whi, xhi, start=False, stop=stop)


def pe_unit(pe, e, lay, j, q, order=range(KD), ready=None, banks=None, tokens=False):
    pe_unit_at(pe, e, lay, j // 2, j % 2, q, order, ready, banks, tokens)


def pe_unit_at(pe, e, lay, j2, p, q, order=range(KD), ready=None, banks=None, tokens=False):
    s, b, bank, u = e.s, e.b, e.bank, lay.pair(j2)
    hi, lo = w8(b.w_hi[p]), w8(b.w_lo[p])
    pe.wait_ge(*s.lo_in(u, p))
    for m in range(2):
        if banks is None:
            pe.wait_ge(*lay.bank_free(m, q))
            out = bank[m]
        else:
            pe.wait_ge(*banks(m))
            out = bank[2 + m]
        if tokens:
            for t in (2 * m, 2 * m + 1):
                for n, k in enumerate(order):
                    v = slice(t * P, (t + 1) * P)
                    op = three(pe, out[:, t % 2 * G:(t % 2 + 1) * G], b.h_hi[:, k, v], b.h_lo[:, k, v],
                               hi[:, k, :], lo[:, k, :], n == 0, n == KD - 1)
        else:
            for n, k in enumerate(order):
                if m == 0 and ready is not None:
                    pe.wait_ge(*ready(n))
                op = three(pe, out[:, :], hi[:, k, m * P:(m + 1) * P], lo[:, k, m * P:(m + 1) * P],
                           b.h_hi[:, k, :], b.h_lo[:, k, :], n == 0, n == KD - 1)
        op.then_inc(s.half.up, 1)


def pe_rms(pe, e, c):
    s, b = e.s, e.b
    pe.wait_ge(*s.ssq(c, 7))
    pe.matmul(e.bank[7][:, :], b.ones[:, :], b.sq[:, 0, :], start=True, stop=True).then_inc(s.rms.up, 1)


def pe_turn_probs(pe, e, blk, l, h, prob, first=None):
    s, b, bank = e.s, e.b, e.bank
    t = attention(s, blk)
    if h:
        pe.wait_ge(*t.pt(l, 3 * h))
        pe.wait_ge(*t.po(l, h))
    for g, blocks in enumerate(BY_KEY):
        pe.wait_ge(*t.pn(l, 4 * h + 4))
        for j in blocks:
            c = 0 if j != 3 else 384
            for i in range(j, NB):
                at = c + (i - j) * P
                op = pe.transpose(bank[TP_BANK[g]][:, at:at + P], prob[:, P_AT[i] + j * P:P_AT[i] + (j + 1) * P],
                                  b.eye[:, :])
        op.then_inc(t.tp.up, 1)


def pe_values(pe, e, l, h, val, v0, probT, out, wait, done):
    pe.wait_ge(*wait)
    o = HD * (h % 2)
    for j in range(NB):
        op = pe.matmul(out[o:o + HD, j * P:T], val[:, j, v0:v0 + HD], probT[:, PT_AT[j]:PT_AT[j] + T - j * P],
                       start=(j == 0), stop=(j == NB - 1))
    op.then_inc(done.up, 1)


def pe_ffn(pe, e, lay, j0, c):
    s, b, bank = e.s, e.b, e.bank

    def body(i, first):
        ready = (lambda n: s.hl(c, n + 1)) if first and c is not None else None

        def banks(m):
            return s.upb[m](lay.ffn, i)
        q = Q_FFN if lay.blk == 1 else Q2_FFN
        pe_unit_at(pe, e, lay, i + j0 // 2, 0, i + q, ready=ready)
        pe_unit_at(pe, e, lay, i + j0 // 2, 1, None, banks=banks)

    body(0, True)
    with pe.Fori(1, 11) as i:
        body(i, False)
    q = Q_W2 if lay.blk == 1 else Q2_W2
    lone_wait(pe, s, s.fl.up, lay.ffn * 22 + 24)
    with pe.Fori(0, 4) as i:
        for m in range(2):
            for p in range(2):
                u = lay.pair(i * 2 + (j0 // 2 + 11 + m))
                pe.wait_ge(*s.lo_in(u, p))
                if p == 0:
                    pe.wait_ge(*lay.bank_free(m, i + q))
                for k in range(11):
                    op = three(pe, bank[m][:, :], w11(b.w_hi[p])[:, k, :], w11(b.w_lo[p])[:, k, :],
                               b.f_hi[:, 11 * p + k, :], b.f_lo[:, 11 * p + k, :], p == 0 and k == 0,
                               p == 1 and k == 10)
                op.then_inc(s.half.up, 2)


def pe_layer1(pe, e, l):
    s, b, bank = e.s, e.b, e.bank
    lay = Layer(s, 1, l)
    pe.wait_ge(*s.par_in(l, s.par_in.per))
    pe.transpose(bank[4][:, 0:74], b.rows[:, :], b.eye[0:74, 0:74]).then_inc(s.par_t.up, 1)
    pe.transpose(bank[5][:, 0:2 * TAPS], b.rows2[:, :], b.eye[0:2 * TAPS, 0:2 * TAPS]).then_inc(s.par_t.up, 1)
    with pe.Fori(0, 12) as i:
        for p in range(2):
            pe.wait_ge(s.a_acc.up, l * s.a_acc.per + i * 16 + (s.a_acc.credit + 8 * p + 8))
            for m in range(2):
                op = pe.matmul(bank[6][:, bass.ds(i * 4 + (2 * p + m), 1)], b.a_acc[p][:, m * P:(m + 1) * P],
                               b.ones[:, 0:1], start=True, stop=True)
            op.then_inc(s.a_pe.up, 1)
    c = l * 2
    pe_rms(pe, e, c)
    for k in range(KD):
        pe.wait_ge(*s.hf(c, k + 1))
        op = pe.matmul(bank[2][0:4, :], b.wff[:, k, :], b.hf[:, k, :], start=(k == 0), stop=(k == KD - 1))
    op.then_inc(s.ff.up, 1)

    def turn(n):
        m = n % 2
        pe.wait_ge(*lay.bank_out(m, 2 + n // 2))
        if n >= 2:
            pe.wait_ge(*s.rope(l, 3 * (n - 2) + 2))
        elif m == 0:
            pe.wait_ge(*s.ls_d(l, 1))
        pe.matmul(bank[2 + m][:, :], b.turn[:, :], b.rraw[:, m, :], start=True, stop=True).then_inc(s.rot.up, 1)

    def retain_scores(h):
        o, m = HD * (h % 2), h // 2
        if h:
            pe.wait_ge(*s.rs(l, 4 * h))
        pe.wait_ge(*s.rope(l, 12))
        for g, blocks in enumerate(BY_KEY):
            for j in blocks:
                c0, n = (0 if j != 3 else 384), T - P * j
                op = pe.matmul(bank[TP_BANK[g]][:, c0:c0 + n], b.rk[o:o + HD, m, j * P:(j + 1) * P],
                               b.rq[o:o + HD, m, j * P:T], start=True, stop=True)
            op.then_inc(s.rs_ps.up, 1)

    def retain_values(h):
        if h:
            pe.wait_ge(*s.rv_o(l, h))
        pe.wait_ge(*lay.bank_out(0, 4))
        pe.wait_ge(*lay.bank_out(1, 4))
        if h == 3:
            pe.wait_ge(*s.ex(l, 4))
        pe_values(pe, e, l, h, b.rv, HD * h, b.rs, bank[2], s.rs(l, 4 * h + 4), s.rv_ps)

    def scores(h):
        o, m = HD * (h % 2), h // 2
        if h:
            pe.wait_ge(*s.ex(l, 4 * h))
        else:
            pe.wait_ge(*lay.bank_out(0, 6))
            pe.wait_ge(*lay.bank_out(1, 6))
            pe.wait_ge(*s.ls_d(l, 4))
        if h < 2:
            pe.wait_ge(*s.rv_o(l, 3 + h))
        for g, blocks in enumerate(BY_QUERY):
            for i in blocks:
                n = CAUSAL[i]
                c0 = 0 if len(blocks) == 1 else (0 if i == 0 else P)
                sc = bank[SC_BANK[g]][:, c0:c0 + n]
                pe.matmul(sc, b.pick_r[:, h, :], b.cum[:, 0:n], start=True, stop=False)
                pe.matmul(sc, b.fq[o:o + HD, m, i * P:(i + 1) * P], b.fk[o:o + HD, m, 0:n], start=False, stop=False)
                op = pe.matmul(bank[SC_BANK[g]][:, c0 + n - P:c0 + n], b.eye_r[:, :], b.causal_r[:, :],
                               start=False, stop=True)
            op.then_inc(s.sc.up, 1)

    def values(h):
        if h == 0:
            pe.wait_ge(*lay.bank_out(0, 7))
            pe.wait_ge(*lay.bank_out(1, 7))
        pe_values(pe, e, l, h, b.fv, HD * h, b.probT, bank[5], s.pt(l, 3 * h + 3), s.pv)

    for j in range(10):
        pe_unit(pe, e, lay, j, j, ready=(lambda n: s.hl(c, n + 1)) if j == 0 else None, tokens=j in (4, 7))
        if j == 3:
            turn(0)
            turn(1)
        if j == 4:
            turn(2)
            turn(3)
        if 6 <= j:
            retain_values(j - 6)
        if 5 <= j <= 8:
            retain_scores(j - 5)
        if j == 8:
            scores(0)
    pe_turn_probs(pe, e, 1, l, 0, b.prob)
    scores(1)
    for m in range(2):
        pe.wait_ge(*lay.bank_free(m, Q_GN1))
        pe.wait_ge(*s.rv_o(l, 2 * m + 2))
        pe.matmul(bank[m][:, :], b.heads[:, :], b.mf[:, 4 + m, :], start=True, stop=True).then_inc(s.gn_ps.up, 1)
    values(0)
    pe_turn_probs(pe, e, 1, l, 1, b.prob)
    scores(2)
    for m in range(2):
        pe.wait_ge(*lay.bank_free(m, Q_GN2))
        pe.wait_ge(*s.gn_sq(l, m + 1))
        pe.matmul(bank[m][:, :], b.heads[:, :], b.ln_s[:, m, :], start=True, stop=True).then_inc(s.gn_ps.up, 1)
    values(1)
    pe.wait_ge(*s.pl_d(l, 4))
    for m in range(2):
        lone_wait(pe, s, *lay.bank_free(m, Q_POOL))
        for h in range(2):
            o = HD * h
            op = pe.matmul(bank[m][o:o + HD, :], b.pw[o:o + HD, m, :], b.wb[o:o + HD, m, 0:T], start=True, stop=True)
        op.then_inc(s.pl_ps.up, 1)
    pe_turn_probs(pe, e, 1, l, 2, b.prob)
    scores(3)
    values(2)
    pe.wait_ge(*lay.bank_free(0, Q_CONV))
    pe.wait_ge(*s.conv(l, 2 * TAPS))
    for m in range(2):
        op = pe.matmul(bank[0][:, :], b.ones[:, :], b.cv[:, m, :], start=(m == 0), stop=(m == 1))
    op.then_inc(s.cn_ps.up, 1)
    pe_turn_probs(pe, e, 1, l, 3, b.prob)
    pe.wait_ge(*lay.bank_free(1, Q_CONV))
    for m in range(2):
        pe.wait_ge(*s.cn_sq(l, m + 1))
        op = pe.matmul(bank[1][:, :], b.ones[:, :], b.ln_s[:, m, :], start=(m == 0), stop=(m == 1))
    op.then_inc(s.cn_ps.up, 1)
    values(3)
    for j in range(4):
        pe_unit(pe, e, lay, 10 + j, Q_OUT + j, order=MIX_ORDER, ready=(lambda n: s.ml(l, n + 1)) if j == 0 else None)
    pe_rms(pe, e, c + 1)
    pe_ffn(pe, e, lay, 14, c + 1)


def pe_layer_norm(pe, e, c):
    s, b, bank = e.s, e.b, e.bank
    pe.wait_ge(*s.lsum(c, 7))
    pe.matmul(bank[6][:, :], b.ones[:, :], b.r[:, :], start=True, stop=True).then_inc(s.lmean.up, 1)
    for k in range(KD):
        pe.wait_ge(*s.lsq(c, k + 1))
        op = pe.matmul(bank[7][:, :], b.ones[:, :], b.sq[:, k, :], start=(k == 0), stop=(k == KD - 1))
    op.then_inc(s.lvar.up, 1)


def pe_layer2(pe, e, l):
    s, b, bank = e.s, e.b, e.bank
    lay = Layer(s, 2, l)
    lone_wait(pe, s, *s.in2(l, s.in2.per))
    pe.transpose(bank[2][:, 0:32], b.n_rows[:, :], b.eye[0:32, 0:32]).then_inc(s.par2_t.up, 1)
    for g in range(8):
        op = pe.transpose(bank[3 + g // 4][:, g % 4 * P:(g % 4 + 1) * P], b.n_sw[:, g, :], b.eye[:, :])
        if g % 4 == 3:
            op.then_inc(s.par2_t.up, 1)
    pe.wait_ge(*s.lx(l * 2 - 1, KD))
    for t in range(NB):
        for k in range(KD):
            op = pe.matmul(bank[5][:, 4 * t:4 * t + 4], b.x[:, k, t * P:(t + 1) * P], b.n_wiw[:, k, :],
                           start=(k == 0), stop=(k == KD - 1))
    op.then_inc(s.wi_ps.up, 1)

    def turn(r):
        j, m = [(0, 0), (0, 1), (1, 1), (2, 0), (2, 1), (3, 0), (3, 1), (4, 0), (4, 1)][r]
        pe.wait_ge(*lay.bank_out(m, j))
        if r >= 2:
            pe.wait_ge(*s.rope2(l, 3 * (r - 2) + 2))
        else:
            pe.wait_ge(*s.swt(l, 8))
            pe.wait_ge(*s.par2(l, 1))
        pe.matmul(bank[2 + r % 2][:, :], b.turn[:, :], b.n_raw[:, r % 2, :], start=True, stop=True)\
          .then_inc(s.rot2.up, 1)

    def index_logits(i):
        pe.wait_ge(*s.rope2(l, 9))
        pe.wait_ge(*s.wi(l, 1))
        for h in range(4):
            if i > 1:
                pe.wait_ge(*s.is_sum(l, 7 * (i - 2) + max(1, 2 * h)))
            o = HD * (h % 2)
            pe.matmul(bank[4 + h][:, 0:CAUSAL[i]], b.n_qi[o:o + HD, h // 2, i * P:(i + 1) * P],
                      b.n_ki[o:o + HD, 0, 0:CAUSAL[i]], start=True, stop=True).then_inc(s.is_ps.up, 1)

    def scores(h):
        o = HD * (h % 2)
        if h:
            pe.wait_ge(*s.ex2(l, 4 * h))
        else:
            pe.wait_ge(*s.rope2(l, 27))
            pe.wait_ge(*s.is_sum(l, 21))
        for g, blocks in enumerate(BY_QUERY):
            for i in blocks:
                n = CAUSAL[i]
                c0 = 0 if len(blocks) == 1 else (0 if i == 0 else P)
                sc = bank[SC_BANK[g]][:, c0:c0 + n]
                if i and h == 0:
                    pe.wait_ge(*s.mask(l, 2 * i))
                pe.matmul(sc, b.eye_r[:, :], b.n_mask[:, i - 1, 0:n] if i else b.chunked_r[:, :], start=True, stop=False)
                op = pe.matmul(sc, b.n_q[o:o + HD, h // 2, i * P:(i + 1) * P], b.n_k[o:o + HD, h // 4, 0:n],
                               start=False, stop=True)
            op.then_inc(s.sc2.up, 1)

    def values(h):
        if h == 0:
            pe.wait_ge(*lay.bank_out(0, 1))
        pe_values(pe, e, l, h, b.n_v, HD * (h // 4), b.n_probT, bank[5], s.pt2(l, 3 * h + 3), s.pv2)

    def gating(m):
        pe.wait_ge(*lay.bank_free(m % 2, Q2_SGU + m // 2))
        pe.wait_ge(*s.v_g(l, 8))
        for c in range(NB):
            v = slice(c * P, (c + 1) * P)
            pe.matmul(bank[m % 2][:, v], b.pairs[:, m, :], b.n_sb[:, :], start=True, stop=False)
            for g in range(2):
                o = HD * g
                f = m * P + o
                op = pe.matmul(bank[m % 2][o:o + HD, v], b.n_vs[:, c, f:f + HD], b.n_swT[:, 2 * m + g, :],
                               start=False, stop=True)
        op.then_inc(s.sg.up, 1)

    ready = [s.lhl(l * 2 - 1, n + 1) for n in range(KD)]
    for j in range(9):
        if j == 1:
            pe_values_and_key(pe, e, lay)
        else:
            pe_unit(pe, e, lay, j, j, ready=(lambda n: ready[n]) if j == 0 else None, tokens=j in (7, 8))
        if j == 1:
            turn(0)
            turn(1)
        if j == 2:
            turn(2)
        if j == 3:
            turn(3)
            turn(4)
            index_logits(1)
        if j == 4:
            turn(5)
            turn(6)
            index_logits(2)
        if j == 5:
            turn(7)
            turn(8)
        if j == 6:
            index_logits(3)
    scores(0)
    for h in range(8):
        pe_turn_probs(pe, e, 2, l, h, b.n_prob)
        if h < 7:
            scores(h + 1)
        if 2 <= h < 6:
            gating(h - 2)
        values(h)
    for j in range(4):
        pe_unit(pe, e, lay, 9 + j, Q2_OUT + j, order=MIX2_ORDER,
                ready=(lambda n: s.ml2(l, n + 1)) if j == 0 else None)
    pe.wait_ge(*s.p_in(l, 16))
    for m in range(2):
        for t in range(NB):
            op = pe.transpose(bank[2 + m][:, t * P:(t + 1) * P], b.e_p[:, t, m * P:(m + 1) * P], b.eye[:, :])
        op.then_inc(s.p_t.up, 1)
    pe_layer_norm(pe, e, l * 2)
    u = lay.pair(6)
    hi, lo = (x[1][:, :].rearrange("p (k c) -> p k c", k=2) for x in (b.w_hi, b.w_lo))
    pe.wait_ge(*s.lo_in(u, 1))
    pe.wait_ge(*s.p_l(l, 2))
    for m in range(KD):
        pe.wait_ge(*lay.bank_free(m % 2, Q2_PLE + m // 2))
        for k in range(2):
            v = slice(m * P, (m + 1) * P)
            op = three(pe, bank[m % 2][:, :], hi[:, k, v], lo[:, k, v], b.e_hi[:, k, :], b.e_lo[:, k, :],
                       k == 0, k == 1)
        if m < KD - 1:
            op.then_inc(s.ple.up, 1)
        else:
            op.then_inc(s.half.up, 2)
    for j in range(4):
        pe_unit(pe, e, lay, 14 + j, Q2_GATE + j, ready=(lambda n: s.lhl(l * 2, n + 1)) if j == 0 else None)
    pe_ffn(pe, e, lay, 18, None)
    pe_layer_norm(pe, e, l * 2 + 1)


def pe_values_and_key(pe, e, lay):
    s, b, bank, u = e.s, e.b, e.bank, lay.pair(0)
    hi, lo = w8(b.w_hi[1]), w8(b.w_lo[1])
    pe.wait_ge(*s.lo_in(u, 1))
    pe.wait_ge(*lay.bank_free(0, 1))
    for t in range(NB):
        v = slice(t * P, (t + 1) * P)
        for k in range(KD):
            op = three(pe, bank[0][:, v], b.h_hi[:, k, v], b.h_lo[:, k, v], hi[:, k, 0:P], lo[:, k, 0:P],
                       k == 0, k == KD - 1)
    op.then_inc(s.half.up, 1)
    pe.wait_ge(*lay.bank_free(1, 1))
    for k in range(KD):
        op = three(pe, bank[1][:, :], hi[:, k, P:G], lo[:, k, P:G], b.h_hi[:, k, :], b.h_lo[:, k, :],
                   k == 0, k == KD - 1)
    op.then_inc(s.half.up, 1)


def pe_program(pe, e):
    s, b, bank = e.s, e.b, e.bank
    pe.sem_inc(s.half.up, s.half.credit)
    pe.sem_inc(s.a_pe.up, s.a_pe.credit)
    pe.wait_ge(s.z_in.up, 64)
    pe.wait_ge(s.z_copied.up, Z_COPIES)
    pe.wait_ge(s.z_ready.up, 5)
    for k in range(KD):
        if k >= 4:
            pe.wait_ge(s.z_x.up, k - 3)
        for t in range(NB):
            op = pe.transpose(bank[2 + k % 4][:, t * P:(t + 1) * P], b.z_x[:, t, k * P:(k + 1) * P], b.eye[:, :])
        op.then_inc(s.z_xt.up, 1)
    pe.wait_ge(s.z_act.up, 1)
    pe.transpose(bank[6][:, 0:KD], b.z_cs[:, :], b.eye[0:KD, 0:KD]).then_inc(s.z_xt.up, 1)
    pe.transpose(bank[7][:, 0:KD], b.z_fg[:, :], b.eye[0:KD, 0:KD]).then_inc(s.z_xt.up, 1)
    pe.wait_ge(s.z_x.up, KD + 2)
    with pe.Fori(0, DEPTH) as l:
        pe_layer1(pe, e, l)
    pe_rms(pe, e, 2 * DEPTH)
    pe.wait_ge(*s.hl(2 * DEPTH, KD))
    with pe.Fori(0, DEPTH) as l:
        pe_layer2(pe, e, l)
    pe_output(pe, e)


def pe_output(pe, e):
    s, b, bank = e.s, e.b, e.bank
    for t in range(NB):
        for g in range(2):
            if t >= 2:
                pe.wait_ge(s.y.up, 2 * (t - 2) + g + 1)
            for n in range(4):
                k = 4 * g + n
                pe.wait_ge(*s.lx(2 * DEPTH - 1, k + 1))
                op = pe.transpose(bank[2 + 2 * (t % 2) + g][:, n * P:(n + 1) * P], b.x[:, k, t * P:(t + 1) * P],
                                  b.eye[:, :])
            op.then_inc(s.y_t.up, 1)


_OUT = (1, T, D)


def kernel(**inputs):
    import numpy as _np
    import concourse.bacc as _bacc
    from concourse import mybir as _mybir
    from concourse.bass_utils import run_bass_kernel_spmd as _run

    nc = _bacc.Bacc("TRN2", target_bir_lowering=False, num_devices=1)
    table, table_at, decay = consts()
    arrays = {name: _np.ascontiguousarray(x) for name, x in inputs.items()}
    arrays["table"], arrays["decay"] = table, decay
    dram = {name: nc.dram_tensor(f"in_{name}", x.shape, _mybir.dt.from_np(x.dtype), kind="ExternalInput").ap()
            for name, x in arrays.items()}
    out = nc.dram_tensor("out_0", _OUT, _mybir.dt.from_np(_np.dtype("float32")), kind="ExternalOutput").ap()
    build(nc, dram, table_at, out)
    r = _run(nc, [{f"in_{name}": x for name, x in arrays.items()}], core_ids=[0])
    return r.results[0]["out_0"]
```

```python
from contextlib import ExitStack

import numpy as np
import concourse.bass as bass
from concourse import mybir

F32 = mybir.dt.float32
F32R = mybir.dt.float32r
I32 = mybir.dt.int32
ALU = mybir.AluOpType
ACT = mybir.ActivationFunctionType
AX = mybir.AxisListType.X

P = 128
T = 512
D = 1024
KD = D // P
NB = T // P
G = 256
HD = 64
FF = 2816
KF = FF // P
DEPTH = 2
TAPS = 31
MODS = 6 * KD
NEG = -1e30
FLOOR = -3e38
TAKEN = -3.4e38
TOPK = T // 4
EPS, LN_EPS = 1e-6, 1e-5
ALPHA = (2 * DEPTH) ** 0.25
IN1 = dict(fq=0, fk=256, fv=512, ff=768, pu=772, rq=1028, rk=1284, rv=1540, rg=1796, ca=2052, cg=2308)
IN2 = dict(q=0, k=512, v=640, qi=768, ki=1024, wi=1088, u=1092, vs=1604)
MOD_BANK = [6, 3, 6]
A_CHUNKS, B_CHUNKS = 16, 8
CAUSAL = [P * (i + 1) for i in range(NB)]
P_AT = [P * i * (i + 1) // 2 for i in range(NB)]
PT_AT = [0, 512, 896, 1152]
TRI = sum(CAUSAL)
BY_QUERY = [(0, 2), (1,), (3,)]
BY_KEY = [(1, 3), (2,), (0,)]

UNITS = {1: 10 + 4 + 22 + 16, 2: 9 + 4 + 5 + 22 + 16}
UNIT0 = {1: 0, 2: DEPTH * UNITS[1]}


def consts():
    eye = np.eye(P)
    k = np.arange(P)[:, None]
    q = np.arange(P)[None, :]
    parts = {}
    parts["eye"] = eye
    parts["causal"] = np.where(k >= q, 0.0, NEG)
    parts["chunked"] = np.where((k < 64) & (q >= 64), NEG, 0.0)
    parts["tril"] = (k <= q) * 1.0
    parts["heads"] = (k // HD == q // HD) / float(HD)
    for name, half, width in (("turn1", HD // 2, HD), ("turn2", HD // 8, HD // 4)):
        m = np.zeros((P, P))
        for p in range(P):
            r = p % HD
            if r < half:
                m[p + half, p] = -1.0
            elif r < width:
                m[p - half, p] = 1.0
        parts[name] = m
    sel = np.zeros((P, 4, P))
    for h in range(4):
        sel[h, h] = sel[32 + h, h] = -8.0
    parts["pick"] = sel.reshape(P, -1)
    sel = np.zeros((P, 4, P))
    for m in range(4):
        for p in range(P):
            sel[2 * m + p // HD, m, p] = 1.0
    parts["pairs"] = sel.reshape(P, -1)
    p = np.arange(P)
    parts["freq1"] = (10000.0 ** (-(p % 32) / 32.0))[:, None]
    parts["freq2"] = np.where(p % HD < 16, 500000.0 ** (-2.0 * (p % 8) / 16.0), 0.0)[:, None]
    w = np.stack([np.where(p < 64, 2, 4), np.where(p < 64, 8, 16)], 1)
    parts["window"] = 1.0 / w
    parts["counts"] = (1.0 / np.minimum(np.arange(1, 17)[None, None, :], w[:, :, None])).reshape(P, -1)
    at, cols = {}, 0
    for name, a in parts.items():
        at[name] = (cols, a.shape[1])
        cols += a.shape[1]
    table = np.concatenate(list(parts.values()), 1).astype(np.float32)
    t = np.arange(T)[None, :] - np.arange(P)[:, None]
    decay = [np.where(t >= 0, HD ** -0.5 * np.exp(np.log(1.0 - 2.0 ** (-5.0 - h)) * np.maximum(t, 0)), 0.0)
             for h in range(4)]
    return table, at, np.stack(decay, 1).astype(np.float32)


class Named:
    pass


def build(nc, a, table_at, out):
    with ExitStack() as ctx:
        top = [nc.sbuf_base + 31 & ~31]

        def place(name, shape, dt, at=None):
            size = 4
            for x in shape[1:]:
                size *= x
            off = top[0] if at is None else at
            t = nc.alloc_sbuf_tensor_at(name, shape, dt, offset=off)
            if at is None:
                top[0] = off + (size + 31 & ~31)
            return t

        b = Named()
        b.x = place("x", [P, KD, T], F32)
        h_at = top[0]
        b.h_hi = place("h_hi", [P, KD, T], F32R)
        b.h_lo = place("h_lo", [P, KD, T], F32R)
        b.a_raw = [place(f"a_raw{i}", [P, KD // 2, G], F32, at=h_at + 2 * KD * G * i) for i in range(4)]
        b.a_acc = place("a_acc", [P, A_CHUNKS * G], F32, at=h_at + 4 * KD * T)
        b.raw = [place(f"raw{i}", [P, 2048], F32) for i in range(2)]
        b.w_hi = [place(f"w_hi{i}", [P, 2048], F32R) for i in range(2)]
        b.w_lo = [place(f"w_lo{i}", [P, 2048], F32R) for i in range(2)]
        ncst = sum(n for nm, (_, n) in table_at.items())
        b.eye = place("eye", [P, P], F32)
        b.ones = place("ones", [P, P], F32)
        b.turn = place("turn", [P, P], F32)
        b.heads = place("heads", [P, P], F32)
        b.tril = place("tril", [P, P], F32)
        b.eye_r = place("eye_r", [P, P], F32R)
        b.causal_r = place("causal_r", [P, P], F32R)
        b.chunked_r = place("chunked_r", [P, P], F32R)
        b.pick_r = place("pick_r", [P, 4, P], F32R)
        b.freq = place("freq", [P, 2], F32)
        b.window = place("window", [P, 2], F32)
        b.counts = place("counts", [P, 2, 16], F32)
        b.eps = place("eps", [P, 4], F32)
        b.wff = place("wff", [P, KD, 4], F32)
        b.cosine = place("cosine", [P, T], F32)
        b.sine = place("sine", [P, T], F32)
        b.r = place("r", [P, T], F32)
        b.mod = place("mod", [P, MODS], F32)
        b.gain = place("gain", [P, 2 * KD], F32)
        b.par = place("par", [P, 74], F32)
        b.taps = place("taps", [P, 2 * TAPS], F32)
        b.c = place("c", [P, KD], F32)
        b.fb = place("fb", [4, 1], F32)
        b.fg = place("fg", [P, KD], F32)
        b.small = place("small", [P, 24], F32)
        b.base = top[0]
        mid = b.base

        class Region:
            def __init__(self, tag, at):
                self.tag, self.at = tag, at

            def __call__(self, name, shape, dt=F32):
                size = 4
                for x in shape[1:]:
                    size *= x
                t = place(self.tag + name, shape, dt, at=self.at)
                self.at += size + 31 & ~31
                assert self.at <= nc.sbuf_usable_end, (self.tag, name, self.at - nc.sbuf_usable_end)
                return t

        z = Region("z_", mid)
        b.z_tab = z("tab", [P, ncst])
        b.z_x = z("x", [P, NB, D])
        b.z_c = z("c", [KD, P])
        b.z_cs = z("cs", [KD, P])
        b.z_fg = z("fg", [KD, P])
        z2 = Region("trig_", mid + 61440)
        b.t_pi = z2("pi", [P, T], I32)
        b.t_pf = z2("pf", [P, T])
        b.t_ang = z2("ang", [P, T])
        b.t_n = z2("n", [P, T])
        b.t_ni = z2("ni", [P, T], I32)
        b.t_a = z2("a", [P, T])
        b.t_b = z2("b", [P, T])
        f = Region("f_", mid)
        b.f_hi = f("hi", [P, KF, T], F32R)
        b.f_lo = f("lo", [P, KF, T], F32R)
        b.f_act = f("act", [P, 2, T])
        b.f_full = f("full", [P, 2, T])
        m = Region("m_", mid)
        b.sq = m("sq", [P, KD, T])
        b.mf = place("mf", [P, KD, T], F32, at=mid)
        full_at = m.at
        b.hf = m("hf", [P, KD, T])
        mm = Region("mm_", full_at)
        b.rq = mm("rq", [P, 2, T])
        b.rk = mm("rk", [P, 2, T])
        b.rv = mm("rv", [P, NB, G])
        b.rg = mm("rg", [P, 2, T])
        b.rraw = place("m_rraw", [P, 2, T], F32, at=m.at)
        b.wb = m("wb", [P, 2, T + 16])
        b.cgate = m("cgate", [P, 2, T + 16])
        b.ch = m("ch", [P, 2, T + TAPS - 1])
        b.cv = m("cv", [P, 2, T])
        fq_at = m.at
        b.fq = m("fq", [P, 2, T])
        b.fk = m("fk", [P, 2, T])
        b.fv = m("fv", [P, NB, G])
        b.pu = m("pu", [P, 2, T + 16])
        pool_at = m.at
        b.ln_d = m("ln_d", [P, 2, T])
        b.ln_s = m("ln_s", [P, 2, T])
        b.pw = m("pw", [P, 2, HD])
        b.ls = place("m_ls", [4, 4, T], F32, at=m.at)
        b.prob = m("prob", [P, TRI])
        b.probT = m("probT", [P, TRI])
        b.rs = m("rs", [P, TRI])
        b.decay = m("decay", [P, 4, T])
        b.cum = m("cum", [P, T], F32R)
        b.rows = place("rows", [74, P], F32, at=(nc.sbuf_usable_end & ~31) - 8 * P)
        b.rows2 = place("rows2", [2 * TAPS, P], F32, at=(nc.sbuf_usable_end & ~31) - 4 * P)
        b.b_raw = [place(f"b_raw{i}", [P, KD, G], F32, at=full_at + 4 * KD * G * i) for i in range(2)]
        b.b_acc = place("b_acc", [P, B_CHUNKS * G], F32, at=fq_at)
        n = Region("n_", mid)
        b.n_sq = n("sq", [P, KD, T])
        b.n_rows = n("rows", [32, P])
        b.n_q = n("q", [P, 4, T])
        b.n_k = n("k", [P, 2, T])
        b.n_ki = n("ki", [P, 1, T])
        b.n_qi = n("qi", [P, 2, T])
        b.n_v = n("v", [P, NB, P])
        b.n_wi = n("wi", [P, NB, 4])
        b.n_wiw = n("wiw", [P, KD, 4])
        b.n_score = n("score", [P, 3, T])
        b.n_work = n("work", [P, 3, T])
        b.n_relu = n("relu", [P, 2, T])
        b.n_top = n("top", [P, 3, 8])
        b.n_mask = n("mask", [P, 3, T], F32R)
        b.n_u = n("u", [P, 4, T])
        b.n_vs = n("vs", [P, NB, T])
        b.n_g = n("g", [P, T])
        b.n_b = n("b", [P, T])
        b.n_swT = n("swT", [P, 8, P])
        b.n_sb = n("sb", [8, P])
        b.pairs = n("pairs", [8, 4, P])
        b.n_st = n("st", [P, NB, 8])
        b.n_bn = n("bn", [P, NB, 6])
        b.n_raw = place("n_raw", [P, 3, T], F32, at=n.at + 4096)
        b.n_sw = place("n_sw", [P, 8, P], F32, at=n.at)
        b.n_prob = n("prob", [P, TRI])
        b.n_probT = n("probT", [P, TRI])
        e = Region("e_", mid)
        b.e_sq = e("sq", [P, KD, T])
        b.e_p = e("p", [P, NB, G])
        b.e_pf = e("pf", [P, 2, T])
        b.e_hi = e("hi", [P, 2, T], F32R)
        b.e_lo = e("lo", [P, 2, T], F32R)
        b.e_ple = e("ple", [P, KD, T])
        b.e_sig = e("sig", [P, 2, T])
        b.y_out = place("y_out", [P, NB, D], F32, at=mid + 4 * KD * T)

        bank = [ctx.enter_context(nc.psum_tensor(f"bank{i}", [P, T], F32)) for i in range(8)]
        s = Sems(nc, ctx)
        block = ctx.enter_context(nc.Block())
        e = Named()
        e.nc, e.a, e.b, e.s, e.bank, e.at, e.out = nc, a, b, s, bank, table_at, out

        @block.sync
        def _(eng):
            sp_program(eng, e)

        @block.scalar
        def _(eng):
            act_program(eng, e)

        @block.gpsimd
        def _(eng):
            pool_program(eng, e)

        @block.vector
        def _(eng):
            dve_program(eng, e)

        @block.tensor
        def _(eng):
            pe_program(eng, e)


class Signal:
    def __init__(self, up, per, credit=0):
        self.up, self.per, self.credit = up, per, credit

    def __call__(self, turn, k):
        return self.up, turn * self.per + (self.credit + k)


class Sems:
    def __init__(self, nc, ctx):
        def up(name, per, credit=0):
            return Signal(ctx.enter_context(nc.semaphore(name)), per, credit)

        self.z_in = up("z_in", 0)
        self.z_ready = up("z_ready", 0)
        self.z_copied = up("z_copied", 0)
        self.z_xt = up("z_xt", 0)
        self.z_x = up("z_x", 0)
        self.z_act = up("z_act", 0)
        self.trig_in = up("trig_in", 0)
        self.trig = up("trig", 0)
        self.trig_sin = up("trig_sin", 0)
        self.par_in = up("par_in", 16 * 11)
        self.decay_in = up("decay_in", 16 * 3)
        self.par_t = up("par_t", 2)
        self.par = up("par", 2)
        self.a_acc = up("a_acc", KD * A_CHUNKS, 2 * KD)
        self.a_pe = up("a_pe", 2)
        self.b_acc = up("b_acc", KD * B_CHUNKS)
        self.b_pe = up("b_pe", 1)
        self.mod = up("mod", 3)
        self.gain = up("gain", 2)
        self.a_in = [up(f"a_in{i}", 16 * A_CHUNKS // 2) for i in range(4)]
        self.b_in0 = up("b_in0", 16 * B_CHUNKS // 2)
        self.b_in1 = up("b_in1", 16 * B_CHUNKS // 2)
        self.sq = up("sq", 8)
        self.ssq = up("ssq", 7)
        self.rms = up("rms", 1)
        self.r_ln = up("r_ln", 1)
        self.r = up("r", 1)
        self.xr = up("xr", 8)
        self.hf = up("hf", 8)
        self.hh = up("hh", 8)
        self.hl = up("hl", 8)
        self.ff = up("ff", 1)
        self.ls_a = up("ls_a", 3)
        self.ls_d = up("ls_d", 4)
        self.ls_1 = up("ls_1", 2)
        self.ck = up("ck", 1)
        self.pads = up("pads", 2)
        self.conv = up("conv", 62)
        self.rot = up("rot", 4)
        self.rope = up("rope", 12)
        self.rs_ps = up("rs_ps", 12)
        self.rs = up("rs", 16)
        self.rv_ps = up("rv_ps", 4)
        self.rv_o = up("rv_o", 4)
        self.sc = up("sc", 12)
        self.mxr = up("mxr", 16)
        self.mx = up("mx", 12)
        self.ex = up("ex", 16)
        self.rcp = up("rcp", 4)
        self.pn = up("pn", 16)
        self.tp = up("tp", 12)
        self.pt = up("pt", 12)
        self.pv = up("pv", 4)
        self.po = up("po", 4)
        self.gn_ps = up("gn_ps", 4)
        self.gn_sq = up("gn_sq", 2)
        self.gn_ln = up("gn_ln", 2)
        self.gn_r = up("gn_r", 2)
        self.gn_x = up("gn_x", 2)
        self.gn_m = up("gn_m", 2)
        self.gn_o = up("gn_o", 2)
        self.pl_sum = up("pl_sum", 6)
        self.pl_up = up("pl_up", 2)
        self.pl_d = up("pl_d", 4)
        self.pl_ps = up("pl_ps", 2)
        self.cn_ps = up("cn_ps", 2)
        self.cn_sq = up("cn_sq", 2)
        self.cn_ln = up("cn_ln", 1)
        self.cn_r = up("cn_r", 1)
        self.cn_x = up("cn_x", 2)
        self.cn_xr = up("cn_xr", 2)
        self.cn_o = up("cn_o", 2)
        self.mh = up("mh", 8)
        self.ml = up("ml", 8)
        self.silu = up("silu", 22)
        self.fh = up("fh", 22)
        self.fl = up("fl", 22, 2)
        self.up0 = up("up0", 11, 1)
        self.up1 = up("up1", 11, 1)
        self.raw0 = up("raw0", 0)
        self.raw1 = up("raw1", 0)
        self.hi = up("hi", 0)
        self.lo = up("lo", 0, 2)
        self.half = up("half", 0, 4)
        self.bank0 = up("bank0", 0, 1)
        self.bank1 = up("bank1", 0, 1)
        self.in2 = up("in2", 224)
        self.par2 = up("par2", 1)
        self.par2_t = up("par2_t", 3)
        self.swt = up("swt", 8)
        self.wi_ps = up("wi_ps", 1)
        self.wi = up("wi", 1)
        self.rot2 = up("rot2", 9)
        self.rope2 = up("rope2", 27)
        self.is_ps = up("is_ps", 12)
        self.is_sum = up("is_sum", 21)
        self.floor = up("floor", 3)
        self.top = [up(f"top{i}", TOPK // 8) for i in range(1, NB)]
        self.cut = [up(f"cut{i}", TOPK // 8) for i in range(1, NB)]
        self.mask = up("mask", 6)
        self.sc2 = up("sc2", 24)
        self.mxr2 = up("mxr2", 32)
        self.mx2 = up("mx2", 24)
        self.ex2 = up("ex2", 32)
        self.rcp2 = up("rcp2", 8)
        self.pn2 = up("pn2", 32)
        self.tp2 = up("tp2", 24)
        self.pt2 = up("pt2", 24)
        self.pv2 = up("pv2", 8)
        self.po2 = up("po2", 8)
        self.bn = up("bn", 8)
        self.v_ln = up("v_ln", 1)
        self.v_r = up("v_r", 1)
        self.v_n = up("v_n", 4)
        self.v_g = up("v_g", 8)
        self.sg = up("sg", 4)
        self.mh2 = up("mh2", 8)
        self.ml2 = up("ml2", 8)
        self.lsum = up("lsum", 7)
        self.lmean = up("lmean", 1)
        self.ld = up("ld", 8)
        self.lsq = up("lsq", 8)
        self.lvar = up("lvar", 1)
        self.l_ln = up("l_ln", 1)
        self.l_r = up("l_r", 1)
        self.lxr = up("lxr", 8)
        self.lx = up("lx", 8, 8)
        self.lhh = up("lhh", 8, 8)
        self.lhl = up("lhl", 8, 8)
        self.p_in = up("p_in", 16)
        self.p_t = up("p_t", 2)
        self.p_f = up("p_f", 2)
        self.p_h = up("p_h", 2)
        self.p_l = up("p_l", 2)
        self.ple = up("ple", 7)
        self.gx = up("gx", 16)
        self.passed = up("passed", 0)
        self.y_t = up("y_t", 0)
        self.y = up("y", 0)
        self.y_out = up("y_out", 0)
        self.raw, self.bank, self.upb = (self.raw0, self.raw1), (self.bank0, self.bank1), (self.up0, self.up1)
        self.b_in = (self.b_in0, self.b_in1)

    def raw_in(self, n2, p):
        return self.raw[p].up, n2 * 64 + 64

    def raw_free(self, n2, p):
        return self.lo.up, n2 * 2 + (p + 1)

    def slot_free(self, n2, p):
        return self.half.up, n2 * 4 + (2 * p + 2)

    def hi_in(self, n2, p):
        return self.hi.up, n2 * 2 + (p + 1)

    def lo_in(self, n2, p):
        return self.lo.up, n2 * 2 + (p + 3)

    def tile(self, n2, p, m):
        return self.half.up, n2 * 4 + (2 * p + m + 5)


USES = {1: 10 + 4 + 4 + 11 + 4, 2: 9 + 2 + 4 + 4 + 4 + 11 + 4}
USE0 = {1: 0, 2: DEPTH * USES[1]}


def attention(s, blk):
    t = Named()
    if blk == 1:
        t.sc, t.mxr, t.mx, t.ex, t.rcp, t.pn, t.tp, t.pt, t.pv, t.po = (
            s.sc, s.mxr, s.mx, s.ex, s.rcp, s.pn, s.tp, s.pt, s.pv, s.po)
    else:
        t.sc, t.mxr, t.mx, t.ex, t.rcp, t.pn, t.tp, t.pt, t.pv, t.po = (
            s.sc2, s.mxr2, s.mx2, s.ex2, s.rcp2, s.pn2, s.tp2, s.pt2, s.pv2, s.po2)
    return t


class Layer:
    def __init__(self, s, blk, l):
        self.s, self.blk, self.l = s, blk, l
        self.pair0 = l * (UNITS[blk] // 2) + UNIT0[blk] // 2
        self.use0 = l * USES[blk] + USE0[blk]
        self.ffn = l + DEPTH * (blk - 1)

    def pair(self, j):
        return self.pair0 + j

    def bank_free(self, m, q):
        return self.s.bank[m].up, self.use0 + (q + 1)

    def bank_out(self, m, q):
        return self.s.bank[m].up, self.use0 + (q + 2)


Q_GN1, Q_GN2, Q_POOL, Q_CONV, Q_OUT, Q_FFN, Q_W2 = 10, 11, 12, 13, 14, 18, 29
Q2_SGU, Q2_OUT, Q2_PLE, Q2_GATE, Q2_FFN, Q2_W2 = 9, 11, 15, 19, 23, 34
MIX2_ORDER = [0, 1, 4, 5, 2, 6, 7, 3]
MIX_ORDER = [4, 5, 2, 3, 0, 1, 6, 7]
UNIT_COLS1 = ["cg", "ca", "rq", "rk", "rv", "fq", "fk", "fv", "pu", "rg"]


def lone_wait(eng, s, sem, value):
    eng.wait_ge(sem, value)
    eng.sem_inc(s.passed.up, 1)


def cols(buf, j):
    return buf[:, :, :].rearrange("p k t -> p (k t)")[:, bass.ts(j, T)]


def w8(buf):
    return buf[:, :].rearrange("p (k c) -> p k c", k=KD)


def w11(buf):
    return buf[:, 0:11 * P].rearrange("p (k c) -> p k c", k=11)



def sp_unit(sp, e, lay, j2, p, dst, src):
    s = e.s
    lone_wait(sp, s, *s.raw_free(lay.pair(j2), p))
    sp.dma_start(dst, src).then_inc(s.raw[p].up, 64)


def sp_weights(sp, e, lay, j, w, l, c0):
    sp_unit(sp, e, lay, j // 2, j % 2, w8(e.b.raw[j % 2]),
            w[l, :, c0:c0 + G].rearrange("(k p) c -> p k c", p=P))


def sp_modulation(sp, e, l, i, p):
    s = e.s
    for q in range(2):
        sp.wait_ge(s.a_acc.up, l * s.a_acc.per + i * 16 + (8 * p + 4 * q + 4))
        sp.dma_start(e.b.a_raw[2 * p + q][:, :, :],
                     e.a["ada_w"][l, :, :].rearrange("(q k p) c -> q p k c", p=P, q=2)[q, :, :, bass.ts(i * 2 + p, G)]
                     ).then_inc(s.a_in[2 * p + q].up, 16)


def sp_modulation_b(sp, e, l, n):
    s = e.s
    if n >= 2:
        sp.wait_ge(*s.b_acc(l, KD * (n - 1)))
    c = (A_CHUNKS + n) * G
    sp.dma_start(e.b.b_raw[n % 2][:, :, :], e.a["ada_w"][l, :, c:c + G].rearrange("(k p) c -> p k c", p=P))\
      .then_inc(s.b_in[n % 2].up, 16)


def sp_ffn(sp, e, lay, j0, w1, w3, c3, w2, l, more=False):
    s, b = e.s, e.b

    with sp.Fori(0, 11) as i:
        for p, (w, c0) in enumerate(((w1, 0), (w3, c3))):
            sp_unit(sp, e, lay, i + j0 // 2, p, w8(b.raw[p]),
                    w[l, :, c0:c0 + FF].rearrange("(k p) c -> p k c", p=P)[:, :, bass.ts(i, G)])
    with sp.Fori(0, 8) as i:
        for p in range(2):
            sp_unit(sp, e, lay, i + (j0 // 2 + 11), p, w11(b.raw[p]),
                    w2[l, :, :].rearrange("(h k p) c -> h p k c", p=P, h=2)[p, :, :, bass.ts(i, P)])
        if more:
            sp.wait_ge(*s.tile(lay.pair(j0 // 2 + 10), 1, 1))
            for p in range(2):
                sp_modulation(sp, e, l + 1, i, p)


def sp_parameters(sp, e, l):
    a, b, s = e.a, e.b, e.s
    r = 0
    for name, n in (("norm_mix_g", 8), ("norm_ffn_g", 8), ("ada_b", 48), ("pool_scale", 2), ("ret_gn_g", 2),
                    ("conv_b", 2), ("conv_ln_g", 2), ("conv_ln_b", 2)):
        sp.dma_start(b.rows[r:r + n, :], a[name][l, :].rearrange("(n p) -> n p", p=P)).then_inc(s.par_in.up, 16)
        r += n
    sp.dma_start(b.rows2[:, :], a["conv_w"][l, :, :].rearrange("t (m p) -> (t m) p", p=P)).then_inc(s.par_in.up, 16)
    sp.dma_start(b.fb[:, :], a["fox_fb"][l, :].rearrange("(h o) -> h o", o=1)).then_inc(s.par_in.up, 16)
    sp.dma_start(b.wff[:, :, :], a["w_in"][l, :, IN1["ff"]:IN1["ff"] + 4].rearrange("(k p) c -> p k c", p=P))\
      .then_inc(s.par_in.up, 16)


def sp_layer1(sp, e, l, more):
    a, b, s = e.a, e.b, e.s
    lay = Layer(s, 1, l)
    for j in range(2):
        sp_weights(sp, e, lay, j, a["w_in"], l, IN1[UNIT_COLS1[j]])
    sp.wait_ge(*lay.bank_free(0, 0))
    sp.wait_ge(*lay.bank_free(1, 0))
    sp.dma_start(b.decay[:, :, :], a["decay"]).then_inc(s.decay_in.up, 16)
    for m in range(2):
        sp.dma_start(b.pw[:, m, :], a["pool_w"][l, 2 * m:2 * m + 2, :, :].rearrange("e c d -> (e c) d"))\
          .then_inc(s.decay_in.up, 16)
    for j in range(2, 10):
        sp_weights(sp, e, lay, j, a["w_in"], l, IN1[UNIT_COLS1[j]])
    for j in range(4):
        if j == 2:
            sp.wait_ge(*s.gn_o(l, 2))
        if j >= 2:
            for n in (2 * j - 4, 2 * j - 3):
                sp_modulation_b(sp, e, l, n)
        sp_weights(sp, e, lay, 10 + j, a["w_out"], l, G * j)
    for n in range(4, B_CHUNKS):
        sp_modulation_b(sp, e, l, n)
    sp_ffn(sp, e, lay, 14, a["ffn_w1"], a["ffn_w3"], 0, a["ffn_w2"], l, more)
    if more:
        sp_parameters(sp, e, l + 1)


def sp_layer2(sp, e, l):
    a, b, s = e.a, e.b, e.s
    lay = Layer(s, 2, l)
    sp_weights(sp, e, lay, 0, a["w_in_2"], l, IN2["qi"])
    for m in range(2):
        sp.wait_ge(*lay.bank_free(m, 0))
    for n, name in enumerate(("ln1_g_2", "ln1_b_2", "ln2_g_2", "ln2_b_2")):
        sp.dma_start(b.n_rows[8 * n:8 * n + 8, :], a[name][l, :].rearrange("(n p) -> n p", p=P)).then_inc(s.in2.up, 16)
    sp.dma_start(b.n_wiw[:, :, :], a["w_in_2"][l, :, IN2["wi"]:IN2["wi"] + 4].rearrange("(k p) c -> p k c", p=P))\
      .then_inc(s.in2.up, 16)
    sp.dma_start(b.n_g[:, :], a["sgu_ln_g_2"][l, :].partition_broadcast(P)).then_inc(s.in2.up, 16)
    sp.dma_start(b.n_b[:, :], a["sgu_ln_b_2"][l, :].partition_broadcast(P)).then_inc(s.in2.up, 16)
    sp.dma_start(b.n_sw[:, :, :], a["sgu_w_2"][l, :, :, :].rearrange("g t s -> t g s")).then_inc(s.in2.up, 16)
    sp.dma_start(b.n_sb[:, :], a["sgu_b_2"][l, :, :]).then_inc(s.in2.up, 16)
    c, n = e.at["pairs"]
    sp.dma_start(b.pairs[:, :, :].rearrange("p a b -> p (a b)"), a["table"][0:8, c:c + n]).then_inc(s.in2.up, 16)
    c, n = e.at["turn2"]
    sp.dma_start(b.turn[:, :], a["table"][:, c:c + n]).then_inc(s.in2.up, 64)
    w = a["w_in_2"]

    def piece(c0, n):
        return w[l, :, c0:c0 + n].rearrange("(k p) c -> p k c", p=P)

    lone_wait(sp, s, *s.raw_free(lay.pair(0), 1))
    dst = w8(b.raw[1])
    sp.dma_start(dst[:, :, 0:P], piece(IN2["v"], P)).then_inc(s.raw[1].up, 32)
    for at in (P, P + HD):
        sp.dma_start(dst[:, :, at:at + HD], piece(IN2["ki"], HD)).then_inc(s.raw[1].up, 16)
    lone_wait(sp, s, *s.raw_free(lay.pair(1), 0))
    dst = w8(b.raw[0])
    for n in range(4):
        sp.dma_start(dst[:, :, n * HD:(n + 1) * HD], piece(IN2["k"] + HD * (n // 2), HD)).then_inc(s.raw[0].up, 16)
    for j, c0 in enumerate((IN2["q"], IN2["q"] + G, IN2["u"], IN2["u"] + G, IN2["vs"], IN2["vs"] + G)):
        sp_weights(sp, e, lay, 3 + j, w, l, c0)
    for j in range(4):
        sp_weights(sp, e, lay, 9 + j, a["w_o_2"], l, G * j)
    sp_unit(sp, e, lay, 6, 1, b.raw[1][:, :].rearrange("p (k c) -> p k c", k=2),
            a["w_ple_2"][l, :, :].rearrange("(k p) c -> p k c", p=P))
    sp_weights(sp, e, lay, 14, a["w_ple_gate_2"], l, 0)
    for m in range(2):
        lone_wait(sp, s, *lay.bank_free(m, Q2_PLE))
    sp.dma_start(b.e_p[:, :, :], a["p_2"][l, 0, :, :].rearrange("(t p) c -> p t c", p=P)).then_inc(s.p_in.up, 16)
    for j in range(1, 4):
        sp_weights(sp, e, lay, 14 + j, a["w_ple_gate_2"], l, G * j)
    sp_ffn(sp, e, lay, 18, a["w_ffn_in_2"], a["w_ffn_in_2"], FF, a["w_ffn_out_2"], l)


def sp_program(sp, e):
    a, b, s = e.a, e.b, e.s
    for dst, src in ((b.z_tab[:, :], a["table"]),
                     (b.z_x[:, :, :], a["x"][0, :, :].rearrange("(t p) d -> p t d", p=P)),
                     (b.z_c[:, :], a["c"][0, :].rearrange("(n p) -> n p", p=P)),
                     (b.z_fg[:, :], a["final_g"].rearrange("(n p) -> n p", p=P))):
        sp.dma_start(dst, src).then_inc(s.z_in.up, 16)
    sp_parameters(sp, e, 0)
    with sp.Fori(0, A_CHUNKS // 4) as i:
        for p in range(2):
            sp_modulation(sp, e, 0, i, p)
    sp.wait_ge(s.z_copied.up, Z_COPIES)
    sp.wait_ge(s.z_xt.up, KD + 2)
    sp.dma_start(b.t_pi[:, :], a["positions"].partition_broadcast(P)).then_inc(s.trig_in.up, 16)
    with sp.Fori(A_CHUNKS // 4, A_CHUNKS // 2) as i:
        for p in range(2):
            sp_modulation(sp, e, 0, i, p)
    sp.wait_ge(s.trig_sin.up, 3)
    with sp.Fori(0, DEPTH - 1) as l:
        sp_layer1(sp, e, l, True)
    sp_layer1(sp, e, DEPTH - 1, False)
    lay = Layer(s, 1, DEPTH)
    for m in range(2):
        sp.wait_ge(*lay.bank_free(m, 0))
    sp.dma_start(b.t_pi[:, :], a["positions_2"].partition_broadcast(P)).then_inc(s.trig_in.up, 16)
    with sp.Fori(0, DEPTH) as l:
        sp_layer2(sp, e, l)
    for t in range(NB):
        sp.wait_ge(s.y.up, 2 * t + 2)
        sp.dma_start(e.out[0, t * P:(t + 1) * P, :], b.y_out[:, t, :]).then_inc(s.y_out.up, 16)
    sp.wait_ge(s.y_out.up, 16 * NB)



def act_split(act, e, lay, j2, p, n=2048):
    s, b, u = e.s, e.b, lay.pair(j2)
    act.wait_ge(*s.raw_in(u, p))
    act.wait_ge(*s.slot_free(u, p))
    act.activation(b.w_hi[p][:, 0:n], b.raw[p][:, 0:n], ACT.Copy).then_inc(s.hi.up, 1)


def act_rms(act, e, c, ready, gain, shift, full, between=None):
    s, b, bank = e.s, e.b, e.bank
    for k in range(KD):
        ready(act, k)
        act.activation(b.sq[:, k, :], b.x[:, k, :], ACT.Square).then_inc(s.sq.up, 1)
    if between:
        between()
    act.preload_act_table_set("natural_log_exp_and_others")
    act.wait_ge(*s.rms(c, 1))
    act.activation(b.r[:, :], bank[7][:, :], ACT.Ln, bias=b.eps[:, 0:1], scale=1.0 / D).then_inc(s.r_ln.up, 1)
    act.wait_ge(*s.r_ln(c, 1))
    act.activation(b.r[:, :], b.r[:, :], ACT.Exp, scale=-0.5).then_inc(s.r.up, 1)
    if full:
        for k in range(KD):
            act.wait_ge(*s.xr(c, k + 1))
            act.activation(b.h_hi[:, k, :], b.sq[:, k, :], ACT.Identity,
                           bias=0.0 if shift is None else shift[:, k:k + 1],
                           scale=gain[:, k:k + 1]).then_inc(s.hh.up, 1)


def act_ffn(act, e, lay, j0, q0):
    s, b, bank = e.s, e.b, e.bank
    act.preload_act_table(ACT.Silu)

    def body(i, last):
        for m in range(2):
            act.wait_ge(*s.tile(lay.pair(i + j0 // 2), 0, m))
            act.wait_ge(*s.upb[m](lay.ffn, i))
            act.activation(b.f_act[:, m, :], bank[m][:, :], ACT.Silu).then_inc(s.bank[m].up, 1)
        n = 11 * P if last else 2048
        act_split(act, e, lay, i + (j0 // 2 + 1), 0, n)
        for m in range(2):
            act.wait_ge(*s.upb[m](lay.ffn, i + 1))
            act.activation(cols(b.f_hi, i * 2 + m), b.f_full[:, m, :], ACT.Copy).then_inc(s.fh.up, 1)
        act_split(act, e, lay, i + (j0 // 2 + 1), 1, n)

    with act.Fori(0, 10) as i:
        body(i, False)
    body(10, True)
    with act.Fori(0, 7) as i:
        for p in range(2):
            act_split(act, e, lay, i + (j0 // 2 + 12), p, 11 * P)


def act_attn_exp(act, e, blk, l, h, prob):
    s, b, bank = e.s, e.b, e.bank
    t = attention(s, blk)
    if h >= 1:
        act.wait_ge(*t.tp(l, 3 * h))
    for g, blocks in enumerate(BY_QUERY):
        act.wait_ge(*t.mx(l, 3 * h + g + 1))
        for i in blocks:
            c = 0 if len(blocks) == 1 else (0 if i == 0 else P)
            act.activation(prob[:, P_AT[i]:P_AT[i] + CAUSAL[i]], bank[SC_BANK[g]][:, c:c + CAUSAL[i]], ACT.Exp,
                           bias=b.small[:, i:i + 1], scale=HD ** -0.5,
                           accum_out=b.small[:, 4 + i:5 + i]).then_inc(t.ex.up, 1)


def act_attn_pt(act, e, blk, l, h, probT):
    s, bank = e.s, e.bank
    t = attention(s, blk)
    if h >= 1:
        act.wait_ge(*t.pv(l, h))
    for g, blocks in enumerate(BY_KEY):
        act.wait_ge(*t.tp(l, 3 * h + g + 1))
        for j in blocks:
            c, n = (0 if j != 3 else 384), T - P * j
            op = act.activation(probT[:, PT_AT[j]:PT_AT[j] + n], bank[TP_BANK[g]][:, c:c + n], ACT.Copy)
        op.then_inc(t.pt.up, 1)


def act_attn_out(act, e, blk, l, h, mf, tile):
    s, bank = e.s, e.bank
    t = attention(s, blk)
    o = HD * (h % 2)
    act.wait_ge(*t.pv(l, h + 1))
    act.activation(mf[o:o + HD, tile, :], bank[5][o:o + HD, :], ACT.Copy).then_inc(t.po.up, 1)


SC_BANK = [3, 4, 2]
TP_BANK = [6, 7, 5]


def act_layer1(act, e, l):
    s, b, bank = e.s, e.b, e.bank
    lay = Layer(s, 1, l)

    def first_two():
        act_split(act, e, lay, 0, 0)
        act_split(act, e, lay, 0, 1)

    def x_ready(eng, k):
        if k == 0:
            eng.wait_ge(*lay.bank_free(0, 0))
            eng.wait_ge(*lay.bank_free(1, 0))

    act_rms_pair(act, e, l, 0, x_ready, first_two)
    act.wait_ge(*s.ls_d(l, 1))
    act.activation(b.ls[:, 0, :], b.ls[:, 1, :], ACT.Abs).then_inc(s.ls_a.up, 1)
    act.wait_ge(*s.ls_a(l, 1))
    act.activation(b.ls[:, 0, :], b.ls[:, 0, :], ACT.Exp, scale=-1.0).then_inc(s.ls_a.up, 1)
    act.wait_ge(*s.ls_a(l, 2))
    act.activation(b.ls[:, 0, :], b.ls[:, 0, :], ACT.Ln, bias=b.eps[0:4, 3:4]).then_inc(s.ls_a.up, 1)

    def take(j, m, out, func=ACT.Copy):
        act.wait_ge(*s.tile(lay.pair(j // 2), j % 2, m))
        act.activation(out, bank[m][:, :], func).then_inc(s.bank[m].up, 1)

    def split(j):
        act_split(act, e, lay, j // 2, j % 2)

    for m in range(2):
        take(0, m, b.cgate[:, m, 0:T], ACT.Sigmoid)
    act.preload_act_table_set("natural_log_exp_and_others")
    split(2)
    split(3)
    for j in (2, 3):
        for m in range(2):
            if j == 3:
                act.wait_ge(*s.rot(l, m + 1))
                act.wait_ge(*s.rope(l, 3 * m + 1))
            take(j, m, b.rraw[:, m, :])
        split(j + 2)
    for m in range(2):
        take(4, m, b.rv[:, 2 * m:2 * m + 2, :].rearrange("p t c -> p (t c)"))
    split(6)
    for m in range(2):
        take(5, m, b.fq[:, m, :])
    act.wait_ge(*s.ls_d(l, 3))
    act.activation(b.cum[0:4, :], b.ls[:, 2, :], ACT.Copy).then_inc(s.ck.up, 1)
    split(7)
    for m in range(2):
        take(6, m, b.fk[:, m, :])
    split(8)
    for m in range(2):
        take(7, m, b.fv[:, 2 * m:2 * m + 2, :].rearrange("p t c -> p (t c)"))
    split(9)
    for m in range(2):
        act.wait_ge(*s.pads(l, 2))
        take(8, m, b.pu[:, m, 16:16 + T])
    split(10)
    act_attn_exp(act, e, 1, l, 0, b.prob)
    for m in range(2):
        take(9, m, b.rg[:, m, :], ACT.Silu)
    act.preload_act_table_set("natural_log_exp_and_others")
    split(11)
    act_attn_pt(act, e, 1, l, 0, b.probT)
    act_attn_exp(act, e, 1, l, 1, b.prob)
    for m in range(2):
        act.wait_ge(*s.gn_x(l, m + 1))
        act.activation(b.ln_s[:, m, :], b.ln_d[:, m, :], ACT.Square).then_inc(s.gn_sq.up, 1)
    act_attn_out(act, e, 1, l, 0, b.mf, 0)
    act_attn_pt(act, e, 1, l, 1, b.probT)
    act_attn_exp(act, e, 1, l, 2, b.prob)
    for m in range(2):
        act.wait_ge(*s.gn_ps(l, 2 + m + 1))
        act.activation(b.ln_s[:, m, :], bank[m][:, :], ACT.Ln, bias=b.eps[:, 0:1]).then_inc(s.bank[m].up, 1)
        act.wait_ge(*lay.bank_out(m, Q_GN2))
        act.activation(b.ln_s[:, m, :], b.ln_s[:, m, :], ACT.Exp, scale=-0.5).then_inc(s.gn_r.up, 1)
    for m in range(2):
        act.wait_ge(*s.pl_sum(l, 6))
        act.activation(b.cgate[HD:P, m, 16:], b.wb[HD:P, m, 16:], ACT.Copy).then_inc(s.pl_up.up, 1)
    act_attn_out(act, e, 1, l, 1, b.mf, 0)
    act_attn_pt(act, e, 1, l, 2, b.probT)
    act_attn_exp(act, e, 1, l, 3, b.prob)
    for m in range(2):
        act.wait_ge(*s.pl_ps(l, m + 1))
        act.activation(b.mf[:, 2 + m, :], bank[m][:, :], ACT.Identity, scale=b.par[:, 64 + m:65 + m])\
           .then_inc(s.bank[m].up, 1)
    act_attn_out(act, e, 1, l, 2, b.mf, 1)
    act_attn_pt(act, e, 1, l, 3, b.probT)

    def mix_hi(ns):
        for n in ns:
            k = MIX_ORDER[n]
            act.wait_ge(*{0: s.po(l, 2), 1: s.po(l, 4), 2: lay.bank_out(0, Q_POOL), 3: lay.bank_out(1, Q_POOL),
                          4: s.gn_o(l, 1), 5: s.gn_o(l, 2), 6: s.cn_o(l, 1), 7: s.cn_o(l, 2)}[k])
            act.activation(b.h_hi[:, k, :], b.mf[:, k, :], ACT.Copy).then_inc(s.mh.up, 1)

    act.wait_ge(*s.tile(lay.pair(4), 1, 1))
    mix_hi(range(5))
    for m in range(2):
        act.wait_ge(*s.cn_x(l, m + 1))
        act.activation(b.ln_s[:, m, :], b.ln_d[:, m, :], ACT.Square).then_inc(s.cn_sq.up, 1)
    act.wait_ge(*s.cn_ps(l, 2))
    act.activation(b.r[:, :], bank[1][:, :], ACT.Ln, bias=b.eps[:, 0:1], scale=1.0 / G).then_inc(s.bank[1].up, 1)
    act.wait_ge(*lay.bank_out(1, Q_CONV))
    act.activation(b.r[:, :], b.r[:, :], ACT.Exp, scale=-0.5).then_inc(s.cn_r.up, 1)
    act_attn_out(act, e, 1, l, 3, b.mf, 1)
    for m in range(2):
        act.wait_ge(*s.cn_xr(l, m + 1))
        act.activation(b.mf[:, 6 + m, :], b.ln_d[:, m, :], ACT.Silu, bias=b.par[:, 72 + m:73 + m],
                       scale=b.par[:, 70 + m:71 + m]).then_inc(s.cn_o.up, 1)
    mix_hi(range(5, KD))
    split(12)
    split(13)

    def x_mixed(eng, k):
        eng.wait_ge(*lay.bank_out(k % 2, Q_OUT + k // 2))

    def first_splits():
        split(14)
        split(15)

    act_rms_pair(act, e, l, 1, x_mixed, first_splits)
    act_ffn(act, e, lay, 14, Q_FFN)


def act_rms_pair(act, e, l, j, ready, between=None):
    b = e.b
    shift = b.mod[:, 0:8] if j == 0 else b.mod[:, 24:32]
    act_rms(act, e, l * 2 + j, ready, b.gain[:, 8 * j:8 * j + 8], shift, True, between)


def act_layer_norm(act, e, c, g0, between=None):
    s, b, bank = e.s, e.b, e.bank
    for k in range(KD):
        act.wait_ge(*s.ld(c, k + 1))
        act.activation(b.sq[:, k, :], b.x[:, k, :], ACT.Square).then_inc(s.lsq.up, 1)
    if between:
        between()
    act.preload_act_table_set("natural_log_exp_and_others")
    act.wait_ge(*s.lvar(c, 1))
    act.activation(b.r[:, :], bank[7][:, :], ACT.Ln, bias=b.eps[:, 1:2], scale=1.0 / D).then_inc(s.l_ln.up, 1)
    act.wait_ge(*s.l_ln(c, 1))
    act.activation(b.r[:, :], b.r[:, :], ACT.Exp, scale=-0.5).then_inc(s.l_r.up, 1)
    for k in range(KD):
        act.wait_ge(*s.lxr(c, k + 1))
        act.activation(b.h_hi[:, k, :], b.sq[:, k, :], ACT.Identity, bias=b.par[:, g0 + 8 + k:g0 + 9 + k],
                       scale=b.par[:, g0 + k:g0 + k + 1]).then_inc(s.lhh.up, 1)


def act_layer2(act, e, l, more):
    s, b, bank = e.s, e.b, e.bank
    lay = Layer(s, 2, l)

    def split(j):
        act_split(act, e, lay, j // 2, j % 2)

    def take(j, m, out, func=ACT.Copy):
        act.wait_ge(*s.tile(lay.pair(j // 2), j % 2, m))
        act.activation(out, bank[m][:, :], func).then_inc(s.bank[m].up, 1)

    def raw(r, j, m):
        if r >= 3:
            act.wait_ge(*s.rot2(l, r - 2))
            act.wait_ge(*s.rope2(l, 3 * (r - 3) + 1))
        take(j, m, b.n_raw[:, r % 3, :])

    split(1)
    raw(0, 0, 0)
    raw(1, 0, 1)
    split(2)
    take(1, 0, b.n_v[:, :, :].rearrange("p t c -> p (t c)"))
    raw(2, 1, 1)
    split(3)
    raw(3, 2, 0)
    raw(4, 2, 1)
    split(4)
    raw(5, 3, 0)
    raw(6, 3, 1)
    split(5)
    raw(7, 4, 0)
    raw(8, 4, 1)
    split(6)
    act.preload_act_table(ACT.Gelu_apprx_tanh)
    for j in (5, 6):
        for m in range(2):
            take(j, m, b.n_u[:, 2 * (j - 5) + m, :], ACT.Gelu_apprx_tanh)
        split(j + 2)
    for j in (7, 8):
        for m in range(2):
            act.wait_ge(*s.tile(lay.pair(j // 2), j % 2, m))
            act.activation(b.n_vs[:, 2 * m:2 * m + 2, (j - 7) * G:(j - 6) * G],
                           bank[m][:, :].rearrange("p (t c) -> p t c", t=2), ACT.Gelu_apprx_tanh)\
               .then_inc(s.bank[m].up, 1)
        split(j + 2)
    act.preload_act_table_set("natural_log_exp_and_others")

    def mix_hi(ns):
        for n in ns:
            k = MIX2_ORDER[n]
            act.wait_ge(*(s.po2(l, 2 * k + 2) if k < 4 else lay.bank_out(k % 2, Q2_SGU + (k - 4) // 2)))
            act.activation(b.h_hi[:, k, :], b.mf[:, k, :], ACT.Copy).then_inc(s.mh2.up, 1)

    act.wait_ge(*s.tile(lay.pair(4), 0, 1))
    for h in range(8):
        act_attn_exp(act, e, 2, l, h, b.n_prob)
        if h >= 1:
            act_attn_out(act, e, 2, l, h - 1, b.mf, (h - 1) // 2)
        act_attn_pt(act, e, 2, l, h, b.n_probT)
        mix_hi({2: [0], 4: [1], 5: [2], 6: [3, 4], 7: [5]}.get(h, []))
        if h == 0:
            act.wait_ge(*s.bn(l, 8))
            act.activation(b.n_st[:, :, 6:7], b.n_st[:, :, 1:2], ACT.Ln, bias=b.eps[:, 1:2]).then_inc(s.v_ln.up, 1)
            act.wait_ge(*s.v_ln(l, 1))
            act.activation(b.n_st[:, :, 6:7], b.n_st[:, :, 6:7], ACT.Exp, scale=-0.5).then_inc(s.v_r.up, 1)
    act_attn_out(act, e, 2, l, 7, b.mf, 3)
    mix_hi(range(6, KD))
    split(11)
    split(12)
    act_split(act, e, lay, 6, 1)
    split(14)
    for m in range(2):
        act.wait_ge(*s.p_t(l, m + 1))
        act.activation(b.e_pf[:, m, :], bank[2 + m][:, :], ACT.Copy).then_inc(s.p_f.up, 1)
    for m in range(2):
        act.wait_ge(*s.p_f(l, m + 1))
        act.activation(b.e_hi[:, m, :], b.e_pf[:, m, :], ACT.Copy).then_inc(s.p_h.up, 1)
    act_layer_norm(act, e, l * 2, 0)
    for k in range(KD):
        if k < KD - 1:
            act.wait_ge(*s.ple(l, k + 1))
        else:
            act.wait_ge(*s.tile(lay.pair(6), 1, 1))
        act.activation(b.e_ple[:, k, :], bank[k % 2][:, :], ACT.Copy).then_inc(s.bank[k % 2].up, 1)
    split(15)
    for k in range(KD):
        if k >= 2:
            act.wait_ge(*s.gx(l, 2 * (k - 2) + 2))
        take(14 + k // 2, k % 2, b.e_sig[:, k % 2, :], ACT.Sigmoid)
        if k % 2:
            split(16 + k // 2)
    act_ffn(act, e, lay, 18, Q2_FFN)
    act_layer_norm(act, e, l * 2 + 1, 16, (lambda: first_unit2(act, e, l + 1)) if more else None)


def first_unit2(act, e, l):
    act_split(act, e, Layer(e.s, 2, l), 0, 0)


def act_program(act, e):
    s, b, bank = e.s, e.b, e.bank
    act.sem_inc(s.lhh.up, s.lhh.credit)
    act.wait_ge(s.z_in.up, 64)
    act.activation(b.z_cs[:, :], b.z_c[:, :], ACT.Silu).then_inc(s.z_act.up, 1)
    act_trig(act, e, 0)
    act.wait_ge(s.z_x.up, KD)
    with act.Fori(0, DEPTH - 1) as l:
        act_layer1(act, e, l)
    act_layer1(act, e, DEPTH - 1)
    lay = Layer(s, 1, DEPTH)

    def x_ready(eng, k):
        if k == 0:
            for m in range(2):
                eng.wait_ge(*lay.bank_free(m, 0))

    act_rms(act, e, 2 * DEPTH, x_ready, b.fg, None, True, lambda: first_unit2(act, e, 0))
    act_trig(act, e, 1)
    with act.Fori(0, DEPTH - 1) as l:
        act_layer2(act, e, l, True)
    act_layer2(act, e, DEPTH - 1, False)


def act_trig(act, e, which):
    s, b = e.s, e.b
    act.wait_ge(s.trig.up, 8 * which + 8)
    act.activation(b.sine[:, :], b.t_a[:, :], ACT.Sin).then_inc(s.trig_sin.up, 1)
    act.activation(b.t_b[:, :], b.t_a[:, :], ACT.Abs).then_inc(s.trig_sin.up, 1)
    act.wait_ge(s.trig_sin.up, 3 * which + 2)
    act.activation(b.cosine[:, :], b.t_b[:, :], ACT.Sin, bias=b.eps[:, 2:3], scale=-1.0).then_inc(s.trig_sin.up, 1)



def pool_split(pool, e, lay, j2, p, n=2048):
    s, b, u = e.s, e.b, lay.pair(j2)
    pool.wait_ge(*s.hi_in(u, p))
    pool.tensor_tensor(b.w_lo[p][:, 0:n], b.raw[p][:, 0:n], b.w_hi[p][:, 0:n].bitcast(F32), ALU.subtract)\
        .then_inc(s.lo.up, 1)


def pool_h_lo(pool, e, c, full=None, done=None, half=None):
    s, b = e.s, e.b
    full = b.hf if full is None else full
    for k in range(KD):
        if k == KD // 2 and half is not None:
            pool.wait_ge(*half)
        pool.wait_ge(*s.hf(c, k + 1))
        pool.wait_ge(*s.hh(c, k + 1))
        pool.tensor_tensor(b.h_lo[:, k, :], full[:, k, :], b.h_hi[:, k, :].bitcast(F32), ALU.subtract)\
            .then_inc((s.hl if done is None else done).up, 1)


def pool_ffn(pool, e, lay, j0):
    s, b = e.s, e.b

    def body(i, last):
        n = 11 * P if last else 2048
        pool_split(pool, e, lay, i + (j0 // 2 + 1), 0, n)
        for m in range(2):
            pool.wait_ge(s.fh.up, lay.ffn * 22 + i * 2 + (m + 1))
            pool.tensor_tensor(cols(b.f_lo, i * 2 + m), b.f_full[:, m, :], cols(b.f_hi, i * 2 + m).bitcast(F32),
                               ALU.subtract).then_inc(s.fl.up, 1)
        pool_split(pool, e, lay, i + (j0 // 2 + 1), 1, n)

    with pool.Fori(0, 10) as i:
        body(i, False)
    body(10, True)
    with pool.Fori(0, 7) as i:
        for p in range(2):
            pool_split(pool, e, lay, i + (j0 // 2 + 12), p, 11 * P)


def pool_window(pool, e, l):
    s, b = e.s, e.b
    lay = Layer(s, 1, l)
    steps = [(b.cgate, b.pu, 0, 0, 1, 2), (b.wb, b.cgate, 0, HD, 2, 4),
             (b.cgate, b.pu, 1, 0, 1, 2), (b.wb, b.cgate, 1, 0, 2, 4), (b.cgate, b.wb, 1, 0, 4, 8),
             (b.wb, b.cgate, 1, HD, 8, 16)]
    for n, (dst, src, m, lo, back, at) in enumerate(steps):
        pool.wait_ge(*lay.bank_out(m, 8))
        if n:
            pool.wait_ge(*s.pl_sum(l, n))
        pool.tensor_tensor(dst[lo:P, m, at:], src[lo:P, m, at:], src[lo:P, m, at - back:T + 16 - back], ALU.add)\
            .then_inc(s.pl_sum.up, 1)


def pool_layer1(pool, e, l):
    s, b = e.s, e.b
    lay = Layer(s, 1, l)
    for m in range(2):
        lone_wait(pool, s, *lay.bank_free(m, 0))
    pool.memset(b.ch[:, :, 0:TAPS - 1], 0.0).then_inc(s.pads.up, 1)
    pool.memset(b.pu[:, :, 0:16], 0.0).then_inc(s.pads.up, 1)
    for j in range(2):
        pool_split(pool, e, lay, 0, j)
    pool_h_lo(pool, e, l * 2, half=s.a_pe(l, 2))
    for j in range(2, 12):
        pool_split(pool, e, lay, j // 2, j % 2)
    pool_window(pool, e, l)
    for n, k in enumerate(MIX_ORDER):
        pool.wait_ge(*s.mh(l, n + 1))
        pool.tensor_tensor(b.h_lo[:, k, :], b.mf[:, k, :], b.h_hi[:, k, :].bitcast(F32), ALU.subtract)\
            .then_inc(s.ml.up, 1)
    for j in range(12, 16):
        pool_split(pool, e, lay, j // 2, j % 2)
    pool_h_lo(pool, e, l * 2 + 1)
    pool_ffn(pool, e, lay, 14)


def pool_layer_norm(pool, e, c):
    s, b = e.s, e.b
    for k in range(KD):
        pool.wait_ge(*s.lx(c, k + 1))
        pool.wait_ge(*s.lhh(c, k + 1))
        pool.tensor_tensor(b.h_lo[:, k, :], b.x[:, k, :], b.h_hi[:, k, :].bitcast(F32), ALU.subtract)\
            .then_inc(s.lhl.up, 1)


def pool_layer2(pool, e, l, more):
    s, b = e.s, e.b
    lay = Layer(s, 2, l)
    for j in range(1, 11):
        pool_split(pool, e, lay, j // 2, j % 2)
    for t in range(NB):
        pool.wait_ge(*s.v_n(l, t + 1))
        pool.tensor_tensor(b.n_vs[:, t, :], b.n_vs[:, t, :], b.n_g[:, :], ALU.mult).then_inc(s.v_g.up, 1)
        pool.wait_ge(*s.v_g(l, 2 * t + 1))
        pool.tensor_tensor(b.n_vs[:, t, :], b.n_vs[:, t, :], b.n_b[:, :], ALU.add).then_inc(s.v_g.up, 1)
    for n, k in enumerate(MIX2_ORDER):
        pool.wait_ge(*s.mh2(l, n + 1))
        pool.tensor_tensor(b.h_lo[:, k, :], b.mf[:, k, :], b.h_hi[:, k, :].bitcast(F32), ALU.subtract)\
            .then_inc(s.ml2.up, 1)
    for j in range(11, 15):
        pool_split(pool, e, lay, j // 2, j % 2)
    for m in range(2):
        pool.wait_ge(*s.p_h(l, m + 1))
        pool.tensor_tensor(b.e_lo[:, m, :], b.e_pf[:, m, :], b.e_hi[:, m, :].bitcast(F32), ALU.subtract)\
            .then_inc(s.p_l.up, 1)
    pool_layer_norm(pool, e, l * 2)
    for j in range(15, 20):
        pool_split(pool, e, lay, j // 2, j % 2)
    pool_ffn(pool, e, lay, 18)
    if more:
        pool_split(pool, e, Layer(s, 2, l + 1), 0, 0)
    pool_layer_norm(pool, e, l * 2 + 1)


def pool_program(pool, e):
    s, b = e.s, e.b
    pool.sem_inc(s.lo.up, s.lo.credit)
    pool.sem_inc(s.fl.up, s.fl.credit)
    pool.wait_ge(s.trig_sin.up, 3)
    with pool.Fori(0, DEPTH - 1) as l:
        pool_layer1(pool, e, l)
    pool_layer1(pool, e, DEPTH - 1)
    pool_split(pool, e, Layer(s, 2, 0), 0, 0)
    pool_h_lo(pool, e, 2 * DEPTH, b.x, s.lhl)
    with pool.Fori(0, DEPTH - 1) as l:
        pool_layer2(pool, e, l, True)
    pool_layer2(pool, e, DEPTH - 1, False)



COPIES = [("eye", "eye"), ("turn1", "t0"), ("heads", "heads"), ("tril", "tril"), ("eye", "eye_r"),
          ("causal", "causal_r"), ("chunked", "chunked_r"), ("pick", "pick_r"),
          ("freq1", "f0"), ("freq2", "f1"), ("window", "window"), ("counts", "counts")]
Z_COPIES = len(COPIES)
C1 = 6.28125
C2 = float(np.float32(round((2 * np.pi - C1) * 2 ** 21) / 2 ** 21))
C3 = float(np.float32(2 * np.pi - C1 - C2))


def dve_trig(dve, e, which):
    s, b = e.s, e.b
    n = [8 * which]

    def done(op):
        op.then_inc(s.trig.up, 1)
        n[0] += 1
        dve.wait_ge(s.trig.up, n[0])

    done(dve.tensor_copy(b.t_pf[:, :], b.t_pi[:, :]))
    done(dve.tensor_scalar(b.t_ang[:, :], b.t_pf[:, :], b.freq[:, which:which + 1], None, ALU.mult))
    done(dve.tensor_scalar(b.t_ni[:, :], b.t_ang[:, :], 1.0 / (2 * np.pi), None, ALU.mult))
    done(dve.tensor_copy(b.t_n[:, :], b.t_ni[:, :]))
    done(dve.scalar_tensor_tensor(b.t_a[:, :], b.t_n[:, :], -C1, b.t_ang[:, :], ALU.mult, ALU.add))
    done(dve.scalar_tensor_tensor(b.t_b[:, :], b.t_n[:, :], -C2, b.t_a[:, :], ALU.mult, ALU.add))
    done(dve.scalar_tensor_tensor(b.t_a[:, :], b.t_n[:, :], -C3, b.t_b[:, :], ALU.mult, ALU.add))
    dve.tensor_scalar(b.t_a[:, :], b.t_a[:, :], -3.1415925, 3.1415925, ALU.max, ALU.min).then_inc(s.trig.up, 1)


def dve_setup(dve, e):
    b, s, bank = e.b, e.s, e.bank
    dve.memset(b.ones[:, :], 1.0).then_inc(s.z_ready.up, 1)
    for n, v in enumerate((EPS, LN_EPS, float(np.pi / 2), 1.0)):
        dve.memset(b.eps[:, n:n + 1], v).then_inc(s.z_ready.up, 1)
    dve.wait_ge(s.z_in.up, 64)
    dst = dict(eye=b.eye, t0=b.turn, heads=b.heads, tril=b.tril, eye_r=b.eye_r, causal_r=b.causal_r,
               chunked_r=b.chunked_r, window=b.window)
    for src, name in COPIES:
        c, n = e.at[src]
        if name == "pick_r":
            op = dve.tensor_copy(b.pick_r[:, :, :].rearrange("p a b -> p (a b)"), b.z_tab[:, c:c + n])
        elif name == "counts":
            op = dve.tensor_copy(b.counts[:, :, :].rearrange("p a b -> p (a b)"), b.z_tab[:, c:c + n])
        elif name in ("f0", "f1"):
            op = dve.tensor_copy(b.freq[:, int(name[1]):int(name[1]) + 1], b.z_tab[:, c:c + n])
        else:
            op = dve.tensor_copy(dst[name][:, :], b.z_tab[:, c:c + n])
        op.then_inc(s.z_copied.up, 1)
    for k in range(KD):
        dve.wait_ge(s.z_xt.up, k + 1)
        dve.tensor_copy(b.x[:, k, :], bank[2 + k % 4][:, :]).then_inc(s.z_x.up, 1)
    dve.wait_ge(s.z_xt.up, KD + 1)
    dve.tensor_copy(b.c[:, :], bank[6][:, 0:KD]).then_inc(s.z_x.up, 1)
    dve.wait_ge(s.z_xt.up, KD + 2)
    dve.tensor_copy(b.fg[:, :], bank[7][:, 0:KD]).then_inc(s.z_x.up, 1)


def dve_weigh(dve, raw, acc, c, up, base, ks=range(KD)):
    for k in ks:
        if k == 0:
            dve.tensor_scalar(acc, raw[:, 0, :], c[:, 0:1], None, ALU.mult).then_inc(up, 1)
        else:
            dve.wait_ge(up, base + k)
            dve.scalar_tensor_tensor(acc, raw[:, k - ks[0], :], c[:, k:k + 1], acc, ALU.mult, ALU.add)\
               .then_inc(up, 1)


def dve_modulation(dve, e, l, i, p):
    s, b = e.s, e.b
    for q in range(2):
        came = s.a_in[2 * p + q]
        dve.wait_ge(came.up, l * came.per + i * 16 + 16)
        dve_weigh(dve, b.a_raw[2 * p + q], b.a_acc[:, bass.ts(i * 2 + p, G)], b.c, s.a_acc.up,
                  l * s.a_acc.per + i * 16 + (s.a_acc.credit + 8 * p), range(4 * q, 4 * q + 4))


def dve_mod(dve, e, l, part):
    s, b = e.s, e.b
    v = slice(2 * KD * part, 2 * KD * (part + 1))
    dve.tensor_tensor(b.mod[:, v], e.bank[MOD_BANK[part]][:, v], b.par[:, 16 + v.start:16 + v.stop], ALU.add)\
       .then_inc(s.mod.up, 1)


def dve_gains(dve, e, l, norm):
    s, b = e.s, e.b
    dve_mod(dve, e, l, 2 * norm)
    dve.wait_ge(*s.mod(l, 2 * norm + 1))
    dve.scalar_tensor_tensor(b.gain[:, 8 * norm:8 * norm + 8], b.mod[:, 8 + 24 * norm:16 + 24 * norm], 1.0,
                             b.par[:, 8 * norm:8 * norm + 8], ALU.add, ALU.mult).then_inc(s.gain.up, 1)


def dve_rms_sum(dve, e, c, k):
    s, b = e.s, e.b
    dve.wait_ge(*s.sq(c, k + 1))
    if k > 1:
        dve.wait_ge(*s.ssq(c, k - 1))
    dve.tensor_tensor(b.sq[:, 0, :], b.sq[:, 0, :], b.sq[:, k, :], ALU.add).then_inc(s.ssq.up, 1)


def dve_rms(dve, e, c, gain, shift, final=False, summed=False):
    s, b = e.s, e.b
    if not summed:
        for k in range(1, KD):
            dve_rms_sum(dve, e, c, k)
    dve.wait_ge(*s.r(c, 1))

    def finish(k):
        dve.wait_ge(*s.xr(c, k + 1))
        if final:
            dve.tensor_scalar(b.x[:, k, :], b.sq[:, k, :], gain[:, k:k + 1], None, ALU.mult).then_inc(s.hf.up, 1)
        else:
            dve.tensor_scalar(b.hf[:, k, :], b.sq[:, k, :], gain[:, k:k + 1], shift[:, k:k + 1], ALU.mult, ALU.add)\
               .then_inc(s.hf.up, 1)

    for k in range(KD):
        dve.tensor_tensor(b.sq[:, k, :], b.x[:, k, :], b.r[:, :], ALU.mult).then_inc(s.xr.up, 1)
        if k:
            finish(k - 1)
    finish(KD - 1)


def dve_max(dve, e, blk, l, h):
    s, b, bank = e.s, e.b, e.bank
    t = attention(s, blk)
    if h:
        dve.wait_ge(*t.ex(l, 4 * h))
    for g, blocks in enumerate(BY_QUERY):
        dve.wait_ge(*t.sc(l, 3 * h + g + 1))
        for i in blocks:
            c = 0 if len(blocks) == 1 else (0 if i == 0 else P)
            dve.tensor_reduce(b.small[:, 16 + i:17 + i], bank[SC_BANK[g]][:, c:c + CAUSAL[i]], AX, ALU.max)\
               .then_inc(t.mxr.up, 1)
        n = (2, 3, 4)[g]
        dve.wait_ge(*t.mxr(l, 4 * h + n))
        first, step = blocks[0], (2 if g == 0 else 1)
        dve.tensor_scalar(b.small[:, first:blocks[-1] + 1:step], b.small[:, 16 + first:17 + blocks[-1]:step],
                          -HD ** -0.5, None, ALU.mult).then_inc(t.mx.up, 1)


def dve_normalise(dve, e, blk, l, h, prob):
    s, b = e.s, e.b
    t = attention(s, blk)
    dve.wait_ge(*t.ex(l, 4 * h + 4))
    dve.reciprocal(b.small[:, 8:12], b.small[:, 4:8]).then_inc(t.rcp.up, 1)
    dve.wait_ge(*t.rcp(l, h + 1))
    for i in (0, 2, 1, 3):
        v = prob[:, P_AT[i]:P_AT[i] + CAUSAL[i]]
        dve.tensor_scalar(v, v, b.small[:, 8 + i:9 + i], None, ALU.mult).then_inc(t.pn.up, 1)


def dve_ffn(dve, e, lay, j0, gate):
    s, b, bank = e.s, e.b, e.bank

    def body(i):
        for m in range(2):
            dve.wait_ge(*s.tile(lay.pair(i + j0 // 2), 1, m))
            dve.wait_ge(lay.s.bank[m].up, lay.use0 + i + (gate[0] + 2))
            dve.wait_ge(s.fl.up, lay.ffn * 22 + i * 2 + (m + 1))
            dve.tensor_tensor(b.f_full[:, m, :], b.f_act[:, m, :], bank[2 + m][:, :], ALU.mult)\
               .then_inc(s.upb[m].up, 1)

    with dve.Fori(0, 11) as i:
        body(i)


def dve_layer1(dve, e, l, more):
    s, b, bank = e.s, e.b, e.bank
    lay = Layer(s, 1, l)
    for k in range(1, KD):
        dve_rms_sum(dve, e, l * 2, k)
    for n, (dst, w, k) in enumerate(((b.par, 74, 4), (b.taps, 2 * TAPS, 5))):
        dve.wait_ge(*s.par_t(l, n + 1))
        dve.tensor_copy(dst[:, 0:w], bank[k][:, 0:w]).then_inc(s.par.up, 1)
    dve.wait_ge(*s.a_pe(l, 1))
    dve.wait_ge(*s.par(l, 2))
    dve_gains(dve, e, l, 0)
    dve.wait_ge(*s.gain(l, 1))
    dve_rms(dve, e, l * 2, b.gain, b.mod[:, 0:8], summed=True)
    dve.wait_ge(*s.a_pe(l, 2))
    dve_mod(dve, e, l, 1)
    dve.wait_ge(*s.ff(l, 1))
    dve.memset(b.ls[:, 3, :], 1.0).then_inc(s.ls_1.up, 1)
    dve.memset(b.cum[:, :].bitcast(F32), 0.0).then_inc(s.ls_1.up, 1)
    dve.tensor_scalar(b.ls[:, 1, :], bank[2][0:4, :], b.fb[:, 0:1], None, ALU.add).then_inc(s.ls_d.up, 1)
    dve.wait_ge(*s.ls_d(l, 1))
    dve.wait_ge(*s.ls_a(l, 3))
    dve.scalar_tensor_tensor(b.ls[:, 1, :], b.ls[:, 1, :], 0.0, b.ls[:, 0, :], ALU.min, ALU.subtract)\
       .then_inc(s.ls_d.up, 1)
    dve.wait_ge(*s.ls_d(l, 2))
    dve.wait_ge(*s.ls_1(l, 2))
    dve.tensor_tensor_scan(b.ls[:, 2, :], b.ls[:, 3, :], b.ls[:, 1, :], 0.0, ALU.mult, ALU.add)\
       .then_inc(s.ls_d.up, 1)
    for m in range(2):
        dve.wait_ge(*s.tile(lay.pair(0), 1, m))
        dve.wait_ge(*lay.bank_out(m, 0))
        dve.tensor_tensor(b.ch[:, m, TAPS - 1:], bank[m][:, :], b.cgate[:, m, 0:T], ALU.mult)\
           .then_inc(s.bank[m].up, 1)

    def conv(steps):
        for n in steps:
            t, m = n // 2, n % 2
            if n < 2:
                dve.wait_ge(*lay.bank_out(m, 1))
                dve.wait_ge(*s.pads(l, 2))
                dve.tensor_scalar(b.cv[:, m, :], b.ch[:, m, 0:T], b.taps[:, m:m + 1], b.par[:, 68 + m:69 + m],
                                  ALU.mult, ALU.add).then_inc(s.conv.up, 1)
            else:
                dve.wait_ge(*s.conv(l, n - 1))
                dve.scalar_tensor_tensor(b.cv[:, m, :], b.ch[:, m, t:t + T], b.taps[:, n:n + 1], b.cv[:, m, :],
                                         ALU.mult, ALU.add).then_inc(s.conv.up, 1)

    def rope(n):
        m, dst = n % 2, (b.rq if n < 2 else b.rk)
        dve.wait_ge(*lay.bank_out(m, 2 + n // 2))
        dve.tensor_tensor(dst[:, m, :], b.rraw[:, m, :], b.cosine[:, :], ALU.mult).then_inc(s.rope.up, 1)
        dve.wait_ge(*s.rot(l, n + 1))
        dve.tensor_tensor(b.ln_s[:, m, :], bank[2 + m][:, :], b.sine[:, :], ALU.mult).then_inc(s.rope.up, 1)
        dve.wait_ge(*s.rope(l, 3 * n + 2))
        dve.tensor_tensor(dst[:, m, :], dst[:, m, :], b.ln_s[:, m, :], ALU.add).then_inc(s.rope.up, 1)

    def decayed(h):
        if h:
            dve.wait_ge(*s.rv_ps(l, h))
        for g, blocks in enumerate(BY_KEY):
            dve.wait_ge(*s.decay_in(l, s.decay_in.per))
            dve.wait_ge(*s.rs_ps(l, 3 * h + g + 1))
            for j in blocks:
                c, n = (0 if j != 3 else 384), T - P * j
                dve.tensor_tensor(b.rs[:, PT_AT[j]:PT_AT[j] + n], bank[TP_BANK[g]][:, c:c + n],
                                  b.decay[:, h, 0:n], ALU.mult).then_inc(s.rs.up, 1)

    def retained(h):
        o = HD * (h % 2)
        dve.wait_ge(*s.rv_ps(l, h + 1))
        dve.tensor_copy(b.mf[o:o + HD, 4 + h // 2, :], bank[2][o:o + HD, :]).then_inc(s.rv_o.up, 1)

    conv(range(0, 8))
    rope(0)
    rope(1)
    conv(range(8, 16))
    rope(2)
    rope(3)
    conv(range(16, 24))
    decayed(0)
    dve.wait_ge(*s.ck(l, 1))
    dve.tensor_tensor(b.cum[32:36, :], b.ls[:, 2, :], b.cum[0:4, :].bitcast(F32), ALU.subtract)\
       .then_inc(s.ls_d.up, 1)
    conv(range(24, 34))
    retained(0)
    decayed(1)
    conv(range(34, 44))
    retained(1)
    decayed(2)
    conv(range(44, 54))
    retained(2)
    decayed(3)
    dve_max(dve, e, 1, l, 0)
    conv(range(54, 62))
    dve_normalise(dve, e, 1, l, 0, b.prob)
    retained(3)
    dve_max(dve, e, 1, l, 1)
    for m in range(2):
        dve.wait_ge(*s.gn_ps(l, m + 1))
        dve.tensor_tensor(b.ln_d[:, m, :], b.mf[:, 4 + m, :], bank[m][:, :], ALU.subtract).then_inc(s.gn_x.up, 1)
    dve_normalise(dve, e, 1, l, 1, b.prob)
    for m in range(2):
        dve.wait_ge(*s.gn_x(l, m + 1))
        dve.sem_inc(s.bank[m].up, 1)
    dve_max(dve, e, 1, l, 2)
    for m in range(2):
        dve.wait_ge(*s.gn_r(l, m + 1))
        dve.tensor_tensor(b.ln_d[:, m, :], b.ln_d[:, m, :], b.ln_s[:, m, :], ALU.mult).then_inc(s.gn_m.up, 1)
    for m in range(2):
        dve.wait_ge(*s.gn_m(l, m + 1))
        dve.wait_ge(*lay.bank_out(m, 9))
        dve.scalar_tensor_tensor(b.mf[:, 4 + m, :], b.ln_d[:, m, :], b.par[:, 66 + m:67 + m], b.rg[:, m, :],
                                 ALU.mult, ALU.mult).then_inc(s.gn_o.up, 1)
    for m in range(2):
        dve.wait_ge(*s.pl_up(l, m + 1))
        dve.scalar_tensor_tensor(b.wb[:, m, 0:T], b.cgate[:, m, 16:], b.window[:, m:m + 1], b.pu[:, m, 16:],
                                 ALU.mult, ALU.subtract).then_inc(s.pl_d.up, 1)
    dve.wait_ge(*s.pl_d(l, 2))
    dve.tensor_tensor(b.wb[:, :, 0:16], b.cgate[:, :, 16:32], b.counts[:, :, :], ALU.mult).then_inc(s.pl_d.up, 1)
    dve.wait_ge(*s.pl_d(l, 3))
    dve.tensor_tensor(b.wb[:, :, 0:16], b.wb[:, :, 0:16], b.pu[:, :, 16:32], ALU.subtract).then_inc(s.pl_d.up, 1)
    dve_normalise(dve, e, 1, l, 2, b.prob)
    dve_max(dve, e, 1, l, 3)
    dve.wait_ge(*s.cn_ps(l, 1))
    for m in range(2):
        dve.scalar_tensor_tensor(b.ln_d[:, m, :], bank[0][:, :], -1.0 / G, b.cv[:, m, :], ALU.mult, ALU.add)\
           .then_inc(s.cn_x.up, 1)
    dve_normalise(dve, e, 1, l, 3, b.prob)
    dve.wait_ge(*s.cn_x(l, 2))
    dve.sem_inc(s.bank[0].up, 1)
    dve.wait_ge(*s.cn_r(l, 1))
    for m in range(2):
        dve.tensor_tensor(b.ln_d[:, m, :], b.ln_d[:, m, :], b.r[:, :], ALU.mult).then_inc(s.cn_xr.up, 1)

    def weigh_b(n):
        dve.wait_ge(*s.b_in[n % 2](l, 16 * (n // 2) + 16))
        dve_weigh(dve, b.b_raw[n % 2], b.b_acc[:, n * G:(n + 1) * G], b.c, *s.b_acc(l, KD * n))

    weigh_b(0)
    weigh_b(1)
    for k in range(KD):
        if k >= 1 and k + 1 < B_CHUNKS:
            weigh_b(k + 1)
        dve.wait_ge(*s.tile(lay.pair(5 + k // 4), k // 2 % 2, k % 2))
        dve.scalar_tensor_tensor(b.x[:, k, :], bank[k % 2][:, :], b.mod[:, 16 + k:17 + k], b.x[:, k, :],
                                 ALU.mult, ALU.add).then_inc(s.bank[k % 2].up, 1)
        if k >= 2:
            dve_rms_sum(dve, e, l * 2 + 1, k - 1)
    dve_rms_sum(dve, e, l * 2 + 1, KD - 1)
    dve.wait_ge(*s.b_pe(l, 1))
    dve_gains(dve, e, l, 1)
    dve_rms(dve, e, l * 2 + 1, b.gain[:, 8:16], b.mod[:, 24:32], summed=True)
    dve_ffn(dve, e, lay, 14, (Q_FFN,))
    with dve.Fori(0, 4) as i:
        for m in range(2):
            if more:
                for p in range(2):
                    dve_modulation(dve, e, l + 1, i * 2 + m, p)
            dve.wait_ge(*s.tile(lay.pair(i * 2 + (18 + m)), 1, 1))
            xk = cols(b.x, i * 2 + m)
            dve.scalar_tensor_tensor(xk, bank[m][:, :], b.mod[:, bass.ds(i * 2 + (40 + m), 1)], xk,
                                     ALU.mult, ALU.add).then_inc(s.bank[m].up, 1)


def dve_layer_norm(dve, e, c, g0):
    s, b, bank = e.s, e.b, e.bank
    dve.wait_ge(*s.lmean(c, 1))
    for k in range(KD):
        dve.scalar_tensor_tensor(b.x[:, k, :], bank[6][:, :], -1.0 / D, b.x[:, k, :], ALU.mult, ALU.add)\
           .then_inc(s.ld.up, 1)
    dve.wait_ge(*s.l_r(c, 1))
    for k in range(KD):
        dve.wait_ge(*s.ld(c, k + 1))
        dve.tensor_tensor(b.sq[:, k, :], b.x[:, k, :], b.r[:, :], ALU.mult).then_inc(s.lxr.up, 1)
        dve.wait_ge(*s.lxr(c, k + 1))
        dve.tensor_scalar(b.x[:, k, :], b.sq[:, k, :], b.par[:, g0 + k:g0 + k + 1], b.par[:, g0 + 8 + k:g0 + 9 + k],
                          ALU.mult, ALU.add).then_inc(s.lx.up, 1)


def dve_add_up(dve, e, c, k, out):
    s, b = e.s, e.b
    if k == 0:
        return
    dve.wait_ge(*out(k))
    if k == 1:
        dve.wait_ge(*out(0))
        dve.tensor_tensor(b.r[:, :], b.x[:, 0, :], b.x[:, 1, :], ALU.add).then_inc(s.lsum.up, 1)
    else:
        dve.wait_ge(*s.lsum(c, k - 1))
        dve.tensor_tensor(b.r[:, :], b.r[:, :], b.x[:, k, :], ALU.add).then_inc(s.lsum.up, 1)


def dve_layer2(dve, e, l):
    s, b, bank = e.s, e.b, e.bank
    lay = Layer(s, 2, l)
    dve.wait_ge(*s.par2_t(l, 1))
    dve.wait_ge(*s.lhh(l * 2 - 1, KD))
    dve.wait_ge(*s.lx(l * 2 - 1, KD))
    dve.tensor_copy(b.par[:, 0:32], bank[2][:, 0:32]).then_inc(s.par2.up, 1)
    for g in range(8):
        dve.wait_ge(*s.par2_t(l, 2 + g // 4))
        dve.tensor_tensor(b.n_swT[:, g, :], bank[3 + g // 4][:, g % 4 * P:(g % 4 + 1) * P], b.tril[:, :], ALU.mult)\
           .then_inc(s.swt.up, 1)
    def index_weights():
        dve.wait_ge(*s.wi_ps(l, 1))
        dve.tensor_scalar(b.n_wi[:, :, :].rearrange("p t h -> p (t h)"), bank[5][:, 0:16],
                          (4 * HD) ** -0.5, None, ALU.mult).then_inc(s.wi.up, 1)

    def rope(r):
        dst = ([b.n_qi[:, 0, :], b.n_qi[:, 1, :], b.n_ki[:, 0, :], b.n_k[:, 0, :], b.n_k[:, 1, :]]
               + [b.n_q[:, m, :] for m in range(4)])[r]
        j, m = [(0, 0), (0, 1), (1, 1), (2, 0), (2, 1), (3, 0), (3, 1), (4, 0), (4, 1)][r]
        dve.wait_ge(*lay.bank_out(m, j))
        dve.tensor_tensor(dst, b.n_raw[:, r % 3, :], b.cosine[:, :], ALU.mult).then_inc(s.rope2.up, 1)
        dve.wait_ge(*s.rot2(l, r + 1))
        dve.tensor_tensor(b.sq[:, r % 2, :], bank[2 + r % 2][:, :], b.sine[:, :], ALU.mult).then_inc(s.rope2.up, 1)
        dve.wait_ge(*s.rope2(l, 3 * r + 2))
        dve.tensor_tensor(dst, dst, b.sq[:, r % 2, :], ALU.add).then_inc(s.rope2.up, 1)

    def index_scores(i):
        n = CAUSAL[i]
        score = b.n_score[:, i - 1, 0:n]
        for h in range(4):
            dve.wait_ge(*s.is_ps(l, 4 * (i - 1) + h + 1))
            dve.wait_ge(*s.wi(l, 1))
            if h >= 2:
                dve.wait_ge(*s.is_sum(l, 7 * (i - 1) + 2 * (h - 1) + 1))
            dst = score if h == 0 else b.n_relu[:, h % 2, 0:n]
            dve.tensor_scalar(dst, bank[4 + h][:, 0:n], 0.0, b.n_wi[:, i, h:h + 1], ALU.max, ALU.mult)\
               .then_inc(s.is_sum.up, 1)
            if h:
                dve.wait_ge(*s.is_sum(l, 7 * (i - 1) + 2 * h))
                dve.tensor_tensor(score, score, dst, ALU.add).then_inc(s.is_sum.up, 1)

    def top(blocks, rounds=range(TOPK // 8)):
        def of(i):
            n = CAUSAL[i]
            return b.n_score[:, i - 1, 0:n], b.n_work[:, i - 1, 0:n], b.n_top[:, i - 1, :]

        for n8 in rounds:
            for i in blocks:
                score, work, eight = of(i)
                if n8 == 0:
                    dve.wait_ge(*s.is_sum(l, 7 * i))
                    dve.memset(b.n_score[0:HD, i - 1, CAUSAL[i] - HD:CAUSAL[i]], FLOOR).then_inc(s.floor.up, 1)
                    lone_wait(dve, s, *s.floor(l, i))
                else:
                    lone_wait(dve, s, *s.cut[i - 1](l, n8))
                dve.max(eight, work if n8 else score).then_inc(s.top[i - 1].up, 1)
            for i in blocks:
                score, work, eight = of(i)
                lone_wait(dve, s, *s.top[i - 1](l, n8 + 1))
                dve.match_replace(work, eight, work if n8 else score, TAKEN).then_inc(s.cut[i - 1].up, 1)

    def mask(i):
        score, work = b.n_score[:, i - 1, 0:CAUSAL[i]], b.n_work[:, i - 1, 0:CAUSAL[i]]
        dve.wait_ge(*s.cut[i - 1](l, TOPK // 8))
        dve.tensor_tensor(work, work, score, ALU.is_equal).then_inc(s.mask.up, 1)
        dve.wait_ge(*s.mask(l, 2 * i - 1))
        dve.tensor_scalar(b.n_mask[:, i - 1, 0:CAUSAL[i]], work, NEG, None, ALU.mult).then_inc(s.mask.up, 1)

    for n in range(3):
        rope(n)
    index_weights()
    index_scores(1)
    top([1])
    rope(3)
    rope(4)
    mask(1)
    index_scores(2)
    rope(5)
    rope(6)
    index_scores(3)
    top([2, 3], range(0, 5))
    rope(7)
    rope(8)
    top([2, 3], range(5, TOPK // 8))
    mask(2)
    mask(3)
    def gating_moments():
        for t in range(NB):
            dve.wait_ge(*lay.bank_out(t // 2, 8))
            dve.bn_stats(b.n_bn[:, t, :], b.n_vs[:, t, :]).then_inc(s.bn.up, 1)
        for t in range(NB):
            lone_wait(dve, s, *s.bn(l, t + 1))
            dve.bn_aggr(b.n_st[:, t, 0:2], b.n_bn[:, t, :]).then_inc(s.bn.up, 1)

    def gating_norm():
        dve.wait_ge(*s.v_r(l, 1))
        for t in range(NB):
            dve.tensor_scalar(b.n_vs[:, t, :], b.n_vs[:, t, :], b.n_st[:, t, 0:1], b.n_st[:, t, 6:7],
                              ALU.subtract, ALU.mult).then_inc(s.v_n.up, 1)

    def gate(m):
        dve.wait_ge(*s.sg(l, m + 1))
        dve.tensor_tensor(b.mf[:, 4 + m, :], bank[m % 2][:, :], b.n_u[:, m, :], ALU.mult)\
           .then_inc(s.bank[m % 2].up, 1)

    for h in range(8):
        dve_max(dve, e, 2, l, h)
        dve_normalise(dve, e, 2, l, h, b.n_prob)
        if h == 0:
            gating_moments()
        if h == 1:
            gating_norm()
        if 4 <= h:
            gate(h - 4)
    c = l * 2
    for k in range(KD):
        j = 9 + k // 2
        dve.wait_ge(*s.tile(lay.pair(j // 2), j % 2, k % 2))
        dve.scalar_tensor_tensor(b.x[:, k, :], b.x[:, k, :], ALPHA, bank[k % 2][:, :], ALU.mult, ALU.add)\
           .then_inc(s.bank[k % 2].up, 1)
        dve_add_up(dve, e, c, k, lambda k: lay.bank_out(k % 2, Q2_OUT + k // 2))
    dve_layer_norm(dve, e, c, 0)
    for k in range(KD):
        dve.wait_ge(*s.lhl(c, k + 1))
        dve.wait_ge(*lay.bank_out(k % 2, Q2_GATE + k // 2))
        sig = b.e_sig[:, k % 2, :]
        dve.tensor_tensor(sig, sig, b.e_ple[:, k, :], ALU.mult).then_inc(s.gx.up, 1)
        dve.wait_ge(*s.gx(l, 2 * k + 1))
        dve.scalar_tensor_tensor(b.x[:, k, :], b.x[:, k, :], ALPHA, sig, ALU.mult, ALU.add).then_inc(s.gx.up, 1)
    dve_ffn(dve, e, lay, 18, (Q2_FFN,))
    c = l * 2 + 1
    for k in range(KD):
        dve.wait_ge(*s.tile(lay.pair(20 + k), 1, 1))
        dve.tensor_tensor(b.x[:, k, :], bank[k % 2][:, :], b.x[:, k, :], ALU.add).then_inc(s.bank[k % 2].up, 1)
        dve_add_up(dve, e, c, k, lambda k: lay.bank_out(k % 2, Q2_W2 + k // 2))
    dve_layer_norm(dve, e, c, 16)


def dve_program(dve, e):
    s, b, bank = e.s, e.b, e.bank
    for x in (s.bank0, s.bank1, s.up0, s.up1, s.a_acc, s.lx):
        dve.sem_inc(x.up, x.credit)
    dve_setup(dve, e)
    dve.wait_ge(s.z_x.up, KD + 2)
    with dve.Fori(0, A_CHUNKS // 4) as i:
        for p in range(2):
            dve_modulation(dve, e, 0, i, p)
    dve.wait_ge(s.z_copied.up, Z_COPIES)
    dve.wait_ge(s.trig_in.up, 16)
    dve_trig(dve, e, 0)
    with dve.Fori(A_CHUNKS // 4, A_CHUNKS // 2) as i:
        for p in range(2):
            dve_modulation(dve, e, 0, i, p)
    with dve.Fori(0, DEPTH - 1) as l:
        dve_layer1(dve, e, l, True)
    dve_layer1(dve, e, DEPTH - 1, False)
    for k in range(1, KD):
        dve_rms_sum(dve, e, 2 * DEPTH, k)
    dve.wait_ge(s.trig_in.up, 32)
    dve_trig(dve, e, 1)
    dve_rms(dve, e, 2 * DEPTH, b.fg, None, True, summed=True)
    with dve.Fori(0, DEPTH) as l:
        dve_layer2(dve, e, l)
    dve_output(dve, e)


def dve_output(dve, e):
    s, b, bank = e.s, e.b, e.bank
    for t in range(NB):
        for g in range(2):
            dve.wait_ge(s.y_t.up, 2 * t + g + 1)
            dve.tensor_copy(b.y_out[:, t, g * T:(g + 1) * T], bank[2 + 2 * (t % 2) + g][:, :]).then_inc(s.y.up, 1)



def three(pe, out, whi, wlo, xhi, xlo, start, stop):
    pe.matmul(out, wlo, xhi, start=start, stop=False)
    pe.matmul(out, whi, xlo, start=False, stop=False)
    return pe.matmul(out, whi, xhi, start=False, stop=stop)


def pe_unit(pe, e, lay, j, q, order=range(KD), ready=None, banks=None, tokens=False):
    pe_unit_at(pe, e, lay, j // 2, j % 2, q, order, ready, banks, tokens)


def pe_unit_at(pe, e, lay, j2, p, q, order=range(KD), ready=None, banks=None, tokens=False):
    s, b, bank, u = e.s, e.b, e.bank, lay.pair(j2)
    hi, lo = w8(b.w_hi[p]), w8(b.w_lo[p])
    pe.wait_ge(*s.lo_in(u, p))
    for m in range(2):
        if banks is None:
            pe.wait_ge(*lay.bank_free(m, q))
            out = bank[m]
        else:
            pe.wait_ge(*banks(m))
            out = bank[2 + m]
        if tokens:
            for t in (2 * m, 2 * m + 1):
                for n, k in enumerate(order):
                    v = slice(t * P, (t + 1) * P)
                    op = three(pe, out[:, t % 2 * G:(t % 2 + 1) * G], b.h_hi[:, k, v], b.h_lo[:, k, v],
                               hi[:, k, :], lo[:, k, :], n == 0, n == KD - 1)
        else:
            for n, k in enumerate(order):
                if m == 0 and ready is not None:
                    pe.wait_ge(*ready(n))
                op = three(pe, out[:, :], hi[:, k, m * P:(m + 1) * P], lo[:, k, m * P:(m + 1) * P],
                           b.h_hi[:, k, :], b.h_lo[:, k, :], n == 0, n == KD - 1)
        op.then_inc(s.half.up, 1)


def pe_rms(pe, e, c):
    s, b = e.s, e.b
    pe.wait_ge(*s.ssq(c, 7))
    pe.matmul(e.bank[7][:, :], b.ones[:, :], b.sq[:, 0, :], start=True, stop=True).then_inc(s.rms.up, 1)


def pe_turn_probs(pe, e, blk, l, h, prob, first=None):
    s, b, bank = e.s, e.b, e.bank
    t = attention(s, blk)
    if h:
        pe.wait_ge(*t.pt(l, 3 * h))
        pe.wait_ge(*t.po(l, h))
    for g, blocks in enumerate(BY_KEY):
        pe.wait_ge(*t.pn(l, 4 * h + 4))
        for j in blocks:
            c = 0 if j != 3 else 384
            for i in range(j, NB):
                at = c + (i - j) * P
                op = pe.transpose(bank[TP_BANK[g]][:, at:at + P], prob[:, P_AT[i] + j * P:P_AT[i] + (j + 1) * P],
                                  b.eye[:, :])
        op.then_inc(t.tp.up, 1)


def pe_values(pe, e, l, h, val, v0, probT, out, wait, done):
    pe.wait_ge(*wait)
    o = HD * (h % 2)
    for j in range(NB):
        op = pe.matmul(out[o:o + HD, j * P:T], val[:, j, v0:v0 + HD], probT[:, PT_AT[j]:PT_AT[j] + T - j * P],
                       start=(j == 0), stop=(j == NB - 1))
    op.then_inc(done.up, 1)


def pe_ffn(pe, e, lay, j0, c):
    s, b, bank = e.s, e.b, e.bank

    def body(i, first):
        ready = (lambda n: s.hl(c, n + 1)) if first and c is not None else None

        def banks(m):
            return s.upb[m](lay.ffn, i)
        q = Q_FFN if lay.blk == 1 else Q2_FFN
        pe_unit_at(pe, e, lay, i + j0 // 2, 0, i + q, ready=ready)
        pe_unit_at(pe, e, lay, i + j0 // 2, 1, None, banks=banks)

    body(0, True)
    with pe.Fori(1, 11) as i:
        body(i, False)
    q = Q_W2 if lay.blk == 1 else Q2_W2
    lone_wait(pe, s, s.fl.up, lay.ffn * 22 + 24)
    with pe.Fori(0, 4) as i:
        for m in range(2):
            for p in range(2):
                u = lay.pair(i * 2 + (j0 // 2 + 11 + m))
                pe.wait_ge(*s.lo_in(u, p))
                if p == 0:
                    pe.wait_ge(*lay.bank_free(m, i + q))
                for k in range(11):
                    op = three(pe, bank[m][:, :], w11(b.w_hi[p])[:, k, :], w11(b.w_lo[p])[:, k, :],
                               b.f_hi[:, 11 * p + k, :], b.f_lo[:, 11 * p + k, :], p == 0 and k == 0,
                               p == 1 and k == 10)
                op.then_inc(s.half.up, 2)


def pe_layer1(pe, e, l):
    s, b, bank = e.s, e.b, e.bank
    lay = Layer(s, 1, l)

    def add_partitions(part):
        half = A_CHUNKS // 2
        pe.wait_ge(*s.a_acc(l, KD * half * (part + 1)))
        for n in range(2 * half * part, 2 * half * (part + 1)):
            op = pe.matmul(bank[MOD_BANK[part]][:, n:n + 1], b.a_acc[:, n * P:(n + 1) * P], b.ones[:, 0:1],
                           start=True, stop=True)
        op.then_inc(s.a_pe.up, 1)

    add_partitions(0)
    pe.wait_ge(*s.par_in(l, s.par_in.per))
    pe.transpose(bank[4][:, 0:74], b.rows[:, :], b.eye[0:74, 0:74]).then_inc(s.par_t.up, 1)
    pe.transpose(bank[5][:, 0:2 * TAPS], b.rows2[:, :], b.eye[0:2 * TAPS, 0:2 * TAPS]).then_inc(s.par_t.up, 1)
    c = l * 2
    pe_rms(pe, e, c)
    add_partitions(1)
    for k in range(KD):
        pe.wait_ge(*s.hf(c, k + 1))
        op = pe.matmul(bank[2][0:4, :], b.wff[:, k, :], b.hf[:, k, :], start=(k == 0), stop=(k == KD - 1))
    op.then_inc(s.ff.up, 1)

    def turn(n):
        m = n % 2
        pe.wait_ge(*lay.bank_out(m, 2 + n // 2))
        if n >= 2:
            pe.wait_ge(*s.rope(l, 3 * (n - 2) + 2))
        elif m == 0:
            pe.wait_ge(*s.ls_d(l, 1))
        pe.matmul(bank[2 + m][:, :], b.turn[:, :], b.rraw[:, m, :], start=True, stop=True).then_inc(s.rot.up, 1)

    def retain_scores(h):
        o, m = HD * (h % 2), h // 2
        if h:
            pe.wait_ge(*s.rs(l, 4 * h))
        pe.wait_ge(*s.rope(l, 12))
        for g, blocks in enumerate(BY_KEY):
            for j in blocks:
                c0, n = (0 if j != 3 else 384), T - P * j
                op = pe.matmul(bank[TP_BANK[g]][:, c0:c0 + n], b.rk[o:o + HD, m, j * P:(j + 1) * P],
                               b.rq[o:o + HD, m, j * P:T], start=True, stop=True)
            op.then_inc(s.rs_ps.up, 1)

    def retain_values(h):
        if h:
            pe.wait_ge(*s.rv_o(l, h))
        pe.wait_ge(*lay.bank_out(0, 4))
        pe.wait_ge(*lay.bank_out(1, 4))
        if h == 3:
            pe.wait_ge(*s.ex(l, 4))
        pe_values(pe, e, l, h, b.rv, HD * h, b.rs, bank[2], s.rs(l, 4 * h + 4), s.rv_ps)

    def scores(h):
        o, m = HD * (h % 2), h // 2
        if h:
            pe.wait_ge(*s.ex(l, 4 * h))
        else:
            pe.wait_ge(*lay.bank_out(0, 6))
            pe.wait_ge(*lay.bank_out(1, 6))
            pe.wait_ge(*s.ls_d(l, 4))
        if h < 2:
            pe.wait_ge(*s.rv_o(l, 3 + h))
        for g, blocks in enumerate(BY_QUERY):
            for i in blocks:
                n = CAUSAL[i]
                c0 = 0 if len(blocks) == 1 else (0 if i == 0 else P)
                sc = bank[SC_BANK[g]][:, c0:c0 + n]
                pe.matmul(sc, b.pick_r[:, h, :], b.cum[:, 0:n], start=True, stop=False)
                pe.matmul(sc, b.fq[o:o + HD, m, i * P:(i + 1) * P], b.fk[o:o + HD, m, 0:n], start=False, stop=False)
                op = pe.matmul(bank[SC_BANK[g]][:, c0 + n - P:c0 + n], b.eye_r[:, :], b.causal_r[:, :],
                               start=False, stop=True)
            op.then_inc(s.sc.up, 1)

    def values(h):
        if h == 0:
            pe.wait_ge(*lay.bank_out(0, 7))
            pe.wait_ge(*lay.bank_out(1, 7))
        pe_values(pe, e, l, h, b.fv, HD * h, b.probT, bank[5], s.pt(l, 3 * h + 3), s.pv)

    for j in range(10):
        pe_unit(pe, e, lay, j, j, ready=(lambda n: s.hl(c, n + 1)) if j == 0 else None, tokens=j in (4, 7))
        if j == 3:
            turn(0)
            turn(1)
        if j == 4:
            turn(2)
            turn(3)
        if 6 <= j:
            retain_values(j - 6)
        if 5 <= j <= 8:
            retain_scores(j - 5)
        if j == 8:
            scores(0)
    pe_turn_probs(pe, e, 1, l, 0, b.prob)
    scores(1)
    for m in range(2):
        pe.wait_ge(*lay.bank_free(m, Q_GN1))
        pe.wait_ge(*s.rv_o(l, 2 * m + 2))
        pe.matmul(bank[m][:, :], b.heads[:, :], b.mf[:, 4 + m, :], start=True, stop=True).then_inc(s.gn_ps.up, 1)
    values(0)
    pe_turn_probs(pe, e, 1, l, 1, b.prob)
    scores(2)
    values(1)
    for m in range(2):
        pe.wait_ge(*lay.bank_free(m, Q_GN2))
        pe.wait_ge(*s.gn_sq(l, m + 1))
        pe.matmul(bank[m][:, :], b.heads[:, :], b.ln_s[:, m, :], start=True, stop=True).then_inc(s.gn_ps.up, 1)
    pe.wait_ge(*s.decay_in(l, s.decay_in.per))
    pe.wait_ge(*s.pl_d(l, 4))
    for m in range(2):
        lone_wait(pe, s, *lay.bank_free(m, Q_POOL))
        for h in range(2):
            o = HD * h
            op = pe.matmul(bank[m][o:o + HD, :], b.pw[o:o + HD, m, :], b.wb[o:o + HD, m, 0:T], start=True, stop=True)
        op.then_inc(s.pl_ps.up, 1)
    pe_turn_probs(pe, e, 1, l, 2, b.prob)
    scores(3)
    values(2)
    pe.wait_ge(*lay.bank_free(0, Q_CONV))
    pe.wait_ge(*s.conv(l, 2 * TAPS))
    for m in range(2):
        op = pe.matmul(bank[0][:, :], b.ones[:, :], b.cv[:, m, :], start=(m == 0), stop=(m == 1))
    op.then_inc(s.cn_ps.up, 1)
    pe_turn_probs(pe, e, 1, l, 3, b.prob)
    pe.wait_ge(*lay.bank_free(1, Q_CONV))
    for m in range(2):
        pe.wait_ge(*s.cn_sq(l, m + 1))
        op = pe.matmul(bank[1][:, :], b.ones[:, :], b.ln_s[:, m, :], start=(m == 0), stop=(m == 1))
    op.then_inc(s.cn_ps.up, 1)
    values(3)
    for j in range(4):
        pe_unit(pe, e, lay, 10 + j, Q_OUT + j, order=MIX_ORDER, ready=(lambda n: s.ml(l, n + 1)) if j == 0 else None)
        pe.wait_ge(*s.b_acc(l, KD * (2 * j + 2)))
        for n in range(4 * j, 4 * j + 4):
            at = 2 * A_CHUNKS + n
            op = pe.matmul(bank[6][:, at:at + 1], b.b_acc[:, n * P:(n + 1) * P], b.ones[:, 0:1], start=True, stop=True)
    op.then_inc(s.b_pe.up, 1)
    pe_rms(pe, e, c + 1)
    pe_ffn(pe, e, lay, 14, c + 1)


def pe_layer_norm(pe, e, c):
    s, b, bank = e.s, e.b, e.bank
    pe.wait_ge(*s.lsum(c, 7))
    pe.matmul(bank[6][:, :], b.ones[:, :], b.r[:, :], start=True, stop=True).then_inc(s.lmean.up, 1)
    for k in range(KD):
        pe.wait_ge(*s.lsq(c, k + 1))
        op = pe.matmul(bank[7][:, :], b.ones[:, :], b.sq[:, k, :], start=(k == 0), stop=(k == KD - 1))
    op.then_inc(s.lvar.up, 1)


def pe_layer2(pe, e, l):
    s, b, bank = e.s, e.b, e.bank
    lay = Layer(s, 2, l)
    def parameters():
        lone_wait(pe, s, *s.in2(l, s.in2.per))
        pe.transpose(bank[2][:, 0:32], b.n_rows[:, :], b.eye[0:32, 0:32]).then_inc(s.par2_t.up, 1)
        for g in range(8):
            op = pe.transpose(bank[3 + g // 4][:, g % 4 * P:(g % 4 + 1) * P], b.n_sw[:, g, :], b.eye[:, :])
            if g % 4 == 3:
                op.then_inc(s.par2_t.up, 1)

    def index_weights():
        pe.wait_ge(*s.lx(l * 2 - 1, KD))
        for t in range(NB):
            for k in range(KD):
                op = pe.matmul(bank[5][:, 4 * t:4 * t + 4], b.x[:, k, t * P:(t + 1) * P], b.n_wiw[:, k, :],
                               start=(k == 0), stop=(k == KD - 1))
        op.then_inc(s.wi_ps.up, 1)

    def turn(r):
        j, m = [(0, 0), (0, 1), (1, 1), (2, 0), (2, 1), (3, 0), (3, 1), (4, 0), (4, 1)][r]
        pe.wait_ge(*lay.bank_out(m, j))
        if r >= 2:
            pe.wait_ge(*s.rope2(l, 3 * (r - 2) + 2))
        else:
            pe.wait_ge(*s.swt(l, 8))
            pe.wait_ge(*s.par2(l, 1))
        pe.matmul(bank[2 + r % 2][:, :], b.turn[:, :], b.n_raw[:, r % 3, :], start=True, stop=True)\
          .then_inc(s.rot2.up, 1)

    def index_logits(i):
        pe.wait_ge(*s.rope2(l, 9))
        pe.wait_ge(*s.wi(l, 1))
        for h in range(4):
            if i > 1:
                pe.wait_ge(*s.is_sum(l, 7 * (i - 2) + max(1, 2 * h)))
            o = HD * (h % 2)
            pe.matmul(bank[4 + h][:, 0:CAUSAL[i]], b.n_qi[o:o + HD, h // 2, i * P:(i + 1) * P],
                      b.n_ki[o:o + HD, 0, 0:CAUSAL[i]], start=True, stop=True).then_inc(s.is_ps.up, 1)

    def scores(h):
        o = HD * (h % 2)
        if h:
            pe.wait_ge(*s.ex2(l, 4 * h))
        else:
            pe.wait_ge(*s.rope2(l, 27))
            pe.wait_ge(*s.is_sum(l, 21))
        for g, blocks in enumerate(BY_QUERY):
            for i in blocks:
                n = CAUSAL[i]
                c0 = 0 if len(blocks) == 1 else (0 if i == 0 else P)
                sc = bank[SC_BANK[g]][:, c0:c0 + n]
                if i and h == 0:
                    pe.wait_ge(*s.mask(l, 2 * i))
                pe.matmul(sc, b.eye_r[:, :], b.n_mask[:, i - 1, 0:n] if i else b.chunked_r[:, :],
                          start=True, stop=False)
                op = pe.matmul(sc, b.n_q[o:o + HD, h // 2, i * P:(i + 1) * P], b.n_k[o:o + HD, h // 4, 0:n],
                               start=False, stop=True)
            op.then_inc(s.sc2.up, 1)

    def values(h):
        if h == 0:
            pe.wait_ge(*lay.bank_out(0, 1))
        pe_values(pe, e, l, h, b.n_v, HD * (h // 4), b.n_probT, bank[5], s.pt2(l, 3 * h + 3), s.pv2)

    def gating(m):
        pe.wait_ge(*lay.bank_free(m % 2, Q2_SGU + m // 2))
        pe.wait_ge(*s.v_g(l, 8))
        for c in range(NB):
            v = slice(c * P, (c + 1) * P)
            pe.matmul(bank[m % 2][:, v], b.pairs[:, m, :], b.n_sb[:, :], start=True, stop=False)
            for g in range(2):
                o = HD * g
                f = m * P + o
                op = pe.matmul(bank[m % 2][o:o + HD, v], b.n_vs[:, c, f:f + HD], b.n_swT[:, 2 * m + g, :],
                               start=False, stop=True)
        op.then_inc(s.sg.up, 1)

    ready = [s.lhl(l * 2 - 1, n + 1) for n in range(KD)]
    for j in range(9):
        if j == 1:
            pe_values_and_key(pe, e, lay)
        else:
            pe_unit(pe, e, lay, j, j, ready=(lambda n: ready[n]) if j == 0 else None, tokens=j in (7, 8))
        if j == 0:
            parameters()
        if j == 1:
            turn(0)
            turn(1)
            index_weights()
            turn(2)
            index_logits(1)
        if j == 2:
            turn(3)
            turn(4)
            index_logits(2)
        if j == 3:
            turn(5)
            turn(6)
            index_logits(3)
        if j == 4:
            turn(7)
            turn(8)
    scores(0)
    for h in range(8):
        pe_turn_probs(pe, e, 2, l, h, b.n_prob)
        if h < 7:
            scores(h + 1)
        if 3 <= h < 7:
            gating(h - 3)
        values(h)
    for j in range(4):
        pe_unit(pe, e, lay, 9 + j, Q2_OUT + j, order=MIX2_ORDER,
                ready=(lambda n: s.ml2(l, n + 1)) if j == 0 else None)
    pe.wait_ge(*s.p_in(l, 16))
    for m in range(2):
        for t in range(NB):
            op = pe.transpose(bank[2 + m][:, t * P:(t + 1) * P], b.e_p[:, t, m * P:(m + 1) * P], b.eye[:, :])
        op.then_inc(s.p_t.up, 1)
    pe_layer_norm(pe, e, l * 2)
    u = lay.pair(6)
    hi, lo = (x[1][:, :].rearrange("p (k c) -> p k c", k=2) for x in (b.w_hi, b.w_lo))
    pe.wait_ge(*s.lo_in(u, 1))
    pe.wait_ge(*s.p_l(l, 2))
    for m in range(KD):
        pe.wait_ge(*lay.bank_free(m % 2, Q2_PLE + m // 2))
        for k in range(2):
            v = slice(m * P, (m + 1) * P)
            op = three(pe, bank[m % 2][:, :], hi[:, k, v], lo[:, k, v], b.e_hi[:, k, :], b.e_lo[:, k, :],
                       k == 0, k == 1)
        if m < KD - 1:
            op.then_inc(s.ple.up, 1)
        else:
            op.then_inc(s.half.up, 2)
    for j in range(4):
        pe_unit(pe, e, lay, 14 + j, Q2_GATE + j, ready=(lambda n: s.lhl(l * 2, n + 1)) if j == 0 else None)
    pe_ffn(pe, e, lay, 18, None)
    pe_layer_norm(pe, e, l * 2 + 1)


def pe_values_and_key(pe, e, lay):
    s, b, bank, u = e.s, e.b, e.bank, lay.pair(0)
    hi, lo = w8(b.w_hi[1]), w8(b.w_lo[1])
    pe.wait_ge(*s.lo_in(u, 1))
    pe.wait_ge(*lay.bank_free(0, 1))
    for t in range(NB):
        v = slice(t * P, (t + 1) * P)
        for k in range(KD):
            op = three(pe, bank[0][:, v], b.h_hi[:, k, v], b.h_lo[:, k, v], hi[:, k, 0:P], lo[:, k, 0:P],
                       k == 0, k == KD - 1)
    op.then_inc(s.half.up, 1)
    pe.wait_ge(*lay.bank_free(1, 1))
    for k in range(KD):
        op = three(pe, bank[1][:, :], hi[:, k, P:G], lo[:, k, P:G], b.h_hi[:, k, :], b.h_lo[:, k, :],
                   k == 0, k == KD - 1)
    op.then_inc(s.half.up, 1)


def pe_program(pe, e):
    s, b, bank = e.s, e.b, e.bank
    pe.sem_inc(s.half.up, s.half.credit)
    pe.wait_ge(s.z_in.up, 64)
    pe.wait_ge(s.z_copied.up, Z_COPIES)
    pe.wait_ge(s.z_ready.up, 5)
    for k in range(KD):
        if k >= 4:
            pe.wait_ge(s.z_x.up, k - 3)
        for t in range(NB):
            op = pe.transpose(bank[2 + k % 4][:, t * P:(t + 1) * P], b.z_x[:, t, k * P:(k + 1) * P], b.eye[:, :])
        op.then_inc(s.z_xt.up, 1)
    pe.wait_ge(s.z_act.up, 1)
    pe.transpose(bank[6][:, 0:KD], b.z_cs[:, :], b.eye[0:KD, 0:KD]).then_inc(s.z_xt.up, 1)
    pe.transpose(bank[7][:, 0:KD], b.z_fg[:, :], b.eye[0:KD, 0:KD]).then_inc(s.z_xt.up, 1)
    pe.wait_ge(s.z_x.up, KD + 2)
    with pe.Fori(0, DEPTH - 1) as l:
        pe_layer1(pe, e, l)
    pe_layer1(pe, e, DEPTH - 1)
    pe_rms(pe, e, 2 * DEPTH)
    with pe.Fori(0, DEPTH) as l:
        pe_layer2(pe, e, l)
    pe_output(pe, e)


def pe_output(pe, e):
    s, b, bank = e.s, e.b, e.bank
    for t in range(NB):
        for g in range(2):
            if t >= 2:
                pe.wait_ge(s.y.up, 2 * (t - 2) + g + 1)
            for n in range(4):
                k = 4 * g + n
                pe.wait_ge(*s.lx(2 * DEPTH - 1, k + 1))
                op = pe.transpose(bank[2 + 2 * (t % 2) + g][:, n * P:(n + 1) * P], b.x[:, k, t * P:(t + 1) * P],
                                  b.eye[:, :])
            op.then_inc(s.y_t.up, 1)


_OUT = (1, T, D)


def kernel(**inputs):
    import numpy as _np
    import concourse.bacc as _bacc
    from concourse import mybir as _mybir
    from concourse.bass_utils import run_bass_kernel_spmd as _run

    nc = _bacc.Bacc("TRN2", target_bir_lowering=False, num_devices=1)
    table, table_at, decay = consts()
    arrays = {name: _np.ascontiguousarray(x) for name, x in inputs.items()}
    arrays["table"], arrays["decay"] = table, decay
    dram = {name: nc.dram_tensor(f"in_{name}", x.shape, _mybir.dt.from_np(x.dtype), kind="ExternalInput").ap()
            for name, x in arrays.items()}
    out = nc.dram_tensor("out_0", _OUT, _mybir.dt.from_np(_np.dtype("float32")), kind="ExternalOutput").ap()
    build(nc, dram, table_at, out)
    r = _run(nc, [{f"in_{name}": x for name, x in arrays.items()}], core_ids=[0])
    return r.results[0]["out_0"]
```
